# Optimizing a Trainium2 kernel written in Bass

```python
import jax, jax.numpy as jnp
from jax import lax
import numpy as np
import math
import jax
import jax.numpy as jnp

D_MODEL = 1024
BATCH = 1
SEQ = 512
DEPTH = 1

CHUNK = 64
N_MEM = 256

A_HEADS = 8
A_HEAD_DIM = 64
A_WIDTH = A_HEADS * A_HEAD_DIM
DECAY_LORA = 64
AAA_LORA = 64
GATE_LORA = 128
LNX_EPS = 64e-5

B_BLOCKS = 8
B_WIDTH = 512
B_BLOCK_DIM = B_WIDTH // B_BLOCKS
B_CONV = 4
LRU_C = 8.0

X_HEADS = 4
X_HEAD_DIM = D_MODEL // X_HEADS

D_FF = 2816
FFN_CONV = 3

NORM_EPS = 1e-6

RWKV_COLS = 3 * A_WIDTH + DECAY_LORA + AAA_LORA + GATE_LORA
P_IN = RWKV_COLS + 2 * B_WIDTH + 2 * D_MODEL


def rms_norm(x, g):
    xf = x.astype(jnp.float32)
    y = xf * lax.rsqrt(jnp.mean(xf * xf, axis=-1, keepdims=True) + NORM_EPS)
    return (y * g.astype(jnp.float32)).astype(x.dtype)

def causal_dwconv(x, w, b):
    k_width = w.shape[0]
    s = x.shape[1]
    xp = jnp.pad(x, ((0, 0), (k_width - 1, 0), (0, 0)))
    y = b
    for j in range(k_width):
        y = y + xp[:, j:j + s] * w[j]
    return y

def token_shift(p):
    return jnp.pad(p, ((0, 0), (1, 0), (0, 0)))[:, :-1]

def rwkv7_recurrence(r, decay, k, v, a, b):
    def step(state, inp):
        r_t, w_t, k_t, v_t, a_t, b_t = inp
        sa = jnp.einsum('bhij,bhj->bhi', state, a_t)
        state = (state * w_t[:, :, None, :]
                 + sa[..., None] * b_t[:, :, None, :]
                 + v_t[..., None] * k_t[:, :, None, :])
        y_t = jnp.einsum('bhij,bhj->bhi', state, r_t)
        return state, y_t
    bsz, _, nh, nd = r.shape
    xs = tuple(jnp.swapaxes(t, 0, 1) for t in (r, decay, k, v, a, b))
    s0 = jnp.zeros((bsz, nh, nd, nd), jnp.float32)
    _, ys = lax.scan(step, s0, xs)
    return jnp.swapaxes(ys, 0, 1)

def rwkv7_branch(p, mu, w0, w_up, a0, a_up, g_up, k_k, k_a, r_k, lnx_g, lnx_b):
    bsz, s, _ = p.shape
    p = p.astype(jnp.float32)
    p = p + (token_shift(p) - p) * mu
    c0, c1, c2 = A_WIDTH, 2 * A_WIDTH, 3 * A_WIDTH
    c3, c4 = c2 + DECAY_LORA, c2 + DECAY_LORA + AAA_LORA
    r, k, v = p[..., :c0], p[..., c0:c1], p[..., c1:c2]
    pw, pa, pg = p[..., c2:c3], p[..., c3:c4], p[..., c4:]
    w_log = -jax.nn.softplus(-(w0 + jnp.tanh(pw) @ w_up)) - 0.5
    decay = jnp.exp(-jnp.exp(w_log))
    a = jax.nn.sigmoid(a0 + pa @ a_up)
    g = jax.nn.sigmoid(pg) @ g_up
    kk = k * k_k
    k = k * (1.0 + (a - 1.0) * k_a)
    hs = lambda t: t.reshape(bsz, s, A_HEADS, A_HEAD_DIM)
    r, k, v, kk, a, decay = hs(r), hs(k), hs(v), hs(kk), hs(a), hs(decay)
    kk = kk / jnp.maximum(jnp.sqrt(jnp.sum(kk * kk, axis=-1, keepdims=True)), 1e-12)
    y = rwkv7_recurrence(r, decay, k, v, -kk, kk * a)
    mean = jnp.mean(y, axis=-1, keepdims=True)
    var = jnp.mean(jnp.square(y - mean), axis=-1, keepdims=True)
    y = ((y - mean) * lax.rsqrt(var + LNX_EPS)).reshape(bsz, s, A_WIDTH) * lnx_g + lnx_b
    bonus = jnp.sum(r * k * r_k, axis=-1, keepdims=True) * v
    return (y + bonus.reshape(bsz, s, A_WIDTH)) * g

def _lin_combine(c1, c2):
    a1, b1 = c1
    a2, b2 = c2
    return a1 * a2, a2 * b1 + b2

def rglru_branch(px, py, conv_w, conv_b, w_ga, b_ga, w_gx, b_gx, lam):
    bsz, s, _ = px.shape
    xb = causal_dwconv(px.astype(jnp.float32), conv_w, conv_b)
    xh = xb.reshape(bsz, s, B_BLOCKS, B_BLOCK_DIM)
    gate_a = jax.nn.sigmoid(jnp.einsum('bshi,hij->bshj', xh, w_ga).reshape(bsz, s, B_WIDTH) + b_ga)
    gate_x = jax.nn.sigmoid(jnp.einsum('bshi,hij->bshj', xh, w_gx).reshape(bsz, s, B_WIDTH) + b_gx)
    log_a = LRU_C * gate_a * jax.nn.log_sigmoid(lam)
    a = jnp.exp(log_a)
    mult = jnp.sqrt(-jnp.expm1(2.0 * log_a))
    pos = jnp.arange(s)[None, :, None]
    mult = jnp.where(pos == 0, 1.0, mult)
    u = xb * gate_x * mult
    _, h = lax.associative_scan(_lin_combine, (a, u), axis=1)
    return h * jax.nn.gelu(py.astype(jnp.float32))

def cross_attention(h, m, w_q, w_kv, w_o):
    bsz, s, _ = h.shape
    q = (h @ w_q).reshape(bsz, s, X_HEADS, X_HEAD_DIM)
    kv = m @ w_kv
    k = kv[..., :D_MODEL].reshape(bsz, -1, X_HEADS, X_HEAD_DIM)
    v = kv[..., D_MODEL:].reshape(bsz, -1, X_HEADS, X_HEAD_DIM)
    sc = jnp.einsum('bqhd,bkhd->bhqk', q, k).astype(jnp.float32) * (X_HEAD_DIM ** -0.5)
    pr = jax.nn.softmax(sc, axis=-1).astype(v.dtype)
    o = jnp.einsum('bhqk,bkhd->bqhd', pr, v).reshape(bsz, s, D_MODEL)
    return o @ w_o

def conv_ffn(h, w_in, conv_w, conv_b, w_out):
    u = h @ w_in
    gate = causal_dwconv(u[..., :D_FF], conv_w, conv_b)
    return (jax.nn.gelu(gate) * u[..., D_FF:]) @ w_out

def first_inputs(seed: int = 0) -> dict:
    key = jax.random.key(seed)
    ks = iter(jax.random.split(key, 48))
    L = DEPTH
    f32 = jnp.float32

    def nrm(shape, scale):
        return jax.random.normal(next(ks), shape, f32) * scale

    u_lam = jax.random.uniform(next(ks), (L, B_WIDTH), f32, minval=0.9, maxval=0.999)
    return {
        "x": nrm((BATCH, SEQ, D_MODEL), 1.0),
        "mem": nrm((BATCH, N_MEM, D_MODEL), 1.0),
        "norm_mix_g": 1.0 + nrm((L, D_MODEL), 0.05),
        "w_in": nrm((L, D_MODEL, P_IN), D_MODEL ** -0.5),
        "b_in": nrm((L, P_IN), 0.02),
        "mu_shift": jax.random.uniform(next(ks), (L, RWKV_COLS), f32),
        "w0": nrm((L, A_WIDTH), 0.5) - 0.5,
        "w_lora_up": nrm((L, DECAY_LORA, A_WIDTH), 0.1),
        "a0": nrm((L, A_WIDTH), 0.5),
        "a_lora_up": nrm((L, AAA_LORA, A_WIDTH), AAA_LORA ** -0.5),
        "g_lora_up": nrm((L, GATE_LORA, A_WIDTH), GATE_LORA ** -0.5),
        "k_k": 0.85 + nrm((L, A_WIDTH), 0.05),
        "k_a": 1.0 + nrm((L, A_WIDTH), 0.05),
        "r_k": nrm((L, A_HEADS, A_HEAD_DIM), 0.1),
        "lnx_g": 1.0 + nrm((L, A_WIDTH), 0.05),
        "lnx_b": nrm((L, A_WIDTH), 0.02),
        "w_branch_a": nrm((L, A_WIDTH, D_MODEL), A_WIDTH ** -0.5),
        "conv_b_w": nrm((L, B_CONV, B_WIDTH), B_CONV ** -0.5),
        "conv_b_b": nrm((L, B_WIDTH), 0.02),
        "w_rg_a": nrm((L, B_BLOCKS, B_BLOCK_DIM, B_BLOCK_DIM), B_BLOCK_DIM ** -0.5),
        "b_rg_a": nrm((L, B_WIDTH), 0.02),
        "w_rg_x": nrm((L, B_BLOCKS, B_BLOCK_DIM, B_BLOCK_DIM), B_BLOCK_DIM ** -0.5),
        "b_rg_x": nrm((L, B_WIDTH), 0.02),
        "lru_lambda": jnp.log(u_lam) - jnp.log1p(-u_lam),
        "w_branch_b": nrm((L, B_WIDTH, D_MODEL), B_WIDTH ** -0.5),
        "w_mix_out": nrm((L, D_MODEL, D_MODEL), D_MODEL ** -0.5),
        "norm_x_g": 1.0 + nrm((L, D_MODEL), 0.05),
        "norm_mem_g": 1.0 + nrm((L, D_MODEL), 0.05),
        "w_cq": nrm((L, D_MODEL, D_MODEL), D_MODEL ** -0.5),
        "w_ckv": nrm((L, D_MODEL, 2 * D_MODEL), D_MODEL ** -0.5),
        "w_co": nrm((L, D_MODEL, D_MODEL), D_MODEL ** -0.5),
        "norm_ffn_g": 1.0 + nrm((L, D_MODEL), 0.05),
        "w_ffn_in": nrm((L, D_MODEL, 2 * D_FF), D_MODEL ** -0.5),
        "ffn_conv_w": nrm((L, FFN_CONV, D_FF), FFN_CONV ** -0.5),
        "ffn_conv_b": nrm((L, D_FF), 0.02),
        "w_ffn_out": nrm((L, D_FF, D_MODEL), D_FF ** -0.5),
        "norm_final_g": 1.0 + nrm((D_MODEL,), 0.05),
    }

def first_block(x, mem, norm_mix_g, w_in, b_in, mu_shift, w0, w_lora_up, a0, a_lora_up,
              g_lora_up, k_k, k_a, r_k, lnx_g, lnx_b, w_branch_a, conv_b_w, conv_b_b,
              w_rg_a, b_rg_a, w_rg_x, b_rg_x, lru_lambda, w_branch_b, w_mix_out,
              norm_x_g, norm_mem_g, w_cq, w_ckv, w_co, norm_ffn_g, w_ffn_in,
              ffn_conv_w, ffn_conv_b, w_ffn_out, norm_final_g):
    dt = x.dtype
    cb0 = RWKV_COLS
    cb1 = cb0 + B_WIDTH
    cb2 = cb1 + B_WIDTH
    cg1 = cb2 + D_MODEL
    for l in range(DEPTH):
        h = rms_norm(x, norm_mix_g[l])
        proj = h @ w_in[l] + b_in[l]
        y_a = rwkv7_branch(proj[..., :cb0], mu_shift[l], w0[l], w_lora_up[l], a0[l],
                           a_lora_up[l], g_lora_up[l], k_k[l], k_a[l], r_k[l],
                           lnx_g[l], lnx_b[l]).astype(dt) @ w_branch_a[l]
        y_b = rglru_branch(proj[..., cb0:cb1], proj[..., cb1:cb2], conv_b_w[l], conv_b_b[l],
                           w_rg_a[l], b_rg_a[l], w_rg_x[l], b_rg_x[l],
                           lru_lambda[l]).astype(dt) @ w_branch_b[l]
        merged = (jax.nn.sigmoid(proj[..., cb2:cg1]) * y_a
                  + jax.nn.sigmoid(proj[..., cg1:]) * y_b)
        x = x + merged @ w_mix_out[l]
        x = x + cross_attention(rms_norm(x, norm_x_g[l]), rms_norm(mem, norm_mem_g[l]),
                                w_cq[l], w_ckv[l], w_co[l])
        x = x + conv_ffn(rms_norm(x, norm_ffn_g[l]), w_ffn_in[l], ffn_conv_w[l],
                         ffn_conv_b[l], w_ffn_out[l])
    return rms_norm(x, norm_final_g)


DEPTH_2 = 2

DEEPNORM_ALPHA = (2 * DEPTH_2) ** 0.25
DEEPNORM_BETA = (8 * DEPTH_2) ** -0.25
LN_EPS = 1e-5
RMS_EPS = 1e-6
NUM_BUCKETS = 32
REL_MAX_DIST = 2048
REL_HEADS = 4
GDN_HEADS = 6
GDN_DK = 128
GDN_DV = 128
GDN_CONV = 4
GDN_CHUNK = 64
GDN_QK = GDN_HEADS * GDN_DK
GDN_V = GDN_HEADS * GDN_DV
SWA_CONFIGS = ((128, 1), (512, 4), (2048, 16))
SWA_GROUPS = len(SWA_CONFIGS)
SWA_HEADS = 4
SWA_HEAD_DIM = 64
SWA_BLOCK = 128
SWA_QKV = SWA_GROUPS * SWA_HEADS * SWA_HEAD_DIM
SWA_OUT = SWA_HEADS * SWA_HEAD_DIM
DIFF_HEADS = 4
DIFF_HEAD_DIM = 64
DIFF_QK = DIFF_HEADS * 2 * DIFF_HEAD_DIM
DIFF_V = DIFF_HEADS * 2 * DIFF_HEAD_DIM
Q_BLOCK = 128
GLA_HEADS = 4
GLA_DK = 64
GLA_DV = 128
GLA_GATE_RANK = 16
GLA_GATE_TAU = 16.0
GLA_CHUNK = 64
GLA_QK = GLA_HEADS * GLA_DK
GLA_V = GLA_HEADS * GLA_DV

EVEN_SIZES = (GDN_QK, GDN_QK, GDN_V, GDN_V, GDN_HEADS, GDN_HEADS, SWA_QKV, SWA_QKV, SWA_QKV)
EVEN_IN = sum(EVEN_SIZES)
EVEN_SPLITS = tuple(int(v) for v in np.cumsum(EVEN_SIZES)[:-1])
EVEN_OUT = GDN_V + SWA_OUT
ODD_SIZES = (DIFF_QK, DIFF_QK, DIFF_V, GLA_QK, GLA_QK, GLA_V, GLA_V, GLA_GATE_RANK)
ODD_IN = sum(ODD_SIZES)
ODD_SPLITS = tuple(int(v) for v in np.cumsum(ODD_SIZES)[:-1])
ODD_OUT = DIFF_V + GLA_V
N_EVEN = (DEPTH_2 + 1) // 2
N_ODD = DEPTH_2 // 2


def layer_norm(x, g, b):
    xf = x.astype(jnp.float32)
    mu = jnp.mean(xf, -1, keepdims=True)
    var = jnp.mean(jnp.square(xf - mu), -1, keepdims=True)
    y = (xf - mu) * lax.rsqrt(var + LN_EPS) * g.astype(jnp.float32) + b.astype(jnp.float32)
    return y.astype(x.dtype)

def rms_norm_2(x, w):
    xf = x.astype(jnp.float32)
    return xf * lax.rsqrt(jnp.mean(xf * xf, -1, keepdims=True) + RMS_EPS) * w.astype(jnp.float32)

def l2_normalize(x):
    return x * lax.rsqrt(jnp.sum(x * x, -1, keepdims=True) + RMS_EPS)

def causal_depthwise_conv(x, w):
    width, seq = w.shape[0], x.shape[1]
    xp = jnp.pad(x, ((0, 0), (width - 1, 0), (0, 0)))
    y = w[0] * xp[:, :seq]
    for j in range(1, width):
        y = y + w[j] * xp[:, j:j + seq]
    return y

def rel_bucket(dist):
    max_exact = NUM_BUCKETS // 2
    d = jnp.maximum(dist, 1).astype(jnp.float32)
    large = max_exact + (jnp.log(d / max_exact) / math.log(REL_MAX_DIST / max_exact)
                         * (NUM_BUCKETS - max_exact)).astype(jnp.int32)
    large = jnp.minimum(large, NUM_BUCKETS - 1)
    return jnp.where(dist < max_exact, dist, large)

def gated_delta_rule(q, k, v, g, beta):
    bsz, seq, nh, dk = q.shape
    dv = v.shape[-1]
    c = GDN_CHUNK
    n = seq // c

    def chunk(t):
        return jnp.moveaxis(t.reshape((bsz, n, c, nh) + t.shape[3:]), 3, 1)

    qc, kc, vc, gc, bc = chunk(q), chunk(k), chunk(v), chunk(g), chunk(beta)
    gam = jnp.cumsum(gc, axis=-1)
    idx = jnp.arange(c)
    incl = idx[:, None] >= idx[None, :]
    strict = idx[:, None] > idx[None, :]
    decay = jnp.exp(jnp.where(incl, gam[..., :, None] - gam[..., None, :], -jnp.inf))
    kk = jnp.einsum('bhnid,bhnjd->bhnij', kc, kc)
    lower = jnp.eye(c, dtype=jnp.float32) + jnp.where(strict, bc[..., :, None] * kk * decay, 0.0)
    rhs = jnp.concatenate([vc * bc[..., None], kc * (bc * jnp.exp(gam))[..., None]], axis=-1)
    sol = lax.linalg.triangular_solve(lower, rhs, left_side=True, lower=True, unit_diagonal=True)
    u, w = sol[..., :dv], sol[..., dv:]
    qk = jnp.einsum('bhnid,bhnjd->bhnij', qc, kc) * decay
    q_dec = qc * jnp.exp(gam)[..., None]
    k_dec = kc * jnp.exp(gam[..., -1:] - gam)[..., None]
    g_last = jnp.exp(gam[..., -1])

    def step(state, inp):
        u_n, w_n, qk_n, qd_n, kd_n, gl_n = inp
        delta = u_n - jnp.einsum('bhck,bhkv->bhcv', w_n, state)
        o_n = jnp.einsum('bhck,bhkv->bhcv', qd_n, state) + jnp.einsum('bhij,bhjv->bhiv', qk_n, delta)
        state = gl_n[..., None, None] * state + jnp.einsum('bhck,bhcv->bhkv', kd_n, delta)
        return state, o_n

    xs = tuple(jnp.moveaxis(t, 2, 0) for t in (u, w, qk, q_dec, k_dec, g_last))
    state0 = jnp.zeros((bsz, nh, dk, dv), jnp.float32)
    _, o = lax.scan(step, state0, xs)
    return o.transpose(1, 0, 3, 2, 4).reshape(bsz, seq, nh, dv)

def dilated_branch(q, k, v, window, dilation, rel_bias):
    bsz, seq, nh, dh = q.shape
    span = window // dilation
    sub = seq // dilation
    nb = -(-sub // SWA_BLOCK)
    padded = nb * SWA_BLOCK

    def to_blocks(t):
        t = t.reshape(bsz, sub, dilation, nh, dh).transpose(0, 2, 1, 3, 4)
        t = jnp.pad(t, ((0, 0), (0, 0), (0, padded - sub), (0, 0), (0, 0)))
        return t.reshape(bsz, dilation, nb, SWA_BLOCK, nh, dh)

    def with_prev(t):
        prev = jnp.pad(t, ((0, 0), (0, 0), (1, 0), (0, 0), (0, 0), (0, 0)))[:, :, :-1]
        return jnp.concatenate([prev, t], axis=3)

    qb = to_blocks(q)
    kb, vb = with_prev(to_blocks(k)), with_prev(to_blocks(v))
    qi = jnp.arange(SWA_BLOCK)[:, None] + SWA_BLOCK
    kj = jnp.arange(2 * SWA_BLOCK)[None, :]
    rel = qi - kj
    key_sub = jnp.arange(nb)[:, None, None] * SWA_BLOCK + kj[None] - SWA_BLOCK
    mask = (rel >= 0) & (rel <= span) & (key_sub >= 0)
    bias = jnp.moveaxis(rel_bias[rel_bucket(jnp.maximum(rel, 0) * dilation)], -1, 0)
    s = jnp.einsum('bgnqhd,bgnkhd->bgnhqk', qb, kb).astype(jnp.float32) * dh ** -0.5
    s = s + bias.astype(jnp.float32)
    s = jnp.where(mask[None, None, :, None], s, -jnp.inf)
    m = jnp.max(s, axis=-1, keepdims=True)
    p = jnp.exp(s - m)
    l = jnp.sum(p, axis=-1, keepdims=True)
    o = jnp.einsum('bgnhqk,bgnkhd->bgnqhd', (p / l).astype(v.dtype), vb)
    lse = (m + jnp.log(l))[..., 0]
    o = o.reshape(bsz, dilation, padded, nh, dh)[:, :, :sub]
    o = o.transpose(0, 2, 1, 3, 4).reshape(bsz, seq, nh, dh)
    lse = lse.transpose(0, 1, 2, 4, 3).reshape(bsz, dilation, padded, nh)[:, :, :sub]
    lse = lse.transpose(0, 2, 1, 3).reshape(bsz, seq, nh)
    return o, lse

def dilated_attention(q, k, v, rel_bias):
    bsz, seq = q.shape[0], q.shape[1]
    outs, lses = [], []
    for g, (window, dilation) in enumerate(SWA_CONFIGS):
        o, lse = dilated_branch(q[:, :, g], k[:, :, g], v[:, :, g], window, dilation, rel_bias)
        outs.append(o)
        lses.append(lse)
    wts = jax.nn.softmax(jnp.stack(lses, 0), axis=0)
    o = jnp.einsum('gbsh,gbshd->bshd', wts, jnp.stack(outs, 0).astype(jnp.float32))
    return o.reshape(bsz, seq, SWA_OUT)

def even_mixer(x, rel_bias, w_in, conv_w, a_log, dt_bias, norm_w, w_out):
    bsz, seq, _ = x.shape
    f32 = jnp.float32
    q_a, k_a, v_a, z_a, b_a, a_a, q_b, k_b, v_b = jnp.split(x @ w_in, EVEN_SPLITS, axis=-1)
    qkv = jax.nn.silu(causal_depthwise_conv(jnp.concatenate([q_a, k_a, v_a], -1), conv_w)).astype(f32)
    q_a, k_a, v_a = jnp.split(qkv, (GDN_QK, 2 * GDN_QK), axis=-1)
    hk = (bsz, seq, GDN_HEADS, GDN_DK)
    q_a = l2_normalize(q_a.reshape(hk)) * GDN_DK ** -0.5
    k_a = l2_normalize(k_a.reshape(hk))
    v_a = v_a.reshape(bsz, seq, GDN_HEADS, GDN_DV)
    beta = jax.nn.sigmoid(b_a.astype(f32))
    g = -jnp.exp(a_log.astype(f32)) * jax.nn.softplus(a_a.astype(f32) + dt_bias.astype(f32))
    o_a = gated_delta_rule(q_a, k_a, v_a, g, beta)
    o_a = rms_norm_2(o_a, norm_w) * jax.nn.silu(z_a.astype(f32).reshape(bsz, seq, GDN_HEADS, GDN_DV))
    o_a = o_a.reshape(bsz, seq, GDN_V).astype(x.dtype)
    shp = (bsz, seq, SWA_GROUPS, SWA_HEADS, SWA_HEAD_DIM)
    o_b = dilated_attention(q_b.reshape(shp), k_b.reshape(shp), v_b.reshape(shp), rel_bias).astype(x.dtype)
    return jnp.concatenate([o_a, o_b], axis=-1) @ w_out

def diff_attention(q, k, v, lam, rel_bias):
    bsz, seq, nh, _, dh = q.shape
    nq = seq // Q_BLOCK
    qb = q.reshape(bsz, nq, Q_BLOCK, nh, 2, dh).transpose(1, 0, 3, 4, 2, 5)
    kt = k.transpose(0, 2, 3, 1, 4)
    vt = v.transpose(0, 2, 1, 3)
    k_pos = jnp.arange(seq)

    def block(args):
        q_blk, start = args
        dist = (start + jnp.arange(Q_BLOCK))[:, None] - k_pos[None, :]
        bias = jnp.moveaxis(rel_bias[rel_bucket(jnp.maximum(dist, 0))], -1, 0).astype(jnp.float32)
        s = jnp.einsum('bhcqd,bhckd->bhcqk', q_blk, kt).astype(jnp.float32) * dh ** -0.5
        s = jnp.where(dist >= 0, s + bias[None, :, None], -jnp.inf)
        p = jax.nn.softmax(s, axis=-1)
        attn = p[:, :, 0] - lam * p[:, :, 1]
        return jnp.einsum('bhqk,bhkv->bhqv', attn.astype(v.dtype), vt)

    o = lax.map(block, (qb, jnp.arange(nq) * Q_BLOCK))
    return o.transpose(1, 0, 3, 2, 4).reshape(bsz, seq, nh, 2 * dh)

def gla_chunked(q, k, v, log_a):
    bsz, seq, nh, dk = q.shape
    dv = v.shape[-1]
    c = GLA_CHUNK
    n = seq // c

    def chunk(t):
        return t.reshape(bsz, n, c, nh, t.shape[-1]).transpose(1, 0, 3, 2, 4)

    qc, kc, vc = chunk(q), chunk(k), chunk(v)
    bc = jnp.cumsum(chunk(log_a), axis=3)
    idx = jnp.arange(c)
    incl = (idx[:, None] >= idx[None, :])[:, :, None]

    def step(state, inp):
        q_n, k_n, v_n, b_n = inp
        dec = jnp.exp(jnp.where(incl, b_n[..., :, None, :] - b_n[..., None, :, :], -jnp.inf))
        attn = jnp.einsum('bhik,bhjk,bhijk->bhij', q_n, k_n, dec)
        o_n = jnp.einsum('bhik,bhkv->bhiv', q_n * jnp.exp(b_n), state) + jnp.einsum('bhij,bhjv->bhiv', attn, v_n)
        b_last = b_n[..., -1:, :]
        state = jnp.exp(b_last[..., 0, :])[..., None] * state + jnp.einsum(
            'bhck,bhcv->bhkv', k_n * jnp.exp(b_last - b_n), v_n)
        return state, o_n

    state0 = jnp.zeros((bsz, nh, dk, dv), jnp.float32)
    _, o = lax.scan(step, state0, (qc, kc, vc, bc))
    return o.transpose(1, 0, 3, 2, 4).reshape(bsz, seq, nh, dv)

def odd_mixer(x, rel_bias, w_in, lam_params, diff_norm_w, gla_w_gate, gla_b_gate, gla_norm_w, w_out, lam_init):
    bsz, seq, _ = x.shape
    f32 = jnp.float32
    q_c, k_c, v_c, q_d, k_d, v_d, r_d, g_d = jnp.split(x @ w_in, ODD_SPLITS, axis=-1)
    lp = lam_params.astype(f32)
    lam = jnp.exp(jnp.sum(lp[0] * lp[1])) - jnp.exp(jnp.sum(lp[2] * lp[3])) + lam_init
    shp = (bsz, seq, DIFF_HEADS, 2, DIFF_HEAD_DIM)
    o_c = diff_attention(q_c.reshape(shp), k_c.reshape(shp),
                         v_c.reshape(bsz, seq, DIFF_HEADS, 2 * DIFF_HEAD_DIM), lam, rel_bias)
    o_c = (rms_norm_2(o_c, diff_norm_w) * (1.0 - lam_init)).reshape(bsz, seq, DIFF_V).astype(x.dtype)
    log_a = jax.nn.log_sigmoid((g_d @ gla_w_gate + gla_b_gate).astype(f32)) / GLA_GATE_TAU
    hk = (bsz, seq, GLA_HEADS, GLA_DK)
    o_d = gla_chunked(q_d.astype(f32).reshape(hk) * GLA_DK ** -0.5, k_d.astype(f32).reshape(hk),
                      v_d.astype(f32).reshape(bsz, seq, GLA_HEADS, GLA_DV), log_a.reshape(hk))
    o_d = rms_norm_2(o_d, gla_norm_w) * jax.nn.silu(r_d.astype(f32).reshape(bsz, seq, GLA_HEADS, GLA_DV))
    o_d = o_d.reshape(bsz, seq, GLA_V).astype(x.dtype)
    return jnp.concatenate([o_c, o_d], axis=-1) @ w_out

def conv_ffn_2(x, w_up, conv_w, conv_b, w_down):
    h = causal_depthwise_conv(x @ w_up, conv_w) + conv_b
    gate, val = jnp.split(h, 2, axis=-1)
    return (jax.nn.silu(gate) * val) @ w_down

def second_inputs(seed: int = 0) -> dict:
    key = jax.random.key(seed)
    ks = jax.random.split(key, 24)
    f32 = jnp.float32

    def normal(k, shape, scale):
        return jax.random.normal(k, shape, f32) * scale

    dt = jnp.exp(jax.random.uniform(ks[5], (N_EVEN, GDN_HEADS), f32, math.log(1e-3), math.log(1e-1)))
    return {
        'x': normal(ks[0], (BATCH, SEQ, D_MODEL), 1.0),
        'rel_bias': normal(ks[1], (NUM_BUCKETS, REL_HEADS), 0.1),
        'w_in_even': normal(ks[2], (N_EVEN, D_MODEL, EVEN_IN), D_MODEL ** -0.5),
        'gdn_conv_w': normal(ks[3], (N_EVEN, GDN_CONV, 2 * GDN_QK + GDN_V), GDN_CONV ** -0.5),
        'gdn_a_log': jnp.log(jax.random.uniform(ks[4], (N_EVEN, GDN_HEADS), f32, 1.0, 16.0)),
        'gdn_dt_bias': dt + jnp.log(-jnp.expm1(-dt)),
        'gdn_norm_w': 1.0 + normal(ks[6], (N_EVEN, GDN_DV), 0.05),
        'w_out_even': normal(ks[7], (N_EVEN, EVEN_OUT, D_MODEL), EVEN_OUT ** -0.5 * DEEPNORM_BETA),
        'w_in_odd': normal(ks[8], (N_ODD, D_MODEL, ODD_IN), D_MODEL ** -0.5),
        'diff_lambda': normal(ks[9], (N_ODD, 4, DIFF_HEAD_DIM), 0.1),
        'diff_norm_w': 1.0 + normal(ks[10], (N_ODD, 2 * DIFF_HEAD_DIM), 0.05),
        'gla_w_gate': normal(ks[11], (N_ODD, GLA_GATE_RANK, GLA_QK), GLA_GATE_RANK ** -0.5),
        'gla_b_gate': normal(ks[12], (N_ODD, GLA_QK), 0.1),
        'gla_norm_w': 1.0 + normal(ks[13], (N_ODD, GLA_DV), 0.05),
        'w_out_odd': normal(ks[14], (N_ODD, ODD_OUT, D_MODEL), ODD_OUT ** -0.5 * DEEPNORM_BETA),
        'ffn_w_up': normal(ks[15], (DEPTH_2, D_MODEL, 2 * D_FF), D_MODEL ** -0.5),
        'ffn_conv_w': normal(ks[16], (DEPTH_2, FFN_CONV, 2 * D_FF), FFN_CONV ** -0.5),
        'ffn_conv_b': normal(ks[17], (DEPTH_2, 2 * D_FF), 0.02),
        'ffn_w_down': normal(ks[18], (DEPTH_2, D_FF, D_MODEL), D_FF ** -0.5 * DEEPNORM_BETA),
        'ln_g': 1.0 + normal(ks[19], (DEPTH_2, 2, D_MODEL), 0.05),
        'ln_b': normal(ks[20], (DEPTH_2, 2, D_MODEL), 0.02),
    }

def second_block(x, rel_bias, w_in_even, gdn_conv_w, gdn_a_log, gdn_dt_bias, gdn_norm_w, w_out_even,
              w_in_odd, diff_lambda, diff_norm_w, gla_w_gate, gla_b_gate, gla_norm_w, w_out_odd,
              ffn_w_up, ffn_conv_w, ffn_conv_b, ffn_w_down, ln_g, ln_b):
    h = x
    for layer in range(DEPTH_2):
        i = layer // 2
        if layer % 2 == 0:
            mix = even_mixer(h, rel_bias, w_in_even[i], gdn_conv_w[i], gdn_a_log[i], gdn_dt_bias[i],
                             gdn_norm_w[i], w_out_even[i])
        else:
            lam_init = 0.8 - 0.6 * math.exp(-0.3 * layer)
            mix = odd_mixer(h, rel_bias, w_in_odd[i], diff_lambda[i], diff_norm_w[i], gla_w_gate[i],
                            gla_b_gate[i], gla_norm_w[i], w_out_odd[i], lam_init)
        h = layer_norm(DEEPNORM_ALPHA * h + mix, ln_g[layer, 0], ln_b[layer, 0])
        ffn = conv_ffn_2(h, ffn_w_up[layer], ffn_conv_w[layer], ffn_conv_b[layer], ffn_w_down[layer])
        h = layer_norm(DEEPNORM_ALPHA * h + ffn, ln_g[layer, 1], ln_b[layer, 1])
    return h


def setup_inputs(seed=0):
    out = dict(first_inputs(seed))
    for name, value in second_inputs(seed + 1).items():
        if name != "x":
            out[name + "_2"] = value
    return out


def reference(
    x, mem, norm_mix_g, w_in, b_in, mu_shift, w0, w_lora_up, a0, a_lora_up, g_lora_up, k_k, k_a,
    r_k, lnx_g, lnx_b, w_branch_a, conv_b_w, conv_b_b, w_rg_a, b_rg_a, w_rg_x, b_rg_x,
    lru_lambda, w_branch_b, w_mix_out, norm_x_g, norm_mem_g, w_cq, w_ckv, w_co, norm_ffn_g,
    w_ffn_in, ffn_conv_w, ffn_conv_b, w_ffn_out, norm_final_g, rel_bias_2, w_in_even_2,
    gdn_conv_w_2, gdn_a_log_2, gdn_dt_bias_2, gdn_norm_w_2, w_out_even_2, w_in_odd_2,
    diff_lambda_2, diff_norm_w_2, gla_w_gate_2, gla_b_gate_2, gla_norm_w_2, w_out_odd_2,
    ffn_w_up_2, ffn_conv_w_2, ffn_conv_b_2, ffn_w_down_2, ln_g_2, ln_b_2,
):
    x = first_block(
        x, mem, norm_mix_g, w_in, b_in, mu_shift, w0, w_lora_up, a0, a_lora_up, g_lora_up, k_k,
        k_a, r_k, lnx_g, lnx_b, w_branch_a, conv_b_w, conv_b_b, w_rg_a, b_rg_a, w_rg_x, b_rg_x,
        lru_lambda, w_branch_b, w_mix_out, norm_x_g, norm_mem_g, w_cq, w_ckv, w_co, norm_ffn_g,
        w_ffn_in, ffn_conv_w, ffn_conv_b, w_ffn_out, norm_final_g,
    )
    return second_block(
        x, rel_bias_2, w_in_even_2, gdn_conv_w_2, gdn_a_log_2, gdn_dt_bias_2, gdn_norm_w_2,
        w_out_even_2, w_in_odd_2, diff_lambda_2, diff_norm_w_2, gla_w_gate_2, gla_b_gate_2,
        gla_norm_w_2, w_out_odd_2, ffn_w_up_2, ffn_conv_w_2, ffn_conv_b_2, ffn_w_down_2, ln_g_2,
        ln_b_2,
    )


_drawn_inputs = setup_inputs


def setup_inputs(seed=0):
    import zlib

    import numpy as np

    out = dict(_drawn_inputs(seed))
    spreads = {}
    factors = {'k_k': 8.0,
     'k_a': 2.711,
     'lnx_g': 3.281,
     'lnx_b': 8.0,
     'conv_b_b': 3.028,
     'b_rg_a': 8.0,
     'b_rg_x': 8.0,
     'norm_x_g': 8.0,
     'norm_mem_g': 6.599,
     'ffn_conv_b': 4.787,
     'rel_bias_2': 4.539,
     'gdn_norm_w_2': 5.49,
     'diff_lambda_2': 8.0,
     'diff_norm_w_2': 6.988,
     'gla_w_gate_2': 3.25,
     'gla_b_gate_2': 8.0,
     'gla_norm_w_2': 7.445,
     'ffn_conv_b_2': 6.484}
    for name, (base, spread) in spreads.items():
        noise = np.random.default_rng([zlib.crc32(name.encode()), seed]).standard_normal(out[name].shape)
        drawn = base * np.exp(spread * noise) if base else spread * noise
        out[name] = jnp.asarray(drawn.astype(out[name].dtype))
    for name, factor in factors.items():
        out[name] = (out[name] * factor).astype(out[name].dtype)
    return out
```

```python
from contextlib import ExitStack, contextmanager
import math

import numpy as np
import concourse.bass as bass
from concourse import mybir

F32 = mybir.dt.float32
ALU = mybir.AluOpType
ACT = mybir.ActivationFunctionType
AX_X = mybir.AxisListType.X

P = 128
S, D = 512, 1024
NT, ND = S // P, D // P
NMEM = 256
A_HEADS, A_DIM, A_WIDTH = 8, 64, 512
NA = A_WIDTH // P
B_WIDTH, B_CONV = 512, 4
NB = B_WIDTH // P
X_HEADS = 4
D_FF, FFN_CONV = 2816, 3
NF = D_FF // P
RWKV_BLOCKS = (3 * A_WIDTH + 64 + 64 + 128) // P
MASKED = -1e30
GDN_HEADS, GDN_CONV = 6, 4
SWA_GROUPS, SWA_HEADS, SWA_DIM = 3, 4, 64
SWA_DIL = 4
GLA_HEADS, GLA_TAU, GLA_SUB = 4, 16.0, 16
ALPHA = 4.0 ** 0.25
LEVELS = 7
NORM_EPS, LN_EPS, RMS_EPS, LNX_EPS = 1e-6, 1e-5, 1e-6, 64e-5
LAM_INIT = 0.8 - 0.6 * math.exp(-0.3)
EXP_CAP = 43.0

RING, CHUNK_K = 6, 8

G0_W, G1_W, TZ_W = 516, 256, 896


def buckets(dist):
    d = np.maximum(dist, 1).astype(np.float32)
    large = 16 + (np.log(d / np.float32(16)) / np.float32(math.log(2048 / 16)) * np.float32(16)).astype(np.int32)
    return np.where(dist < 16, dist, np.minimum(large, 31))


def one_hot_positions():
    parts = []
    e = np.arange(G0_W + 4 * 127)
    dist = 4 * 127 + 3 - e
    parts.append(np.where((dist >= 0) & (dist <= 128), buckets(np.maximum(dist, 0)), 32))
    e = np.arange(G1_W)
    step = 127 - e
    parts.append(np.where(step >= 0, buckets(np.maximum(step, 0) * 4), 32))
    parts.append(np.where((step >= 0) & (step % 4 == 0), buckets(np.maximum(step, 0) * 4), 32))
    e = np.arange(TZ_W + 127)
    dist = 127 + 384 - e
    parts.append(np.where(dist >= 0, buckets(np.maximum(dist, 0)), 32))
    at = np.cumsum([0] + [len(x) for x in parts])
    which = np.concatenate(parts)
    pad = -len(which) % 512
    which = np.concatenate([which, np.full(pad, 32)])
    return (which[None, :] == np.arange(33)[:, None]).astype(np.float32), [int(a) for a in at]


class Steps:

    def __init__(self, eng, sem):
        self.eng, self.sem, self.n = eng, sem, 0

    def __call__(self, ins):
        ins.then_inc(self.sem, 1)
        self.n += 1

    def wait(self):
        self.eng.wait_ge(self.sem, self.n)

    def one(self, ins):
        self(ins)
        self.wait()


STAGES = [0]


@contextmanager
def stage(nc, *names):
    STAGES[0] += 1
    sems = [nc.alloc_semaphore(f"{name}_{STAGES[0]}") for name in names]
    with nc.Block(no_gpsimd_drain=True) as block:
        yield (block, *sems)
    nc.clear_and_free_semaphores(sems)
    nc.all_engine_barrier(sem_only=True)


@contextmanager
def Memory(nc):
    with ExitStack() as stack:
        def tensor(name, *shape):
            STAGES[0] += 1
            return stack.enter_context(nc.sbuf_tensor(f"{name}_{STAGES[0]}", list(shape), F32))

        yield tensor


class Weights:

    def __init__(self, nc, mem, plan):
        self.nc = nc
        self.slots = [mem(f"w_slot{i}", P, CHUNK_K, P) for i in range(RING)]
        self.landed = [nc.alloc_semaphore(f"w_landed{i}") for i in range(RING)]
        self.used = nc.alloc_semaphore("w_used")
        self.chunks, self.first, self.shape, self.issued = [], {}, {}, 0
        for name, (dram, blocks, depth) in plan.items():
            self.first[name], self.shape[name] = len(self.chunks), (blocks, depth)
            for n in range(blocks):
                for k in range(0, depth, CHUNK_K):
                    self.chunks.append((dram, n, k, min(CHUNK_K, depth - k)))

    def per(self, name):
        return -(-self.shape[name][1] // CHUNK_K)

    def done(self, name, n):
        return self.first[name] + (n + 1) * self.per(name)

    def load(self, sp, name):
        end = self.done(name, self.shape[name][0] - 1)
        while self.issued < min(len(self.chunks), end + RING):
            c = self.issued
            dram, n, k, kc = self.chunks[c]
            if c >= RING:
                sp.wait_ge(self.used, c - RING + 1)
            sp.dma_start(self.slots[c % RING][:, 0:kc, :], dram[n, :, k:k + kc, :]).then_inc(
                self.landed[c % RING], 16)
            self.issued += 1

    def sums(self, pe, name, bank, moving, free, rows=False):
        nc = self.nc
        blocks, depth = self.shape[name]
        for n in range(blocks):
            if free(n):
                pe.wait_ge(*free(n))
            out = bank(n)
            for part in range(self.per(name)):
                c = self.first[name] + n * self.per(name) + part
                slot = self.slots[c % RING]
                pe.wait_ge(self.landed[c % RING], 16 * (c // RING + 1))
                ks = range(part * CHUNK_K, min(depth, (part + 1) * CHUNK_K))
                if rows:
                    for t in range(rows):
                        for k in ks:
                            last = nc.tensor.matmul(out[:, t * P:(t + 1) * P], moving(k, t, n), slot[:, k, :],
                                                    start=k == 0, stop=k == depth - 1)
                else:
                    for k in ks:
                        last = nc.tensor.matmul(out, slot[:, k - ks[0], :], moving(k),
                                                start=k == 0, stop=k == depth - 1)
                last.then_inc(self.used, 1)


def project(nc, W, PS, name, act, width=S, evac=None, banks=4, extra=None):
    who, emit = evac
    blocks = W.shape[name][0]
    with stage(nc, "read_out", "own") as (block, read_out, own):
        @block.sync
        def _(sp):
            W.load(sp, name)

        @block.tensor
        def _(pe):
            W.sums(pe, name, lambda n: PS[n % banks][:, 0:width], act,
                   lambda n: (read_out, n - banks + 1) if n >= banks else None)

        def reader(eng):
            steps = Steps(eng, own)
            for n in range(blocks):
                eng.wait_ge(W.used, W.done(name, n))
                emit(n, PS[n % banks][:, 0:width], steps).then_inc(read_out, 1)

        if who == "scalar":
            block.scalar(reader)
        else:
            block.vector(reader)


def normalise(nc, C, PS, src, dst, gain, width=S, bias=None, eps=NORM_EPS, scratch=None):
    centred = dst if bias is not None else src
    squares = scratch if bias is not None else dst
    with stage(nc, "centred", "squared", "mean", "var", "rstd", "own") as (
            block, centred_ok, squared, mean_ok, var_ok, rstd_ok, own), Memory(nc) as mem:
        rstd = mem("rstd", P, width)
        mean, var = PS[0][:, 0:width], PS[1][:, 0:width]

        @block.tensor
        def _(pe):
            if bias is not None:
                for k in range(ND):
                    last = nc.tensor.matmul(mean, C["over_d"][:], src[:, k, :], start=k == 0, stop=k == ND - 1)
                last.then_inc(mean_ok, 1)
            for k in range(ND):
                pe.wait_ge(squared, k + 1)
                last = nc.tensor.matmul(var, C["over_d"][:], squares[:, k, :], start=k == 0, stop=k == ND - 1)
            last.then_inc(var_ok, 1)

        @block.scalar
        def _(act):
            for k in range(ND):
                if bias is not None:
                    act.wait_ge(centred_ok, k + 1)
                nc.scalar.activation(squares[:, k, :], centred[:, k, :], ACT.Square).then_inc(squared, 1)
            act.wait_ge(rstd_ok, 1)
            nc.scalar.activation(rstd[:], rstd[:], ACT.Ln).then_inc(rstd_ok, 1)
            act.wait_ge(rstd_ok, 2)
            nc.scalar.activation(rstd[:], rstd[:], ACT.Exp, scale=-0.5).then_inc(rstd_ok, 1)

        @block.vector
        def _(dve):
            if bias is not None:
                dve.wait_ge(mean_ok, 1)
                for k in range(ND):
                    nc.vector.tensor_tensor(dst[:, k, :], src[:, k, :], mean, ALU.subtract).then_inc(centred_ok, 1)
            dve.wait_ge(var_ok, 1)
            nc.vector.tensor_scalar(rstd[:], var, eps, None, ALU.add).then_inc(rstd_ok, 1)
            dve.wait_ge(rstd_ok, 3)
            steps = Steps(dve, own)
            for k in range(ND):
                steps(nc.vector.scalar_tensor_tensor(dst[:, k, :], centred[:, k, :], gain[:, k:k + 1], rstd[:],
                                                     ALU.mult, ALU.mult))
            if bias is not None:
                steps.wait()
                for k in range(ND):
                    steps(nc.vector.tensor_scalar(dst[:, k, :], dst[:, k, :], bias[:, k:k + 1], None, ALU.add))
            steps.wait()


def unit_lower_inverse(nc, C, PS, MT, TT, T, BT, W1, heads):
    groups = [(a, min(a + 4, heads)) for a in range(0, heads, 4)]
    with stage(nc, "first", "masked", "bt_sums", "bt_ready", "t_sums", "tt_ready") as (
            block, first, masked, bt_sums, bt_ready, t_sums, tt_ready):
        G = len(groups)

        @block.gpsimd
        def _(pool):
            for level in range(1, LEVELS):
                for g, (a, b) in enumerate(groups):
                    if level > 1:
                        pool.wait_ge(bt_sums, (level - 1) * G + g + 1)
                    nc.gpsimd.tensor_tensor(BT[:, a:b, :], MT[:, a:b, :],
                                            C["level_mask"][:, level:level + 1, :].broadcast_to([P, b - a, P]),
                                            ALU.mult).then_inc(masked, 1)

        @block.tensor
        def _(pe):
            for g, (a, b) in enumerate(groups):
                pe.wait_ge(first, 2 * g + 2)
                for h in range(a, b):
                    last = nc.tensor.transpose(PS[3 * g][:, (h - a) * P:(h - a + 1) * P], TT[:, h, :], C["ident"][:])
                last.then_inc(bt_sums, 1)
            for level in range(1, LEVELS):
                for g, (a, b) in enumerate(groups):
                    if level == 1:
                        pe.wait_ge(bt_ready, g + 1)
                    else:
                        pe.wait_ge(tt_ready, (level - 1) * G + g + 1)
                    pe.wait_ge(masked, (level - 1) * G + g + 1)
                    for h in range(a, b):
                        last = nc.tensor.matmul(PS[3 * g][:, (h - a) * P:(h - a + 1) * P], BT[:, h, :], T[:, h, :],
                                                start=True, stop=True)
                    last.then_inc(bt_sums, 1)
                for g, (a, b) in enumerate(groups):
                    pe.wait_ge(bt_ready, level * G + g + 1)
                    for h in range(a, b):
                        o = slice((h - a) * P, (h - a + 1) * P)
                        if level < LEVELS - 1:
                            nc.tensor.matmul(PS[3 * g + 1][:, o], TT[:, h, :], W1[:, h, :], start=True, stop=True)
                        last = nc.tensor.matmul(PS[3 * g + 2][:, o], W1[:, h, :], TT[:, h, :], start=True, stop=True)
                    last.then_inc(t_sums, 1)

        @block.scalar
        def _(act):
            for level in range(LEVELS):
                for g, (a, b) in enumerate(groups):
                    act.wait_ge(bt_sums, level * G + g + 1)
                    if level > 1:
                        act.wait_ge(t_sums, (level - 2) * G + g + 1)
                    nc.scalar.activation((W1 if level else T)[:, a:b, :], PS[3 * g][:, 0:(b - a) * P].rearrange(
                        "p (h t) -> p h t", t=P), ACT.Copy).then_inc(bt_ready, 1)

        @block.vector
        def _(dve):
            for g, (a, b) in enumerate(groups):
                n = b - a
                nc.vector.tensor_tensor(TT[:, a:b, :], MT[:, a:b, :],
                                        C["level_mask"][:, 0:1, :].broadcast_to([P, n, P]), ALU.mult).then_inc(first, 1)
                dve.wait_ge(first, 2 * g + 1)
                nc.vector.tensor_tensor(TT[:, a:b, :], TT[:, a:b, :],
                                        C["ident"][:, None, :].broadcast_to([P, n, P]), ALU.add).then_inc(first, 1)
            for g in range(G):
                dve.wait_ge(bt_ready, g + 1)
                nc.vector.memset(C["spare"][:, g:g + 1], 0.0).then_inc(tt_ready, 1)
            for level in range(1, LEVELS):
                for g, (a, b) in enumerate(groups):
                    dve.wait_ge(t_sums, (level - 1) * G + g + 1)
                    if level < LEVELS - 1:
                        nc.vector.tensor_tensor(T[:, a:b, :], T[:, a:b, :], PS[3 * g + 1][:, 0:(b - a) * P].rearrange(
                            "p (h t) -> p h t", t=P), ALU.add)
                    nc.vector.tensor_tensor(TT[:, a:b, :], TT[:, a:b, :], PS[3 * g + 2][:, 0:(b - a) * P].rearrange(
                        "p (h t) -> p h t", t=P), ALU.add).then_inc(tt_ready, 1)
            dve.wait_ge(tt_ready, LEVELS * G)


def attention(nc, C, PS, items, width, values):
    with stage(nc, "scores_ready", "logits_ready", "max_ready", "exp_ready", "probs_ready", "turned", "turned_sb",
               "pv_ready", "out_ready", "own") as (
            block, scores_ready, logits_ready, max_ready, exp_ready, probs_ready, turned, turned_sb, pv_ready,
            out_ready, own), Memory(nc) as mem:
        L = [mem(f"logits{i}", P, width) for i in range(2)]
        PT = [mem(f"probs_turned{i}", P, width) for i in range(2)]
        nmax = mem("nmax", P, 2, 2)
        tot = mem("tot", P, 2, 2)
        N = len(items)

        @block.tensor
        def _(pe):
            def turn(t):
                it, par = items[t], t % 2
                pe.wait_ge(probs_ready, t + 1)
                if t:
                    pe.wait_ge(turned_sb, t)
                for j in range(len(it["values"])):
                    last = nc.tensor.transpose(PS[4 + j // 4][:, (j % 4) * P:(j % 4 + 1) * P],
                                               L[par][:, j * P:(j + 1) * P], C["ident"][:])
                last.then_inc(turned, 1)

            def pv(t):
                it, par = items[t], t % 2
                pe.wait_ge(turned_sb, t + 1)
                if t >= 2:
                    pe.wait_ge(out_ready, t - 1)
                p0, rows, _ = it["out"]
                n = len(it["values"])
                parts = it.get("parts", 1)
                for q in range(parts):
                    for j in range(n):
                        last = nc.tensor.matmul(PS[6 + par][p0:p0 + rows, q * P:(q + 1) * P],
                                                it["values"][j](q), PT[par][:, j * P:(j + 1) * P],
                                                start=j == 0, stop=j == n - 1)
                last.then_inc(pv_ready, 1)

            for t in range(N + 2):
                if t < N:
                    if t >= 2:
                        pe.wait_ge(logits_ready, t - 1)
                    for bank, c, lhsT, rhs, start, stop in items[t]["scores"]:
                        last = nc.tensor.matmul(PS[2 * (t % 2) + bank][:, c:c + rhs.shape[-1]], lhsT, rhs,
                                                start=start, stop=stop)
                    last.then_inc(scores_ready, 1)
                if 1 <= t <= N:
                    turn(t - 1)
                if t >= 2:
                    pv(t - 2)

        @block.vector
        def _(dve):
            steps = Steps(dve, own)

            def weigh(t):
                it, par = items[t], t % 2
                dve.wait_ge(exp_ready, t + 1)
                sm = it["softmaxes"]
                steps.one(nc.vector.reciprocal(tot[:, par, 0:len(sm)], tot[:, par, 0:len(sm)]))
                (a, b), *more = sm
                if more:
                    c, d = more[0]
                    steps(nc.vector.tensor_scalar(L[par][:, c:d], L[par][:, c:d], tot[:, par, 1:2], C["lam"][:, 0:1],
                                                  ALU.mult, ALU.mult))
                    steps.wait()
                    nc.vector.scalar_tensor_tensor(L[par][:, a:b], L[par][:, a:b], tot[:, par, 0:1], L[par][:, c:d],
                                                   ALU.mult, ALU.subtract).then_inc(probs_ready, 1)
                else:
                    nc.vector.tensor_scalar(L[par][:, a:b], L[par][:, a:b], tot[:, par, 0:1], None,
                                            ALU.mult).then_inc(probs_ready, 1)

            for t in range(N + 1):
                if t < N:
                    it, par = items[t], t % 2
                    dve.wait_ge(scores_ready, t + 1)
                    if t >= 2:
                        dve.wait_ge(turned, t - 1)
                    for i, (c, w, bank, pc, bias) in enumerate(it["logits"]):
                        dst, src = L[par][:, c:c + w], PS[2 * par + bank][:, pc:pc + w]
                        if bias is None:
                            ins = nc.vector.tensor_scalar(dst, src, it["scale"], None, ALU.mult)
                        else:
                            ins = nc.vector.scalar_tensor_tensor(dst, src, it["scale"], bias, ALU.mult, ALU.add)
                        if i < len(it["logits"]) - 1:
                            steps(ins)
                        else:
                            ins.then_inc(logits_ready, 1)
                    steps.wait()
                    dve.wait_ge(logits_ready, t + 1)
                    for i, (a, b) in enumerate(it["softmaxes"]):
                        steps(nc.vector.reduce_max(nmax[:, par, i:i + 1], L[par][:, a:b], AX_X))
                    steps.wait()
                    n = len(it["softmaxes"])
                    nc.vector.tensor_scalar(nmax[:, par, 0:n], nmax[:, par, 0:n], -1.0, None,
                                            ALU.mult).then_inc(max_ready, 1)
                if t >= 1:
                    weigh(t - 1)

        @block.scalar
        def _(act):
            for t in range(N + 2):
                if t < N:
                    it, par = items[t], t % 2
                    act.wait_ge(max_ready, t + 1)
                    for i, (a, b) in enumerate(it["softmaxes"]):
                        ins = nc.scalar.activation(L[par][:, a:b], L[par][:, a:b], ACT.Exp, bias=nmax[:, par, i:i + 1],
                                                   accum_out=tot[:, par, i:i + 1])
                    ins.then_inc(exp_ready, 1)
                if 1 <= t <= N:
                    par, n = (t - 1) % 2, len(items[t - 1]["values"])
                    act.wait_ge(turned, t)
                    if t >= 3:
                        act.wait_ge(pv_ready, t - 2)
                    for bank in range(-(-n // 4)):
                        w = min(4, n - 4 * bank) * P
                        ins = nc.scalar.activation(PT[par][:, 4 * bank * P:4 * bank * P + w], PS[4 + bank][:, 0:w],
                                                   ACT.Copy)
                    ins.then_inc(turned_sb, 1)
                if t >= 2:
                    it, par = items[t - 2], t % 2
                    p0, rows, dst = it["out"]
                    act.wait_ge(pv_ready, t - 1)
                    src = PS[6 + par][p0:p0 + rows, 0:it.get("parts", 1) * P]
                    if it.get("parts", 1) > 1:
                        src = src.rearrange("p (a b) -> p a b", b=P)
                    nc.scalar.activation(dst, src, ACT.Copy).then_inc(out_ready, 1)
            act.wait_ge(out_ready, N)


def chunk(n):
    return slice(n * P, (n + 1) * P)


def causal_conv(nc, steps, dst, src, taps, bias, width):
    last = taps.shape[1] - 1
    steps.one(nc.vector.tensor_scalar(dst, src, taps[:, last:last + 1], bias, ALU.mult, ALU.add)
              if bias is not None else nc.vector.tensor_scalar(dst, src, taps[:, last:last + 1], None, ALU.mult))
    for j in range(1, last + 1):
        ins = nc.vector.scalar_tensor_tensor(dst[:, j:], src[:, 0:width - j], taps[:, last - j:last - j + 1],
                                             dst[:, j:], ALU.mult, ALU.add)
        if j < last:
            steps.one(ins)
    return ins


def mixer_projection(nc, C, W, PS, h, M, PXY):
    with stage(nc, "evacuated", "mixed", "own") as (block, evacuated, mixed, own), Memory(nc) as mem:
        raw = [mem(f"raw{i}", P, S) for i in range(2)]
        diff = mem("diff", P, S)
        blocks = W.shape["mix_in"][0]

        @block.sync
        def _(sp):
            W.load(sp, "mix_in")

        @block.tensor
        def _(pe):
            W.sums(pe, "mix_in", lambda n: PS[n % 4][:], lambda k: h[:, k, :],
                   lambda n: (evacuated, n - 3) if n >= 4 else None)

        @block.scalar
        def _(act):
            for n in range(blocks):
                act.wait_ge(W.used, W.done("mix_in", n))
                if 2 <= n < RWKV_BLOCKS:
                    act.wait_ge(mixed, n - 1)
                dst = raw[n % 2][:] if n < RWKV_BLOCKS else PXY[:, n - RWKV_BLOCKS, :]
                nc.scalar.activation(dst, PS[n % 4][:], ACT.Identity, bias=C["b_in"][:, n:n + 1]).then_inc(evacuated, 1)
            act.wait_ge(evacuated, blocks)

        @block.vector
        def _(dve):
            steps = Steps(dve, own)
            for n in range(RWKV_BLOCKS):
                p = raw[n % 2]
                dve.wait_ge(evacuated, n + 1)
                if n:
                    dve.wait_ge(mixed, n)
                steps(nc.vector.tensor_tensor(diff[:, 1:], p[:, 0:S - 1], p[:, 1:], ALU.subtract))
                steps(nc.vector.tensor_scalar(diff[:, 0:1], p[:, 0:1], -1.0, None, ALU.mult))
                steps.wait()
                nc.vector.scalar_tensor_tensor(M[:, n, :], diff[:], C["mu"][:, n:n + 1], p[:], ALU.mult,
                                               ALU.add).then_inc(mixed, 1)
            dve.wait_ge(mixed, RWKV_BLOCKS)


def griffin(nc, C, PS, PXY, YB):
    with stage(nc, "conv", "gates", "act_done", "dve_done", "own_a", "own_v") as (
            block, conv, gates, act_done, dve_done, own_a, own_v), Memory(nc) as mem:
        xb, ga, gx = mem("xb", P, NB, S), mem("ga", P, NB, S), mem("gx", P, NB, S)
        t, den = mem("t", P, NB, S), mem("den", P, NB, S)
        col = mem("col", P, 4, NB)
        lam8 = col[:, 3, :]

        @block.tensor
        def _(pe):
            for k in range(NB):
                pe.wait_ge(conv, k + 1)
                nc.tensor.matmul(PS[2 * k][:], C["w_rg_a"][:, k, :], xb[:, k, :], start=True, stop=True)
                nc.tensor.matmul(PS[2 * k + 1][:], C["w_rg_x"][:, k, :], xb[:, k, :], start=True,
                                 stop=True).then_inc(gates, 1)

        @block.scalar
        def _(act):
            steps = Steps(act, own_a)
            steps.one(nc.scalar.activation(col[:, 0, :], C["lru_lambda"][:], ACT.Abs))
            nc.scalar.activation(col[:, 1, :], col[:, 0, :], ACT.Exp, scale=-1.0).then_inc(act_done, 1)
            act.wait_ge(dve_done, 1)
            nc.scalar.activation(col[:, 2, :], col[:, 1, :], ACT.Ln).then_inc(act_done, 1)
            for k in range(NB):
                act.wait_ge(gates, k + 1)
                nc.scalar.activation(ga[:, k, :], PS[2 * k][:], ACT.Sigmoid, bias=C["b_rg_a"][:, k:k + 1])
                nc.scalar.activation(gx[:, k, :], PS[2 * k + 1][:], ACT.Sigmoid,
                                     bias=C["b_rg_x"][:, k:k + 1]).then_inc(act_done, 1)
            act.wait_ge(dve_done, 2)
            nc.scalar.activation(t[:], ga[:], ACT.Tanh, scale=-1.0).then_inc(act_done, 1)
            act.wait_ge(act_done, 3 + NB)
            nc.scalar.activation(ga[:], ga[:], ACT.Exp)
            nc.scalar.activation(YB[:], PXY[:, NB:2 * NB, :], ACT.Gelu_apprx_tanh)
            act.wait_ge(dve_done, 3)
            nc.scalar.activation(t[:], t[:], ACT.Sqrt).then_inc(act_done, 1)

        @block.vector
        def _(dve):
            steps = Steps(dve, own_v)
            for k in range(NB):
                causal_conv(nc, steps, xb[:, k, :], PXY[:, k, :], C["conv_b_w"][:, k, :], C["conv_b_b"][:, k:k + 1],
                            S).then_inc(conv, 1)
            steps.one(nc.vector.tensor_scalar(lam8, C["lru_lambda"][:], 0.0, None, ALU.min))
            dve.wait_ge(act_done, 1)
            nc.vector.tensor_scalar(col[:, 1, :], col[:, 1, :], 1.0, None, ALU.add).then_inc(dve_done, 1)
            dve.wait_ge(act_done, 2)
            steps.one(nc.vector.tensor_tensor(lam8, lam8, col[:, 2, :], ALU.subtract))
            steps.one(nc.vector.tensor_scalar(lam8, lam8, 8.0, None, ALU.mult))
            dve.wait_ge(act_done, 2 + NB)
            for k in range(NB):
                ins = nc.vector.tensor_scalar(ga[:, k, :], ga[:, k, :], lam8[:, k:k + 1], None, ALU.mult)
                if k < NB - 1:
                    steps(ins)
            ins.then_inc(dve_done, 1)
            dve.wait_ge(act_done, 3 + NB)
            steps.one(nc.vector.tensor_scalar(den[:], t[:], 1.0, None, ALU.add))
            steps.one(nc.vector.reciprocal(den[:], den[:]))
            nc.vector.scalar_tensor_tensor(t[:], t[:], 2.0, den[:], ALU.mult, ALU.mult).then_inc(dve_done, 1)
            steps.one(nc.vector.tensor_tensor(xb[:], xb[:], gx[:], ALU.mult))
            dve.wait_ge(act_done, 4 + NB)
            steps.one(nc.vector.memset(t[:, :, 0:1], 1.0))
            steps.one(nc.vector.tensor_tensor(xb[:], xb[:], t[:], ALU.mult))
            for k in range(NB):
                steps(nc.vector.tensor_tensor_scan(den[:, k, :], ga[:, k, :], xb[:, k, :], 0.0, ALU.mult, ALU.add))
            steps.wait()
            steps.one(nc.vector.tensor_tensor(YB[:], YB[:], den[:], ALU.mult))


def rwkv_prepare(nc, C, PS, M, LD, CU, KN, BV):
    r, k, v = (M[:, 4 * i:4 * i + 4, :] for i in range(3))
    with stage(nc, "squashed", "lora", "act_done", "dve_done", "head_sums", "own_v") as (
            block, squashed, lora, act_done, dve_done, head_sums, own_v), Memory(nc) as mem:
        tmp = mem("tmp", P, NA, S)
        wide = mem("wide", P, S)
        scaled = mem("scaled", P, S)

        @block.tensor
        def _(pe):
            pe.wait_ge(squashed, 1)
            for n in range(NA):
                nc.tensor.matmul(PS[n][:], C["w_lora"][0:64, chunk(n)], wide[0:64, :], start=True, stop=True)
                last = nc.tensor.matmul(PS[4 + n][:], C["w_lora"][64:128, chunk(n)], M[64:128, 12, :], start=True,
                                        stop=True)
            last.then_inc(lora, 1)
            pe.wait_ge(dve_done, 1)
            for n in range(NA):
                last = nc.tensor.matmul(PS[4 + n][:], C["pair_ones"][:], tmp[:, n, :], start=True, stop=True)
            last.then_inc(head_sums, 1)

        @block.scalar
        def _(act):
            nc.scalar.activation(wide[0:64, :], M[0:64, 12, :], ACT.Tanh).then_inc(squashed, 1)
            act.wait_ge(lora, 1)
            for n in range(NA):
                nc.scalar.activation(LD[:, n, :], PS[n][:], ACT.Sigmoid, bias=C["w0"][:, n:n + 1])
                ins = nc.scalar.activation(BV[:, n, :], PS[4 + n][:], ACT.Sigmoid, bias=C["a0"][:, n:n + 1])
            ins.then_inc(act_done, 1)
            act.wait_ge(head_sums, 1)
            for n in range(NA):
                ins = nc.scalar.activation(tmp[:, n, :], PS[4 + n][:], ACT.Sqrt)
            ins.then_inc(act_done, 1)

        @block.vector
        def _(dve):
            steps = Steps(dve, own_v)
            for n in range(NA):
                steps(nc.vector.tensor_scalar(KN[:, n, :], k[:, n, :], C["k_k"][:, n:n + 1], None, ALU.mult))
            steps.wait()
            dve.wait_ge(act_done, 1)
            nc.vector.tensor_tensor(tmp[:], KN[:], KN[:], ALU.mult).then_inc(dve_done, 1)
            steps.one(nc.vector.tensor_scalar(LD[:], LD[:], -math.exp(-0.5), None, ALU.mult))
            for n in range(NA):
                steps(nc.vector.tensor_tensor_scan(CU[:, n, :], C["restart"][:], LD[:, n, :], 0.0, ALU.mult, ALU.add))
            for n in range(NA):
                steps.one(nc.vector.tensor_scalar(scaled[:], BV[:, n, :], 1.0,
                                                  C["k_a"][:, n:n + 1], ALU.subtract, ALU.mult))
                steps.one(nc.vector.scalar_tensor_tensor(k[:, n, :], scaled[:], 1.0, k[:, n, :], ALU.add, ALU.mult))
            dve.wait_ge(act_done, 2)
            steps.one(nc.vector.tensor_scalar(tmp[:], tmp[:], 1e-12, None, ALU.max))
            steps.one(nc.vector.reciprocal(tmp[:], tmp[:]))
            steps.one(nc.vector.tensor_tensor(KN[:], KN[:], tmp[:], ALU.mult))
            steps.one(nc.vector.tensor_tensor(BV[:], BV[:], KN[:], ALU.mult))


def rwkv_chunk(nc, C, PS, M, LD, CU, KN, BV, ST, Y, n):
    t = chunk(n)
    r, k, v = (M[:, 4 * i:4 * i + 4, t] for i in range(3))
    ld, cu, kn, bv = LD[:, :, t], CU[:, :, t], KN[:, :, t], BV[:, :, t]
    with Memory(nc) as mem:
        R0, A0 = mem("r_start", P, NA, P), mem("a_start", P, NA, P)
        T, BT, W1 = (mem(x, P, A_HEADS, P) for x in ("t", "bt", "w1"))
        (RT, AT), (KT, BTT), (KE, BE) = ((a[:, 0:NA, :], a[:, NA:A_HEADS, :]) for a in (T, BT, W1))
        VT, KET, BET = (mem(x, P, A_WIDTH) for x in ("v_rows", "k_end_rows", "b_end_rows"))
        gend = mem("gend", P, NA)
        with stage(nc, "exponent", "expd", "own_v", "own_a") as (block, exponent, expd, own_v, own_a), \
                Memory(nc) as mem2:
            X = [mem2(f"x{i}", P, NA, P) for i in range(6)]
            mid = CU[:, :, n * P + 63:n * P + 64].broadcast_to([P, NA, P])
            end = CU[:, :, n * P + P - 1:n * P + P].broadcast_to([P, NA, P])

            @block.vector
            def _(dve):
                steps = Steps(dve, own_v)
                steps(nc.vector.tensor_tensor(X[0][:], cu, mid, ALU.subtract))
                steps(nc.vector.tensor_tensor(X[5][:], cu, ld, ALU.subtract))
                steps(nc.vector.tensor_tensor(X[3][:], end, cu, ALU.subtract))
                steps.wait()
                nc.vector.tensor_tensor(X[1][:], X[0][:], ld, ALU.subtract).then_inc(exponent, 1)
                dve.wait_ge(expd, 1)
                steps(nc.vector.tensor_tensor(RT, r, X[0][:], ALU.mult))
                steps(nc.vector.scalar_tensor_tensor(AT, kn, -1.0, X[1][:], ALU.mult, ALU.mult))
                steps(nc.vector.tensor_tensor(KT, k, X[2][:], ALU.mult))
                steps(nc.vector.tensor_tensor(BTT, bv, X[2][:], ALU.mult))
                steps(nc.vector.tensor_tensor(KE, k, X[3][:], ALU.mult))
                steps(nc.vector.tensor_tensor(BE, bv, X[3][:], ALU.mult))
                steps(nc.vector.tensor_tensor(R0[:], r, X[4][:], ALU.mult))
                steps(nc.vector.scalar_tensor_tensor(A0[:], kn, -1.0, X[5][:], ALU.mult, ALU.mult))
                steps.wait()

            @block.scalar
            def _(act):
                steps = Steps(act, own_a)
                steps(nc.scalar.activation(X[4][:], cu, ACT.Exp))
                steps(nc.scalar.activation(gend[:], CU[:, :, n * P + P - 1], ACT.Exp))
                act.wait_ge(exponent, 1)
                steps(nc.scalar.activation(X[2][:], X[0][:], ACT.Exp, scale=-1.0))
                steps.wait()
                steps(nc.scalar.activation(X[0][:], X[0][:], ACT.Exp))
                steps(nc.scalar.activation(X[3][:], X[3][:], ACT.Exp))
                steps(nc.scalar.activation(X[5][:], X[5][:], ACT.Exp))
                nc.scalar.activation(X[1][:], X[1][:], ACT.Exp).then_inc(expd, 1)

        MAB, MAK, MRB, MRK, TT = (mem(x, P, A_HEADS, P) for x in ("m_ab", "m_ak", "m_rb", "m_rk", "tt"))
        pairs = [(BTT, AT, MAB, C["before"]), (KT, AT, MAK, C["before"]), (BTT, RT, MRB, C["until"]), (KT, RT, MRK, C["until"])]
        with stage(nc, "scored", "kept", "turned", "rows_ready") as (block, scored, kept, turned, rows_ready):
            @block.tensor
            def _(pe):
                for i, (left, right, _, _) in enumerate(pairs):
                    for half in range(2):
                        m = 2 * i + half
                        if m >= 5:
                            pe.wait_ge(kept, m - 4)
                        for q in range(4):
                            o = slice(64 * half, 64 * half + 64)
                            last = nc.tensor.matmul(PS[m % 5][:, chunk(q)], left[o, q, :], right[o, q, :],
                                                    start=True, stop=True)
                        last.then_inc(scored, 1)
                for i, src in enumerate((v, KE, BE)):
                    for j in range(NA):
                        last = nc.tensor.transpose(PS[5 + i][:, chunk(j)], src[:, j, :], C["ident"][:])
                    last.then_inc(turned, 1)

            @block.scalar
            def _(act):
                for i, dst in enumerate((VT, KET, BET)):
                    act.wait_ge(turned, i + 1)
                    nc.scalar.activation(dst[:], PS[5 + i][:], ACT.Copy).then_inc(rows_ready, 1)
                act.wait_ge(rows_ready, 3)

            @block.vector
            def _(dve):
                for i, (_, _, dst, mask) in enumerate(pairs):
                    for half in range(2):
                        m = 2 * i + half
                        dve.wait_ge(scored, m + 1)
                        nc.vector.tensor_tensor(dst[:, half::2, :],
                                                PS[m % 5][:].rearrange("p (h t) -> p h t", t=P),
                                                mask[:, None, :].broadcast_to([P, 4, P]), ALU.mult).then_inc(kept, 1)
                dve.wait_ge(kept, 8)

        unit_lower_inverse(nc, C, PS, MAB, TT, T, BT, W1, A_HEADS)

        with stage(nc, "sums", "read", "state") as (block, sums, read, state):
            R, U = (W1[:, i:i + 4, :].rearrange("p h t -> p (h t)") for i in (0, 4))

            @block.tensor
            def _(pe):
                for j in range(NA):
                    nc.tensor.matmul(PS[0][:, chunk(j)], A0[:, j, :], ST[:, j, :], start=j == 0, stop=False,
                                     skip_group_check=True)
                for h in range(A_HEADS):
                    o = slice(64 * h, 64 * h + 64)
                    last = nc.tensor.matmul(PS[0][:, o], MAK[:, h, :], VT[:, o], start=False, stop=h == A_HEADS - 1,
                                            skip_group_check=True)
                last.then_inc(sums, 1)
                pe.wait_ge(read, 1)
                for h in range(A_HEADS):
                    o = slice(64 * h, 64 * h + 64)
                    last = nc.tensor.matmul(PS[1][:, o], TT[:, h, :], R[:, o], start=True, stop=True)
                last.then_inc(sums, 1)
                pe.wait_ge(read, 2)
                for j in range(NA):
                    nc.tensor.matmul(PS[2][:, chunk(j)], ST[:, j, :], R0[:, j, :], start=j == 0, stop=False,
                                     skip_group_check=True)
                for h in range(A_HEADS):
                    o, q = slice(64 * h, 64 * h + 64), slice(64 * (h % 2), 64 * (h % 2) + 64)
                    nc.tensor.matmul(PS[2][q, chunk(h // 2)], U[:, o], MRB[:, h, :], start=False, stop=False,
                                     skip_group_check=True)
                    last = nc.tensor.matmul(PS[2][q, chunk(h // 2)], VT[:, o], MRK[:, h, :], start=False,
                                            stop=h >= A_HEADS - 2, skip_group_check=True)
                last.then_inc(sums, 1)
                for j in range(NA):
                    nc.tensor.matmul(PS[3][:, chunk(j)], KET[:, chunk(j)], VT[:, chunk(j)], start=True, stop=False,
                                     skip_group_check=True)
                    last = nc.tensor.matmul(PS[3][:, chunk(j)], BET[:, chunk(j)], U[:, chunk(j)], start=False,
                                            stop=True, skip_group_check=True)
                last.then_inc(sums, 1)

            @block.scalar
            def _(act):
                act.wait_ge(sums, 1)
                nc.scalar.activation(R, PS[0][:], ACT.Copy).then_inc(read, 1)
                act.wait_ge(sums, 2)
                nc.scalar.activation(U, PS[1][:], ACT.Copy).then_inc(read, 1)
                act.wait_ge(sums, 3)
                nc.scalar.activation(Y[:, :, t], PS[2][:].rearrange("p (j t) -> p j t", t=P), ACT.Copy).then_inc(
                    read, 1)
                act.wait_ge(read, 3)

            @block.vector
            def _(dve):
                dve.wait_ge(sums, 4)
                for j in range(NA):
                    for q in (slice(0, 64), slice(64, 128)):
                        o = slice(j * P + q.start, j * P + q.stop)
                        nc.vector.scalar_tensor_tensor(ST[q, j, q], ST[q, j, q], gend[q, j:j + 1], PS[3][q, o],
                                                       ALU.mult, ALU.add).then_inc(state, 1)
                dve.wait_ge(state, 2 * NA)


def rwkv_finish(nc, C, PS, M, Y):
    r, k, v = (M[:, 4 * i:4 * i + 4, :] for i in range(3))
    with stage(nc, "gated", "mean", "var", "bonus", "dve_done", "act_done", "own_v") as (
            block, gated, mean, var, bonus, dve_done, act_done, own_v), Memory(nc) as mem:
        rk, sq, rstd = mem("rk", P, NA, S), mem("sq", P, NA, S), mem("rstd", P, NA, S)
        G = mem("g", P, NA, S)

        @block.tensor
        def _(pe):
            pe.wait_ge(act_done, 1)
            for j in range(NA):
                last = nc.tensor.matmul(PS[4 + j][:], C["g_lora"][:, chunk(j)], M[:, 13, :], start=True, stop=True)
            last.then_inc(gated, 1)
            for j in range(NA):
                last = nc.tensor.matmul(PS[j][:], C["pair_mean"][:], Y[:, j, :], start=True, stop=True)
            last.then_inc(mean, 1)
            pe.wait_ge(act_done, 2)
            pe.wait_ge(dve_done, 1)
            for j in range(NA):
                last = nc.tensor.matmul(PS[4 + j][:], C["pair_ones"][:], rk[:, j, :], start=True, stop=True)
            last.then_inc(bonus, 1)
            pe.wait_ge(act_done, 3)
            for j in range(NA):
                last = nc.tensor.matmul(PS[j][:], C["pair_mean"][:], sq[:, j, :], start=True, stop=True)
            last.then_inc(var, 1)

        @block.scalar
        def _(act):
            nc.scalar.activation(M[:, 13, :], M[:, 13, :], ACT.Sigmoid).then_inc(act_done, 1)
            act.wait_ge(gated, 1)
            for j in range(NA):
                ins = nc.scalar.activation(G[:, j, :], PS[4 + j][:], ACT.Copy)
            ins.then_inc(act_done, 1)
            act.wait_ge(dve_done, 2)
            nc.scalar.activation(sq[:], Y[:], ACT.Square).then_inc(act_done, 1)
            act.wait_ge(dve_done, 3)
            nc.scalar.activation(rstd[:], rstd[:], ACT.Ln).then_inc(act_done, 1)
            act.wait_ge(act_done, 4)
            nc.scalar.activation(rstd[:], rstd[:], ACT.Exp, scale=-0.5).then_inc(act_done, 1)

        @block.vector
        def _(dve):
            steps = Steps(dve, own_v)
            steps.one(nc.vector.tensor_tensor(rk[:], r, k, ALU.mult))
            for j in range(NA):
                ins = nc.vector.tensor_scalar(rk[:, j, :], rk[:, j, :], C["r_k"][:, j:j + 1], None, ALU.mult)
                if j < NA - 1:
                    steps(ins)
            ins.then_inc(dve_done, 1)
            dve.wait_ge(mean, 1)
            for j in range(NA):
                ins = nc.vector.tensor_tensor(Y[:, j, :], Y[:, j, :], PS[j][:], ALU.subtract)
                if j < NA - 1:
                    steps(ins)
            ins.then_inc(dve_done, 1)
            dve.wait_ge(bonus, 1)
            for j in range(NA):
                steps(nc.vector.tensor_tensor(v[:, j, :], v[:, j, :], PS[4 + j][:], ALU.mult))
            dve.wait_ge(var, 1)
            for j in range(NA):
                ins = nc.vector.tensor_scalar(rstd[:, j, :], PS[j][:], LNX_EPS, None, ALU.add)
                if j < NA - 1:
                    steps(ins)
            ins.then_inc(dve_done, 1)
            dve.wait_ge(act_done, 5)
            steps.wait()
            for j in range(NA):
                steps(nc.vector.scalar_tensor_tensor(Y[:, j, :], Y[:, j, :], C["lnx_g"][:, j:j + 1], rstd[:, j, :],
                                                     ALU.mult, ALU.mult))
            steps.wait()
            for j in range(NA):
                steps(nc.vector.scalar_tensor_tensor(Y[:, j, :], Y[:, j, :], C["lnx_b"][:, j:j + 1], v[:, j, :],
                                                     ALU.add, ALU.add))
            steps.wait()
            steps.one(nc.vector.tensor_tensor(Y[:], Y[:], G[:], ALU.mult))


def bank(PS, base, h):
    return PS[base + h // 4][:, chunk(h % 4)]


def conv_silu_normalise(nc, C, PS, QKV):
    H = GDN_HEADS
    with stage(nc, "conved", "silu", "squared", "summed", "rstd", "own_v", "own_a") as (
            block, conved, silu, squared, summed, rstd_ok, own_v, own_a), Memory(nc) as mem:
        buf = [mem(f"conv{i}", P, S) for i in range(2)]
        sq = [mem(f"sq{i}", P, S) for i in range(2)]
        rs = [mem(f"rs{i}", P, S) for i in range(2)]

        @block.vector
        def _(dve):
            steps = Steps(dve, own_v)
            for b in range(3 * H):
                if b >= 2:
                    dve.wait_ge(silu, b - 1)
                causal_conv(nc, steps, buf[b % 2][:], QKV[:, b, :], C["gdn_conv"][:, b, :], None, S).then_inc(conved, 1)
            for b in range(2 * H):
                dve.wait_ge(rstd_ok, b + 1)
                steps(nc.vector.scalar_tensor_tensor(QKV[:, b, :], QKV[:, b, :], (P ** -0.5 if b < H else 1.0),
                                                     rs[b % 2][:], ALU.mult, ALU.mult))
            steps.wait()

        @block.scalar
        def _(act):
            steps = Steps(act, own_a)
            for b in range(3 * H):
                act.wait_ge(conved, b + 1)
                nc.scalar.activation(QKV[:, b, :], buf[b % 2][:], ACT.Silu).then_inc(silu, 1)
            act.wait_ge(silu, 3 * H)
            for b in range(2 * H):
                if b >= 2:
                    act.wait_ge(summed, b - 1)
                nc.scalar.activation(sq[b % 2][:], QKV[:, b, :], ACT.Square).then_inc(squared, 1)
                act.wait_ge(summed, b + 1)
                if b >= 2:
                    act.wait_ge(own_v, 3 * 3 * H + b - 1)
                steps.one(nc.scalar.activation(rs[b % 2][:], PS[b % 4][:], ACT.Ln, bias=C["rms_eps"][:, 0:1]))
                nc.scalar.activation(rs[b % 2][:], rs[b % 2][:], ACT.Exp, scale=-0.5).then_inc(rstd_ok, 1)

        @block.tensor
        def _(pe):
            for b in range(2 * H):
                pe.wait_ge(squared, b + 1)
                nc.tensor.matmul(PS[b % 4][:], C["ones"][:], sq[b % 2][:], start=True, stop=True).then_inc(summed, 1)


def gdn_gates(nc, C, PS, h, BETA, GAM):
    H = GDN_HEADS
    with stage(nc, "projected", "own_v", "own_a", "act_done", "dve_done") as (
            block, projected, own_v, own_a, act_done, dve_done), Memory(nc) as mem:
        z, e, na = mem("z", H, S), mem("e", H, S), mem("na", H, 1)

        @block.tensor
        def _(pe):
            for i in range(2):
                for k in range(ND):
                    last = nc.tensor.matmul(PS[i][0:H, :], C["w_ba"][:, k, i * H:(i + 1) * H], h[:, k, :], start=k == 0,
                                            stop=k == ND - 1)
            last.then_inc(projected, 1)

        @block.scalar
        def _(act):
            steps = Steps(act, own_a)
            nc.scalar.activation(na[:], C["gdn_a_log"][:], ACT.Exp)
            act.wait_ge(projected, 1)
            nc.scalar.activation(BETA[:], PS[0][0:H, :], ACT.Sigmoid)
            steps(nc.scalar.activation(z[:], PS[1][0:H, :], ACT.Identity, bias=C["gdn_dt"][:, 0:1]))
            steps.wait()
            steps.one(nc.scalar.activation(e[:], z[:], ACT.Abs))
            nc.scalar.activation(e[:], e[:], ACT.Exp, scale=-1.0).then_inc(act_done, 1)
            act.wait_ge(dve_done, 1)
            nc.scalar.activation(e[:], e[:], ACT.Ln).then_inc(act_done, 1)

        @block.vector
        def _(dve):
            steps = Steps(dve, own_v)
            dve.wait_ge(act_done, 1)
            nc.vector.tensor_scalar(e[:], e[:], 1.0, None, ALU.add).then_inc(dve_done, 1)
            steps.one(nc.vector.tensor_scalar(z[:], z[:], 0.0, None, ALU.max))
            dve.wait_ge(act_done, 2)
            steps.one(nc.vector.tensor_tensor(z[:], z[:], e[:], ALU.add))
            steps.one(nc.vector.tensor_scalar(z[:], z[:], na[:, 0:1], -1.0, ALU.mult, ALU.mult))
            steps.one(nc.vector.tensor_tensor_scan(GAM[:], C["restart"][0:H, :], z[:], 0.0, ALU.mult, ALU.add))


def gdn_chunk(nc, C, PS, QKV, BETA, GAM, ST, O, n):
    H = GDN_HEADS
    t = chunk(n)
    q, k, v = (QKV[:, H * i:H * i + H, t] for i in range(3))
    groups = [(0, 4), (4, H)]
    with Memory(nc) as mem:
        QE, KB, BB = (mem(x, P, H, P) for x in ("q_decayed", "k_beta", "beta"))
        DEC, MT, QK, TT = (mem(x, P, H, P) for x in ("decay", "mt", "qk", "tt"))
        KR, VR = mem("k_rows", P, H, P), mem("v_rows", P, H, P)
        col, tail, gl = mem("col", P, 2 * H), mem("tail", P, H), mem("gl", P, H)
        with stage(nc, "spread", "act_done", "dve_done", "own_v", "own_a") as (
                block, spread, act_done, dve_done, own_v, own_a):
            @block.tensor
            def _(pe):
                for h in range(H):
                    nc.tensor.matmul(bank(PS, 0, h), C["pick"][:, h, :], GAM[:, t], start=True, stop=True)
                    nc.tensor.matmul(bank(PS, 2, h), C["pick"][:, h, :], BETA[:, t], start=True, stop=True)
                nc.tensor.matmul(PS[4][:, 0:H], GAM[:, t], C["ident"][0:H, 0:H], start=True, stop=True)
                nc.tensor.matmul(PS[4][:, H:2 * H], BETA[:, t], C["ident"][0:H, 0:H], start=True,
                                 stop=True).then_inc(spread, 1)

            @block.scalar
            def _(act):
                steps = Steps(act, own_a)
                act.wait_ge(spread, 1)
                for g, (a, b) in enumerate(groups):
                    def wide(i):
                        return PS[i + g][:, 0:(b - a) * P].rearrange("p (h t) -> p h t", t=P)
                    nc.scalar.activation(BB[:, a:b, :], wide(2), ACT.Copy)
                    nc.scalar.activation(QE[:, a:b, :], wide(0), ACT.Exp)
                    ins = nc.scalar.activation(gl[:, a:b], wide(0)[:, :, P - 1], ACT.Exp)
                ins.then_inc(act_done, 1)
                act.wait_ge(dve_done, 1)
                nc.scalar.activation(tail[:], tail[:], ACT.Exp)
                nc.scalar.activation(DEC[:], DEC[:], ACT.Exp).then_inc(act_done, 1)

            @block.vector
            def _(dve):
                steps = Steps(dve, own_v)
                dve.wait_ge(spread, 1)
                dve.wait_ge(act_done, 1)
                steps.one(nc.vector.tensor_copy(col[:], PS[4][:, 0:2 * H]))
                for g, (a, b) in enumerate(groups):
                    steps(nc.vector.tensor_tensor(tail[:, a:b], PS[g][:, 0:(b - a) * P].rearrange(
                        "p (h t) -> p h t", t=P)[:, :, P - 1], col[:, a:b], ALU.subtract))
                steps.wait()
                for h in range(H):
                    ins = nc.vector.tensor_scalar(DEC[:, h, :], bank(PS, 0, h), col[:, h:h + 1], 0.0, ALU.subtract,
                                                  ALU.min)
                    if h < H - 1:
                        steps(ins)
                ins.then_inc(dve_done, 1)
                steps.one(nc.vector.tensor_tensor(KB[:], k, QE[:], ALU.mult))
                steps.one(nc.vector.tensor_tensor(KB[:], KB[:], BB[:], ALU.mult))
                steps.one(nc.vector.tensor_tensor(QE[:], QE[:], q, ALU.mult))
                dve.wait_ge(act_done, 2)
                steps.one(nc.vector.tensor_tensor(DEC[:], DEC[:], C["until"][:, None, :].broadcast_to([P, H, P]), ALU.mult))

        with stage(nc, "scored", "own_v") as (block, scored, own_v):
            @block.tensor
            def _(pe):
                for h in range(H):
                    nc.tensor.matmul(bank(PS, 0, h), k[:, h, :], k[:, h, :], start=True, stop=True)
                    nc.tensor.matmul(bank(PS, 2, h), k[:, h, :], q[:, h, :], start=True, stop=True)
                    nc.tensor.transpose(bank(PS, 4, h), k[:, h, :], C["ident"][:])
                    last = nc.tensor.transpose(bank(PS, 6, h), v[:, h, :], C["ident"][:])
                last.then_inc(scored, 1)

            @block.vector
            def _(dve):
                steps = Steps(dve, own_v)
                dve.wait_ge(scored, 1)
                for g, (a, b) in enumerate(groups):
                    def wide(i):
                        return PS[i + g][:, 0:(b - a) * P].rearrange("p (h t) -> p h t", t=P)
                    steps(nc.vector.tensor_tensor(MT[:, a:b, :], wide(0), DEC[:, a:b, :], ALU.mult))
                    steps(nc.vector.tensor_tensor(QK[:, a:b, :], wide(2), DEC[:, a:b, :], ALU.mult))
                    steps(nc.vector.tensor_tensor(KR[:, a:b, :], wide(4),
                                                  tail[:, a:b, None].broadcast_to([P, b - a, P]), ALU.mult))
                    steps(nc.vector.tensor_tensor(VR[:, a:b, :], wide(6),
                                                  col[:, H + a:H + b, None].broadcast_to([P, b - a, P]), ALU.mult))
                steps.wait()
                steps.one(nc.vector.scalar_tensor_tensor(MT[:], MT[:], -1.0, BB[:], ALU.mult, ALU.mult))
                steps.one(nc.vector.tensor_tensor(MT[:], MT[:], C["before"][:, None, :].broadcast_to([P, H, P]), ALU.mult))

        with Memory(nc) as mem2:
            T, BT, W1 = (mem2(x, P, H, P) for x in ("t", "bt", "w1"))
            unit_lower_inverse(nc, C, PS, MT, TT, T, BT, W1, H)

        with stage(nc, "sums", "read", "state") as (block, sums, read, state), Memory(nc) as mem2:
            R, U = mem2("rhs", P, H, P), mem2("delta", P, H, P)

            @block.tensor
            def _(pe):
                for h in range(H):
                    last = nc.tensor.matmul(bank(PS, 0, h), KB[:, h, :], ST[:, h, :], start=True, stop=True)
                last.then_inc(sums, 1)
                pe.wait_ge(read, 1)
                for h in range(H):
                    last = nc.tensor.matmul(bank(PS, 2, h), TT[:, h, :], R[:, h, :], start=True, stop=True)
                last.then_inc(sums, 1)
                pe.wait_ge(read, 2)
                for h in range(H):
                    nc.tensor.matmul(bank(PS, 4, h), ST[:, h, :], QE[:, h, :], start=True, stop=False)
                    last = nc.tensor.matmul(bank(PS, 4, h), U[:, h, :], QK[:, h, :], start=False, stop=True)
                last.then_inc(sums, 1)
                for h in range(H):
                    last = nc.tensor.matmul(bank(PS, 6, h), KR[:, h, :], U[:, h, :], start=True, stop=True)
                last.then_inc(sums, 1)

            @block.scalar
            def _(act):
                act.wait_ge(sums, 2)
                for g, (a, b) in enumerate(groups):
                    ins = nc.scalar.activation(U[:, a:b, :], PS[2 + g][:, 0:(b - a) * P].rearrange(
                        "p (h t) -> p h t", t=P), ACT.Copy)
                ins.then_inc(read, 1)
                act.wait_ge(sums, 3)
                for g, (a, b) in enumerate(groups):
                    ins = nc.scalar.activation(O[:, a:b, t], PS[4 + g][:, 0:(b - a) * P].rearrange(
                        "p (h t) -> p h t", t=P), ACT.Copy)
                ins.then_inc(read, 1)
                act.wait_ge(read, 3)

            @block.vector
            def _(dve):
                dve.wait_ge(sums, 1)
                for g, (a, b) in enumerate(groups):
                    ins = nc.vector.tensor_tensor(R[:, a:b, :], VR[:, a:b, :], PS[g][:, 0:(b - a) * P].rearrange(
                        "p (h t) -> p h t", t=P), ALU.subtract)
                ins.then_inc(read, 1)
                dve.wait_ge(sums, 4)
                for h in range(H):
                    nc.vector.scalar_tensor_tensor(ST[:, h, :], ST[:, h, :], gl[:, h:h + 1], bank(PS, 6, h),
                                                   ALU.mult, ALU.add).then_inc(state, 1)
                dve.wait_ge(state, H)


def gla_decays(nc, C, PS, GD, CU):
    with stage(nc, "projected", "act_done", "dve_done", "own_v", "own_a") as (
            block, projected, act_done, dve_done, own_v, own_a), Memory(nc) as mem:
        z, e = mem("z", P, 2, S), mem("e", P, 2, S)

        @block.tensor
        def _(pe):
            for n in range(2):
                last = nc.tensor.matmul(PS[n][:], C["gla_gate"][:, chunk(n)], GD[:], start=True, stop=True)
            last.then_inc(projected, 1)

        @block.scalar
        def _(act):
            steps = Steps(act, own_a)
            act.wait_ge(projected, 1)
            for n in range(2):
                steps(nc.scalar.activation(z[:, n, :], PS[n][:], ACT.Identity, bias=C["gla_b"][:, n:n + 1]))
            steps.wait()
            steps.one(nc.scalar.activation(e[:], z[:], ACT.Abs))
            nc.scalar.activation(e[:], e[:], ACT.Exp, scale=-1.0).then_inc(act_done, 1)
            act.wait_ge(dve_done, 1)
            nc.scalar.activation(e[:], e[:], ACT.Ln).then_inc(act_done, 1)

        @block.vector
        def _(dve):
            steps = Steps(dve, own_v)
            dve.wait_ge(act_done, 1)
            nc.vector.tensor_scalar(e[:], e[:], 1.0, None, ALU.add).then_inc(dve_done, 1)
            steps.one(nc.vector.tensor_scalar(z[:], z[:], 0.0, None, ALU.min))
            dve.wait_ge(act_done, 2)
            steps.one(nc.vector.tensor_tensor(z[:], z[:], e[:], ALU.subtract))
            steps.one(nc.vector.tensor_scalar(z[:], z[:], 1.0 / GLA_TAU, None, ALU.mult))
            for n in range(2):
                steps(nc.vector.tensor_tensor_scan(CU[:, n, :], C["restart"][:], z[:, n, :], 0.0, ALU.mult, ALU.add))
            steps.wait()


def gla_chunk(nc, C, PS, Q, K, V, CU, ST, O, n):
    t = chunk(n)
    q, k, cu = Q[:, :, t], K[:, :, t], CU[:, :, t]
    subs = P // GLA_SUB
    with Memory(nc) as mem:
        KH, QH = mem("k_about", P, subs, 2, P), mem("q_about", P, 2, P)
        Q0, KE = mem("q_start", P, 2, P), mem("k_end", P, 2, P)
        KER, AT, gend = mem("k_end_rows", P, 2 * P), mem("attn", P, GLA_HEADS, P), mem("gend", P, 2)
        with stage(nc, "exponent", "expd", "own_v") as (block, exponent, expd, own_v):
            @block.vector
            def _(dve):
                steps = Steps(dve, own_v)
                steps(nc.vector.memset(KH[:], 0.0))
                steps.wait()
                for i in range(subs):
                    m, w = n * P + i * GLA_SUB + GLA_SUB // 2 - 1, (i + 1) * GLA_SUB
                    mid = CU[:, :, m:m + 1]
                    steps(nc.vector.tensor_tensor(KH[:, i, :, 0:w], mid.broadcast_to([P, 2, w]), cu[:, :, 0:w],
                                                  ALU.subtract))
                    o = slice(i * GLA_SUB, (i + 1) * GLA_SUB)
                    steps(nc.vector.tensor_tensor(QH[:, :, o], cu[:, :, o], mid.broadcast_to([P, 2, GLA_SUB]),
                                                  ALU.subtract))
                e = n * P + P - 1
                steps(nc.vector.tensor_tensor(KE[:], CU[:, :, e:e + 1].broadcast_to([P, 2, P]), cu, ALU.subtract))
                steps.wait()
                steps(nc.vector.tensor_scalar(KH[:], KH[:], EXP_CAP, None, ALU.min))
                nc.vector.tensor_scalar(QH[:], QH[:], EXP_CAP, None, ALU.min).then_inc(exponent, 1)
                dve.wait_ge(expd, 1)
                for i in range(subs):
                    w = (i + 1) * GLA_SUB
                    steps(nc.vector.tensor_tensor(KH[:, i, :, 0:w], KH[:, i, :, 0:w], k[:, :, 0:w], ALU.mult))
                    if w < P:
                        steps(nc.vector.memset(KH[:, i, :, w:], 0.0))
                steps(nc.vector.tensor_tensor(QH[:], QH[:], q, ALU.mult))
                steps(nc.vector.tensor_tensor(Q0[:], Q0[:], q, ALU.mult))
                steps(nc.vector.tensor_tensor(KE[:], KE[:], k, ALU.mult))
                steps.wait()

            @block.scalar
            def _(act):
                nc.scalar.activation(Q0[:], cu, ACT.Exp)
                nc.scalar.activation(gend[:], CU[:, :, n * P + P - 1], ACT.Exp)
                act.wait_ge(exponent, 1)
                nc.scalar.activation(KH[:], KH[:], ACT.Exp)
                nc.scalar.activation(QH[:], QH[:], ACT.Exp)
                nc.scalar.activation(KE[:], KE[:], ACT.Exp).then_inc(expd, 1)

        with stage(nc, "sums", "read", "kept", "state") as (block, sums, read, kept, state):
            @block.tensor
            def _(pe):
                for h in range(GLA_HEADS):
                    o = slice(64 * (h % 2), 64 * (h % 2) + 64)
                    for i in range(subs):
                        w = slice(i * GLA_SUB, (i + 1) * GLA_SUB)
                        last = nc.tensor.matmul(PS[4 * (h % 2)][:, (h // 2) * P + w.start:(h // 2) * P + w.stop], KH[o, i, h // 2, :],
                                                QH[o, h // 2, w], start=True, stop=True)
                last.then_inc(sums, 1)
                for j in range(2):
                    last = nc.tensor.transpose(PS[1][:, chunk(j)], KE[:, j, :], C["ident"][:])
                last.then_inc(sums, 1)
                pe.wait_ge(kept, 1)
                for h in range(GLA_HEADS):
                    o = slice(64 * (h % 2), 64 * (h % 2) + 64)
                    nc.tensor.matmul(PS[2 + 3 * (h % 2)][:, chunk(h // 2)], ST[o, h // 2, :], Q0[o, h // 2, :], start=True, stop=False)
                    last = nc.tensor.matmul(PS[2 + 3 * (h % 2)][:, chunk(h // 2)], V[:, h, n, :], AT[:, h, :], start=False, stop=True)
                last.then_inc(sums, 1)
                pe.wait_ge(read, 1)
                for h in range(GLA_HEADS):
                    o = slice(64 * (h % 2), 64 * (h % 2) + 64)
                    last = nc.tensor.matmul(PS[3][o, chunk(h // 2)], KER[:, 64 * h:64 * h + 64], V[:, h, n, :],
                                            start=True, stop=True)
                last.then_inc(sums, 1)

            @block.scalar
            def _(act):
                act.wait_ge(sums, 2)
                nc.scalar.activation(KER[:], PS[1][:, 0:2 * P], ACT.Copy).then_inc(read, 1)
                act.wait_ge(sums, 3)
                for g in range(2):
                    ins = nc.scalar.activation(O[:, g::2, t], PS[2 + 3 * g][:, 0:2 * P].rearrange(
                        "p (h t) -> p h t", t=P), ACT.Copy)
                ins.then_inc(read, 1)
                act.wait_ge(read, 2)

            @block.vector
            def _(dve):
                dve.wait_ge(sums, 1)
                for g in range(2):
                    ins = nc.vector.tensor_tensor(AT[:, g::2, :], PS[4 * g][:, 0:2 * P].rearrange(
                        "p (h t) -> p h t", t=P), C["until"][:, None, :].broadcast_to([P, 2, P]), ALU.mult)
                ins.then_inc(kept, 1)
                dve.wait_ge(sums, 4)
                for j in range(2):
                    nc.vector.scalar_tensor_tensor(ST[:, j, :], ST[:, j, :], gend[:, j:j + 1], PS[3][:, chunk(j)],
                                                   ALU.mult, ALU.add).then_inc(state, 1)
                dve.wait_ge(state, 2)


def head_norm(nc, C, PS, O, heads, gain, factor=1.0, gate=None):
    with stage(nc, "squared", "summed", "rstd_ok", "scaled", "own_v", "own_a") as (
            block, squared, summed, rstd_ok, scaled, own_v, own_a), Memory(nc) as mem:
        sq = [mem(f"sq{i}", P, S) for i in range(2)]
        rs = [mem(f"rs{i}", P, S) for i in range(2)]

        @block.scalar
        def _(act):
            steps = Steps(act, own_a)
            if gate is not None:
                nc.scalar.activation(gate, gate, ACT.Silu)
            for b in range(heads):
                if b >= 2:
                    act.wait_ge(summed, b - 1)
                nc.scalar.activation(sq[b % 2][:], O[:, b, :], ACT.Square).then_inc(squared, 1)
                act.wait_ge(summed, b + 1)
                if b >= 2:
                    act.wait_ge(scaled, b - 1)
                steps.one(nc.scalar.activation(rs[b % 2][:], PS[b % 4][:], ACT.Ln, bias=C["rms_eps"][:, 0:1]))
                nc.scalar.activation(rs[b % 2][:], rs[b % 2][:], ACT.Exp, scale=-0.5).then_inc(rstd_ok, 1)

        @block.tensor
        def _(pe):
            for b in range(heads):
                pe.wait_ge(squared, b + 1)
                nc.tensor.matmul(PS[b % 4][:], C["mean_head"][:], sq[b % 2][:], start=True, stop=True).then_inc(summed, 1)

        @block.vector
        def _(dve):
            steps = Steps(dve, own_v)
            for b in range(heads):
                dve.wait_ge(rstd_ok, b + 1)
                steps.one(nc.vector.tensor_scalar(rs[b % 2][:], rs[b % 2][:], gain[:, 0:1], factor, ALU.mult, ALU.mult))
                nc.vector.tensor_tensor(O[:, b, :], O[:, b, :], rs[b % 2][:], ALU.mult).then_inc(scaled, 1)
            dve.wait_ge(scaled, heads)
            if gate is not None:
                steps.one(nc.vector.tensor_tensor(O[:, 0:heads, :], O[:, 0:heads, :], gate, ALU.mult))


def ffn(nc, C, W, PS, h, name, taps, bias, conv_values, func, F):
    with stage(nc, "gate_ready", "gelu_ready", "freed_value", "own_v") as (
            block, gate_ready, gelu_ready, freed_value, own_v), Memory(nc) as mem:
        g = [mem(f"gate{i}", P, S) for i in range(2)]
        val = mem("val", P, S)

        @block.sync
        def _(sp):
            W.load(sp, name)

        @block.tensor
        def _(pe):
            W.sums(pe, name, lambda n: PS[n % 4][:], lambda k: h[:, k, :],
                   lambda n: None if n < 4 else ((gate_ready, freed_value)[n % 2], n // 2 - 1))

        @block.scalar
        def _(act):
            for i in range(NF):
                act.wait_ge(gate_ready, i + 1)
                nc.scalar.activation(g[i % 2][:], g[i % 2][:], func).then_inc(gelu_ready, 1)

        @block.vector
        def _(dve):
            steps = Steps(dve, own_v)
            for i in range(NF):
                dve.wait_ge(W.used, W.done(name, 2 * i))
                if i >= 2:
                    dve.wait_ge(freed_value, i - 1)
                causal_conv(nc, steps, g[i % 2][:], PS[(2 * i) % 4][:], taps[:, i, :], bias[:, i:i + 1],
                            S).then_inc(gate_ready, 1)
                dve.wait_ge(W.used, W.done(name, 2 * i + 1))
                value = PS[(2 * i + 1) % 4][:]
                if conv_values:
                    if i:
                        dve.wait_ge(freed_value, i)
                    steps.one(causal_conv(nc, steps, val[:], value, taps[:, NF + i, :], bias[:, NF + i:NF + i + 1], S))
                    value = val[:]
                dve.wait_ge(gelu_ready, i + 1)
                nc.vector.tensor_tensor(F[:, i, :], g[i % 2][:], value, ALU.mult).then_inc(freed_value, 1)
            dve.wait_ge(freed_value, NF)


def load(nc, items):
    with stage(nc, "landed") as (block, landed):
        @block.sync
        def _(sp):
            for dst, src in items:
                sp.dma_start(dst, src).then_inc(landed, 16)
            sp.wait_ge(landed, 16 * len(items))


def score_biases(nc, C, PS, A, scratch, G0, G12, TZ):
    _, at = one_hot_positions()
    L = scratch.shape[2]
    with Memory(nc) as mem:
        table, rep, hot = mem("table", 33, SWA_HEADS), mem("rep", 33, SWA_HEADS, P), mem("hot", 33, L)
        rows = mem("rows", P, SWA_HEADS, L)
        with stage(nc, "landed", "filled", "sums", "rows_ready", "stored") as (
                block, landed, filled, sums, rows_ready, stored):
            @block.sync
            def _(sp):
                sp.dma_start(table[0:32, :], A["rel_bias"]).then_inc(landed, 16)
                sp.dma_start(hot[:], A["one_hot"]).then_inc(landed, 16)
                for h in range(SWA_HEADS):
                    sp.wait_ge(rows_ready, (h + 1) * (L // 512))
                    sp.dma_start(scratch[h], rows[:, h, :]).then_inc(stored, 16)
                sp.wait_ge(stored, 16 * SWA_HEADS)

            @block.vector
            def _(dve):
                nc.vector.memset(table[32:33, :], MASKED).then_inc(filled, 1)
                dve.wait_ge(landed, 32)
                dve.wait_ge(filled, 1)
                nc.vector.tensor_copy(rep[:], table[:, :, None].broadcast_to([33, SWA_HEADS, P])).then_inc(filled, 1)

            @block.tensor
            def _(pe):
                pe.wait_ge(filled, 2)
                for h in range(SWA_HEADS):
                    for c in range(L // 512):
                        m = h * (L // 512) + c
                        if m >= 4:
                            pe.wait_ge(rows_ready, m - 3)
                        nc.tensor.matmul(PS[m % 4][:], rep[:, h, :], hot[:, 512 * c:512 * c + 512], start=True,
                                         stop=True).then_inc(sums, 1)

            @block.scalar
            def _(act):
                for h in range(SWA_HEADS):
                    for c in range(L // 512):
                        m = h * (L // 512) + c
                        act.wait_ge(sums, m + 1)
                        nc.scalar.activation(rows[:, h, 512 * c:512 * c + 512], PS[m % 4][:], ACT.Copy).then_inc(
                            rows_ready, 1)
    cuts = []
    for h in range(SWA_HEADS):
        base = h * P * L
        cuts.append((G0[:, h, :], bass.AP(scratch.tensor, base + at[0] + 4 * 127, [[L - 4, P], [1, G0_W]])))
        for g in range(2):
            cuts.append((G12[:, h, g, :], bass.AP(scratch.tensor, base + at[1 + g] + 127, [[L - 1, P], [1, P]])))
        cuts.append((TZ[:, h, :], bass.AP(scratch.tensor, base + at[3] + 127, [[L - 1, P], [1, TZ_W]])))
    load(nc, cuts)


def diff_lambda(nc, C, PS, lp):
    with stage(nc, "products", "sums", "expd") as (block, products, sums, expd), Memory(nc) as mem:
        prod, e = mem("prod", 64, 2), mem("e", P, 2)

        @block.vector
        def _(dve):
            nc.vector.tensor_tensor(prod[:, 0:1], lp[:, 0:1], lp[:, 1:2], ALU.mult)
            nc.vector.tensor_tensor(prod[:, 1:2], lp[:, 2:3], lp[:, 3:4], ALU.mult).then_inc(products, 1)
            dve.wait_ge(expd, 1)
            nc.vector.tensor_tensor(C["lam"][:], e[:, 0:1], e[:, 1:2], ALU.subtract).then_inc(products, 1)
            dve.wait_ge(products, 2)
            nc.vector.tensor_scalar(C["lam"][:], C["lam"][:], LAM_INIT, None, ALU.add).then_inc(products, 1)
            dve.wait_ge(products, 3)

        @block.tensor
        def _(pe):
            pe.wait_ge(products, 1)
            nc.tensor.matmul(PS[0][:, 0:2], C["ones"][0:64, :], prod[:], start=True, stop=True).then_inc(sums, 1)

        @block.scalar
        def _(act):
            act.wait_ge(sums, 1)
            nc.scalar.activation(e[:], PS[0][:, 0:2], ACT.Exp).then_inc(expd, 1)


def clear(nc, tensors):
    with stage(nc, "cleared") as (block, cleared):
        @block.vector
        def _(dve):
            for t in tensors:
                nc.vector.memset(t, 0.0).then_inc(cleared, 1)
            dve.wait_ge(cleared, len(tensors))


PROJECTIONS = [
    ("mix_in", 22, ND), ("mix_gate_a", 8, ND), ("branch_a", 8, NA), ("mix_gate_b", 8, ND), ("branch_b", 8, NB),
    ("mix_out", 8, ND), ("cq", 8, ND), ("ck", 8, ND), ("cv", 8, ND), ("co", 8, ND),
    ("ffn_in", 2 * NF, ND), ("ffn_out", 8, NF),
    ("swa_qk", 12, ND), ("swa_v", 6, ND), ("gdn_in", 24, ND), ("even_out", 8, 8),
    ("ffn_in_0", 2 * NF, ND), ("ffn_out_0", 8, NF),
    ("diff_qk", 8, ND), ("diff_v", 4, ND), ("gla_qkr", 8, ND), ("gla_v", 4, ND), ("odd_out", 8, 8),
    ("ffn_in_1", 2 * NF, ND), ("ffn_out_1", 8, NF),
]

CONSTANTS = [
    ("ident", (P, P)), ("over_d", (P, P)), ("pair_ones", (P, P)), ("pair_mean", (P, P)), ("mean_head", (P, P)),
    ("ones", (P, P)), ("level_mask", (P, LEVELS, P)), ("before", (P, P)), ("until", (P, P)), ("restart", (P, S)),
    ("pick", (GDN_HEADS, GDN_HEADS, P)),
    ("norm_mix_g", (P, ND)), ("b_in", (P, 22)), ("b_gates", (P, 16)), ("mu", (P, RWKV_BLOCKS)),
    ("w0", (P, NA)), ("a0", (P, NA)), ("k_k", (P, NA)), ("k_a", (P, NA)), ("r_k", (P, NA)), ("lnx_g", (P, NA)),
    ("lnx_b", (P, NA)), ("w_lora", (P, A_WIDTH)), ("g_lora", (P, A_WIDTH)),
    ("conv_b_w", (P, NB, B_CONV)), ("conv_b_b", (P, NB)), ("w_rg_a", (P, NB, P)), ("w_rg_x", (P, NB, P)),
    ("b_rg_a", (P, NB)), ("b_rg_x", (P, NB)), ("lru_lambda", (P, NB)),
    ("norm_x_g", (P, ND)), ("norm_mem_g", (P, ND)), ("norm_ffn_g", (P, ND)), ("norm_final_g", (P, ND)),
    ("ffn_conv_w", (P, NF, FFN_CONV)), ("ffn_conv_b", (P, NF)),
    ("gdn_conv", (P, 3 * GDN_HEADS, GDN_CONV)), ("w_ba", (P, ND, 2 * GDN_HEADS)), ("gdn_a_log", (GDN_HEADS, 1)),
    ("gdn_dt", (GDN_HEADS, 1)), ("gdn_norm", (P, 1)),
    ("diff_lp", (64, 4)), ("diff_norm", (P, 1)), ("w_gd", (P, ND, 16)), ("gla_gate", (16, 2 * P)), ("gla_b", (P, 2)),
    ("gla_norm", (P, 1)),
    ("ffn_conv_w2", (P, 2, 2 * NF, FFN_CONV)), ("ffn_conv_b2", (P, 2, 2 * NF)),
    ("ln_g", (P, 4, ND)), ("ln_b", (P, 4, ND)),
]


def project_rows(nc, W, PS, name, act, tiles, dst):
    blocks = W.shape[name][0]
    with stage(nc, "read_out") as (block, read_out):
        @block.sync
        def _(sp):
            W.load(sp, name)

        @block.tensor
        def _(pe):
            W.sums(pe, name, lambda n: PS[n % 4], act, lambda n: (read_out, n - 3) if n >= 4 else None, rows=tiles)

        @block.scalar
        def _(act_e):
            for n in range(blocks):
                act_e.wait_ge(W.used, W.done(name, n))
                nc.scalar.activation(dst[:, n, :, :], PS[n % 4][:, 0:tiles * P].rearrange("p (t f) -> p t f", f=P),
                                     ACT.Copy).then_inc(read_out, 1)
            act_e.wait_ge(read_out, blocks)


def build(nc, A, out, scratch):
    with Memory(nc) as keep, ExitStack() as banks:
        PS = [banks.enter_context(nc.psum_tensor(f"bank{i}", [P, 512], F32)) for i in range(8)]
        stored = nc.alloc_semaphore("out_stored")
        W = Weights(nc, keep, {name: (A[name], blocks, depth) for name, blocks, depth in PROJECTIONS})
        x = keep("x", P, ND, S)
        names, items = {}, [(x[:], A["x"])]
        for name, shape in CONSTANTS:
            names[name] = keep(name, *shape)
            items.append((names[name][:], A[name]))
        names["lam"], names["spare"], names["rms_eps"] = keep("lam", P, 1), keep("spare", P, 2), keep("rms_eps", P, 1)
        C = names
        load(nc, items)
        with stage(nc, "filled") as (block, filled):
            @block.vector
            def _(dve):
                nc.vector.memset(C["rms_eps"][:], RMS_EPS).then_inc(filled, 1)
                dve.wait_ge(filled, 1)
        diff_lambda(nc, C, PS, C["diff_lp"])

        def blocks_of(t):
            return lambda k: t[:, k, :]

        def copy_to(t):
            return ("scalar", lambda n, s, steps: nc.scalar.activation(t[:, n, :], s, ACT.Copy))

        def add_to(t, factor=1.0):
            return ("vector", lambda n, s, steps: nc.vector.scalar_tensor_tensor(
                t[:, n, :], t[:, n, :], factor, s, ALU.mult, ALU.add))

        def sigmoid_to(t, bias):
            return ("scalar", lambda n, s, steps: nc.scalar.activation(t[:, n, :], s, ACT.Sigmoid,
                                                                       bias=bias[:, n:n + 1]))

        with Memory(nc) as mem:
            h, YB, Y = mem("h", P, ND, S), mem("y_b", P, NB, S), mem("y_a", P, NA, S)
            normalise(nc, C, PS, x, h, C["norm_mix_g"])
            with Memory(nc) as rw:
                M = rw("mixed", P, RWKV_BLOCKS, S)
                with Memory(nc) as m2:
                    PXY = m2("pxy", P, 2 * NB, S)
                    mixer_projection(nc, C, W, PS, h, M, PXY)
                    griffin(nc, C, PS, PXY, YB)
                LD, CU, KN, BV = (rw(n, P, NA, S) for n in ("log_decay", "cu", "kn", "bv"))
                ST = rw("state", P, NA, P)
                rwkv_prepare(nc, C, PS, M, LD, CU, KN, BV)
                clear(nc, [ST[:]])
                for n in range(NT):
                    rwkv_chunk(nc, C, PS, M, LD, CU, KN, BV, ST, Y, n)
                rwkv_finish(nc, C, PS, M, Y)
            with Memory(nc) as m2:
                SG, merged = m2("gate", P, ND, S), m2("merged", P, ND, S)
                project(nc, W, PS, "mix_gate_a", blocks_of(h), evac=sigmoid_to(SG, C["b_gates"][:, 0:8]))
                project(nc, W, PS, "branch_a", blocks_of(Y), evac=("vector", lambda n, s, steps:
                        nc.vector.tensor_tensor(merged[:, n, :], SG[:, n, :], s, ALU.mult)))
                project(nc, W, PS, "mix_gate_b", blocks_of(h), evac=sigmoid_to(SG, C["b_gates"][:, 8:16]))

                def gated_add(n, s, steps):
                    steps.one(nc.vector.tensor_tensor(SG[:, n, :], SG[:, n, :], s, ALU.mult))
                    return nc.vector.tensor_tensor(merged[:, n, :], merged[:, n, :], SG[:, n, :], ALU.add)

                project(nc, W, PS, "branch_b", blocks_of(YB), evac=("vector", gated_add))
                project(nc, W, PS, "mix_out", blocks_of(merged), evac=add_to(x))

        with Memory(nc) as mem:
            h, q, o = mem("h", P, ND, S), mem("q", P, ND, S), mem("o", P, ND, S)
            mm, k, v = mem("mm", P, ND, NMEM), mem("k", P, ND, NMEM), mem("v", P, ND, 2, P)
            normalise(nc, C, PS, x, h, C["norm_x_g"])
            project(nc, W, PS, "cq", blocks_of(h), evac=copy_to(q))
            raw = o[:, :, 0:NMEM]
            load(nc, [(raw, A["mem"])])
            normalise(nc, C, PS, raw, mm, C["norm_mem_g"], width=NMEM)
            project(nc, W, PS, "ck", blocks_of(mm), width=NMEM, evac=copy_to(k))
            project_rows(nc, W, PS, "cv", lambda kk, t, n: mm[:, kk, chunk(t)], 2, v)
            items = []
            for hd in range(X_HEADS):
                for t in range(NT):
                    items.append({
                        "scores": [(0, 0, q[:, 2 * hd + i, chunk(t)], k[:, 2 * hd + i, :], i == 0, i == 1)
                                   for i in range(2)],
                        "logits": [(0, NMEM, 0, 0, None)], "scale": (D // X_HEADS) ** -0.5,
                        "softmaxes": [(0, NMEM)],
                        "values": [lambda part, hd=hd, j=j: v[:, 2 * hd + part, j, :] for j in range(2)],
                        "parts": 2, "out": (0, P, o[:, 2 * hd:2 * hd + 2, chunk(t)]),
                    })
            attention(nc, C, PS, items, NMEM, v)
            project(nc, W, PS, "co", blocks_of(o), evac=add_to(x))

        with Memory(nc) as mem:
            h, F = mem("h", P, ND, S), mem("f", P, NF, S)
            normalise(nc, C, PS, x, h, C["norm_ffn_g"])
            ffn(nc, C, W, PS, h, "ffn_in", C["ffn_conv_w"], C["ffn_conv_b"], False, ACT.Gelu_apprx_tanh, F)
            project(nc, W, PS, "ffn_out", blocks_of(F), evac=add_to(x))
            normalise(nc, C, PS, x, h, C["norm_final_g"])
            with stage(nc, "copied") as (block, copied):
                @block.vector
                def _(dve):
                    nc.vector.tensor_copy(x[:], h[:]).then_inc(copied, 1)
                    dve.wait_ge(copied, 1)

        def deep_norm(i):
            with Memory(nc) as m2:
                z, scr = m2("z", P, ND, S), m2("scr", P, ND, S)
                normalise(nc, C, PS, x, z, C["ln_g"][:, i, :], bias=C["ln_b"][:, i, :], eps=LN_EPS, scratch=scr)
                with stage(nc, "copied") as (block, copied):
                    @block.vector
                    def _(dve):
                        nc.vector.tensor_copy(x[:], z[:]).then_inc(copied, 1)
                        dve.wait_ge(copied, 1)

        def second_ffn(layer):
            with Memory(nc) as m2:
                F = m2("f", P, NF, S)
                ffn(nc, C, W, PS, x, f"ffn_in_{layer}", C["ffn_conv_w2"][:, layer, :, :], C["ffn_conv_b2"][:, layer, :],
                    True, ACT.Silu, F)
                project(nc, W, PS, f"ffn_out_{layer}", blocks_of(F), evac=add_to(x, ALPHA))
            deep_norm(2 * layer + 1)

        with Memory(nc) as both:
            TZ = both("full_bias", P, SWA_HEADS, TZ_W)
            with Memory(nc) as mem:
                OE = mem("o_even", P, 8, S)
                with Memory(nc) as m2:
                    G0, G12 = m2("g0_bias", P, SWA_HEADS, G0_W), m2("g12_bias", P, SWA_HEADS, 2, P)
                    score_biases(nc, C, PS, A, scratch, G0, G12, TZ)
                    qk, vs = m2("swa_qk", P, 12, S), m2("swa_v", P, 6, NT, P)
                    project(nc, W, PS, "swa_qk", blocks_of(x), evac=copy_to(qk))
                    by_class = x[:].rearrange("p k (i r) -> p k i r", r=SWA_DIL)
                    project_rows(nc, W, PS, "swa_v", lambda k, t, n: x[:, k, chunk(t)] if n < 2
                                 else by_class[:, k, :, t], NT, vs)
                    OB = OE[:, 6:8, :].rearrange("p k (i r) -> p k i r", r=SWA_DIL)
                    cls = qk[:].rearrange("p k (i r) -> p k i r", r=SWA_DIL)
                    items = []
                    for hd in range(SWA_HEADS):
                        b, o = hd // 2, slice(64 * (hd % 2), 64 * (hd % 2) + 64)
                        for r in range(SWA_DIL):
                            items.append({
                                "scores": [(0, 0, cls[o, b, :, r], qk[o, 6 + b, :], True, True)] + [
                                    (1, (g - 1) * P, cls[o, 2 * g + b, :, r], cls[o, 6 + 2 * g + b, :, r], True, True)
                                    for g in (1, 2)],
                                "logits": [(0, S, 0, 0, G0[:, hd, 3 - r:3 - r + S]),
                                           (S, P, 1, 0, G12[:, hd, 0, :]), (S + P, P, 1, P, G12[:, hd, 1, :])],
                                "scale": SWA_DIM ** -0.5, "softmaxes": [(0, S + 2 * P)],
                                "values": [lambda part, j=j, b=b, o=o: vs[:, b, j, o] for j in range(NT)] + [
                                    lambda part, g=g, b=b, r=r, o=o: vs[:, 2 * g + b, r, o] for g in (1, 2)],
                                "out": (o.start, 64, OB[o, b, :, r]),
                            })
                    attention(nc, C, PS, items, S + 2 * P, vs)
                with Memory(nc) as m2:
                    QKVZ, BETA, GAM = m2("qkvz", P, 24, S), m2("beta", GDN_HEADS, S), m2("gam", GDN_HEADS, S)
                    ST = m2("state", P, GDN_HEADS, P)
                    project(nc, W, PS, "gdn_in", blocks_of(x), evac=copy_to(QKVZ))
                    gdn_gates(nc, C, PS, x, BETA, GAM)
                    conv_silu_normalise(nc, C, PS, QKVZ)
                    clear(nc, [ST[:]])
                    for n in range(NT):
                        gdn_chunk(nc, C, PS, QKVZ, BETA, GAM, ST, OE, n)
                    head_norm(nc, C, PS, OE, GDN_HEADS, C["gdn_norm"], gate=QKVZ[:, 18:24, :])
                project(nc, W, PS, "even_out", blocks_of(OE), evac=add_to(x, ALPHA))
            deep_norm(0)
            second_ffn(0)

            with Memory(nc) as mem:
                OD = mem("o_odd", P, 8, S)
                with Memory(nc) as m2:
                    qk, vd = m2("diff_qk", P, 8, S), m2("diff_v", P, 4, NT, P)
                    project(nc, W, PS, "diff_qk", blocks_of(x), evac=copy_to(qk))
                    project_rows(nc, W, PS, "diff_v", lambda k, t, n: x[:, k, chunk(t)], NT, vd)
                    items = []
                    for hd in range(4):
                        for t in range(NT):
                            w = (t + 1) * P
                            bias = TZ[:, hd, 384 - t * P:384 - t * P + w]
                            items.append({
                                "scores": [(c, 0, qk[64 * c:64 * c + 64, hd, chunk(t)],
                                            qk[64 * c:64 * c + 64, 4 + hd, 0:w], True, True) for c in range(2)],
                                "logits": [(c * w, w, c, 0, bias) for c in range(2)], "scale": 64 ** -0.5,
                                "softmaxes": [(0, w), (w, 2 * w)],
                                "values": [lambda part, hd=hd, j=j: vd[:, hd, j, :] for j in range(t + 1)],
                                "out": (0, P, OD[:, hd, chunk(t)]),
                            })
                    attention(nc, C, PS, items, 2 * S, vd)
                    head_norm(nc, C, PS, OD, 4, C["diff_norm"], factor=1.0 - LAM_INIT)
                with Memory(nc) as m2:
                    QKR, vg, CU = m2("gla_qkr", P, 8, S), m2("gla_v", P, 4, NT, P), m2("cu", P, 2, S)
                    GD, ST = m2("g_d", 16, S), m2("state", P, 2, P)

                    def scaled_copy(n, s, steps):
                        return nc.scalar.activation(QKR[:, n, :], s, ACT.Copy, scale=64 ** -0.5 if n < 2 else 1.0)

                    project(nc, W, PS, "gla_qkr", blocks_of(x), evac=("scalar", scaled_copy))
                    project_rows(nc, W, PS, "gla_v", lambda k, t, n: x[:, k, chunk(t)], NT, vg)
                    with stage(nc, "sums", "copied") as (block, sums, copied):
                        @block.tensor
                        def _(pe):
                            for k in range(ND):
                                last = nc.tensor.matmul(PS[0][0:16, :], C["w_gd"][:, k, :], x[:, k, :], start=k == 0,
                                                        stop=k == ND - 1)
                            last.then_inc(sums, 1)

                        @block.scalar
                        def _(act):
                            act.wait_ge(sums, 1)
                            nc.scalar.activation(GD[:], PS[0][0:16, :], ACT.Copy).then_inc(copied, 1)
                            act.wait_ge(copied, 1)
                    gla_decays(nc, C, PS, GD, CU)
                    clear(nc, [ST[:]])
                    OG = OD[:, 4:8, :]
                    for n in range(NT):
                        gla_chunk(nc, C, PS, QKR[:, 0:2, :], QKR[:, 2:4, :], vg, CU, ST, OG, n)
                    head_norm(nc, C, PS, OG, 4, C["gla_norm"], gate=QKR[:, 4:8, :])
                project(nc, W, PS, "odd_out", blocks_of(OD), evac=add_to(x, ALPHA))
            deep_norm(2)
        second_ffn(1)

        with nc.Block() as block:
            @block.sync
            def _(sp):
                sp.dma_start(out, x[:]).then_inc(stored, 16)
                sp.wait_ge(stored, 16)


def columns(v):
    return np.ascontiguousarray(v.reshape(-1, P).T)


def taps(w):
    return np.ascontiguousarray(w.reshape(w.shape[0], -1, P).transpose(2, 1, 0))


def tiled(w):
    k, n = w.shape
    return np.ascontiguousarray(w.reshape(k // P, P, n // P, P).transpose(2, 1, 0, 3))


def features(a):
    return np.ascontiguousarray(a.T.reshape(-1, P, a.shape[0]).transpose(1, 0, 2))


def rows_of(w):
    return np.ascontiguousarray(w.reshape(-1, P, w.shape[1]).transpose(1, 0, 2))


def paired(w):
    r, c = w.shape
    return w.reshape(r, 2, c // 2 // P, P).transpose(0, 2, 1, 3).reshape(r, c)


def block_diagonal(w):
    out = np.zeros((P, w.shape[0] // 2, P), w.dtype)
    for i in range(w.shape[0]):
        o = 64 * (i % 2)
        out[o:o + 64, i // 2, o:o + 64] = w[i]
    return out


def shape_constants():
    f = np.float32
    i = np.arange(P)
    row, col = i[:, None], i[None, :]
    same64 = (row // 64 == col // 64).astype(f)
    level = np.stack([(row // (2 * m) == col // (2 * m)) & (row % (2 * m) < m) & (col % (2 * m) >= m)
                      for m in (1 << l for l in range(LEVELS))], axis=1).astype(f)
    pick = np.zeros((GDN_HEADS, GDN_HEADS, P), f)
    for h in range(GDN_HEADS):
        pick[h, h] = 1
    return {
        "ident": np.eye(P, dtype=f), "over_d": np.full((P, P), 1.0 / D, f), "pair_ones": same64,
        "pair_mean": np.where(same64 > 0, f(1 / 64), f(0)), "mean_head": np.full((P, P), 1.0 / P, f),
        "ones": np.ones((P, P), f), "level_mask": level, "before": (row < col).astype(f),
        "until": (row <= col).astype(f),
        "restart": np.broadcast_to((np.arange(S) % P != 0).astype(f), (P, S)).copy(), "pick": pick,
        "one_hot": one_hot_positions()[0],
    }


def kernel(**inputs):
    import concourse.bacc as _bacc
    from concourse.bass_utils import run_bass_kernel_spmd as _run

    I = {k: np.asarray(v) for k, v in inputs.items()}
    w_in, b_in = I["w_in"][0], I["b_in"][0]
    even, odd = I["w_in_even_2"][0], I["w_in_odd_2"][0]
    g = 2 * GDN_HEADS
    a = shape_constants()
    a.update({
        "x": features(I["x"][0]), "mem": features(I["mem"][0]),
        "mix_in": tiled(w_in[:, 0:2816]), "mix_gate_a": tiled(w_in[:, 2816:3840]), "mix_gate_b": tiled(w_in[:, 3840:]),
        "b_in": columns(b_in[0:2816]), "b_gates": columns(b_in[2816:]),
        "branch_a": tiled(I["w_branch_a"][0]), "branch_b": tiled(I["w_branch_b"][0]),
        "mix_out": tiled(I["w_mix_out"][0]), "cq": tiled(I["w_cq"][0]), "ck": tiled(I["w_ckv"][0][:, 0:D]),
        "cv": tiled(I["w_ckv"][0][:, D:]), "co": tiled(I["w_co"][0]),
        "ffn_in": tiled(paired(I["w_ffn_in"][0])), "ffn_out": tiled(I["w_ffn_out"][0]),
        "swa_qk": tiled(even[:, 3072 + g:3072 + g + 1536]), "swa_v": tiled(even[:, 3072 + g + 1536:]),
        "gdn_in": tiled(even[:, 0:3072]), "w_ba": rows_of(even[:, 3072:3072 + g]),
        "even_out": tiled(I["w_out_even_2"][0]),
        "diff_qk": tiled(odd[:, 0:1024]), "diff_v": tiled(odd[:, 1024:1536]),
        "gla_qkr": tiled(np.concatenate([odd[:, 1536:2048], odd[:, 2560:3072]], axis=1)),
        "gla_v": tiled(odd[:, 2048:2560]), "w_gd": rows_of(odd[:, 3072:]), "odd_out": tiled(I["w_out_odd_2"][0]),
        "w_lora": np.concatenate([I["w_lora_up"][0], I["a_lora_up"][0]], axis=0), "g_lora": I["g_lora_up"][0],
        "w_rg_a": block_diagonal(I["w_rg_a"][0]), "w_rg_x": block_diagonal(I["w_rg_x"][0]),
        "conv_b_w": taps(I["conv_b_w"][0]), "ffn_conv_w": taps(I["ffn_conv_w"][0]),
        "gdn_conv": taps(I["gdn_conv_w_2"][0]),
        "gdn_a_log": I["gdn_a_log_2"].reshape(-1, 1), "gdn_dt": I["gdn_dt_bias_2"].reshape(-1, 1),
        "gdn_norm": columns(I["gdn_norm_w_2"][0]), "diff_lp": np.ascontiguousarray(I["diff_lambda_2"][0].T),
        "diff_norm": columns(I["diff_norm_w_2"][0]), "gla_gate": I["gla_w_gate_2"][0],
        "gla_b": columns(I["gla_b_gate_2"][0]), "gla_norm": columns(I["gla_norm_w_2"][0]),
        "ffn_conv_w2": np.stack([taps(w) for w in I["ffn_conv_w_2"]], axis=1),
        "ffn_conv_b2": np.stack([columns(v) for v in I["ffn_conv_b_2"]], axis=1),
        "ln_g": np.stack([columns(v) for v in I["ln_g_2"].reshape(4, D)], axis=1),
        "ln_b": np.stack([columns(v) for v in I["ln_b_2"].reshape(4, D)], axis=1),
        "rel_bias": I["rel_bias_2"], "mu": columns(I["mu_shift"][0]), "r_k": columns(I["r_k"][0].reshape(-1)),
        "norm_final_g": columns(I["norm_final_g"]),
    })
    for layer in range(2):
        a[f"ffn_in_{layer}"] = tiled(paired(I["ffn_w_up_2"][layer]))
        a[f"ffn_out_{layer}"] = tiled(I["ffn_w_down_2"][layer])
    for name in ("norm_mix_g", "w0", "a0", "k_k", "k_a", "lnx_g", "lnx_b", "conv_b_b", "b_rg_a", "b_rg_x",
                 "lru_lambda", "norm_x_g", "norm_mem_g", "norm_ffn_g", "ffn_conv_b"):
        a[name] = columns(I[name][0])

    nc = _bacc.Bacc("TRN2", target_bir_lowering=False, num_devices=1)
    STAGES[0] = 0
    arrays, A = {}, {}
    for name, v in a.items():
        arrays[f"in_{name}_dram"] = np.ascontiguousarray(v)
        A[name] = nc.dram_tensor(f"in_{name}_dram", v.shape, F32, kind="ExternalInput").ap()
    out = nc.dram_tensor("out_0_dram", (P, ND, S), F32, kind="ExternalOutput").ap()
    scratch = nc.dram_tensor("bias_rows", (SWA_HEADS, P, a["one_hot"].shape[1]), F32, kind="Internal").ap()
    build(nc, A, out, scratch)
    r = _run(nc, [arrays], core_ids=[0])
    got = r.results[0]["out_0_dram"]
    return np.ascontiguousarray(got.transpose(1, 0, 2).reshape(D, S).T)[None]
```

```python
from contextlib import ExitStack, contextmanager
import math

import numpy as np
import concourse.bass as bass
from concourse import mybir

F32 = mybir.dt.float32
F32R = mybir.dt.float32r
ALU = mybir.AluOpType
ACT = mybir.ActivationFunctionType
AX_X = mybir.AxisListType.X

P = 128
S, D = 512, 1024
NT, ND = S // P, D // P
NMEM = 256
A_HEADS, A_DIM, A_WIDTH = 8, 64, 512
NA = A_WIDTH // P
B_WIDTH, B_CONV = 512, 4
NB = B_WIDTH // P
X_HEADS = 4
D_FF, FFN_CONV = 2816, 3
NF = D_FF // P
RWKV_BLOCKS = (3 * A_WIDTH + 64 + 64 + 128) // P
MASKED = -1e30
GDN_HEADS, GDN_CONV = 6, 4
SWA_GROUPS, SWA_HEADS, SWA_DIM = 3, 4, 64
SWA_DIL = 4
GLA_HEADS, GLA_TAU, GLA_SUB = 4, 16.0, 16
ALPHA = 4.0 ** 0.25
LEVELS = 7
NORM_EPS, LN_EPS, RMS_EPS, LNX_EPS = 1e-6, 1e-5, 1e-6, 64e-5
LAM_INIT = 0.8 - 0.6 * math.exp(-0.3)
EXP_CAP = 43.0

RING, CHUNK_K, SPLIT_RING = 5, 8, 2

G0_W, G1_W, TZ_W = 516, 256, 896


def buckets(dist):
    d = np.maximum(dist, 1).astype(np.float32)
    large = 16 + (np.log(d / np.float32(16)) / np.float32(math.log(2048 / 16)) * np.float32(16)).astype(np.int32)
    return np.where(dist < 16, dist, np.minimum(large, 31))


def one_hot_positions():
    parts = []
    e = np.arange(G0_W + 4 * 127)
    dist = 4 * 127 + 3 - e
    parts.append(np.where((dist >= 0) & (dist <= 128), buckets(np.maximum(dist, 0)), 32))
    e = np.arange(G1_W)
    step = 127 - e
    parts.append(np.where(step >= 0, buckets(np.maximum(step, 0) * 4), 32))
    parts.append(np.where((step >= 0) & (step % 4 == 0), buckets(np.maximum(step, 0) * 4), 32))
    e = np.arange(TZ_W + 127)
    dist = 127 + 384 - e
    parts.append(np.where(dist >= 0, buckets(np.maximum(dist, 0)), 32))
    at = np.cumsum([0] + [len(x) for x in parts])
    which = np.concatenate(parts)
    pad = -len(which) % 512
    which = np.concatenate([which, np.full(pad, 32)])
    return (which[None, :] == np.arange(33)[:, None]).astype(np.float32), [int(a) for a in at]


class Steps:

    def __init__(self, eng, sem):
        self.eng, self.sem, self.n = eng, sem, 0

    def __call__(self, ins):
        ins.then_inc(self.sem, 1)
        self.n += 1

    def wait(self):
        self.eng.wait_ge(self.sem, self.n)

    def one(self, ins):
        self(ins)
        self.wait()


STAGES = [0]


@contextmanager
def stage(nc, *names):
    STAGES[0] += 1
    sems = [nc.alloc_semaphore(f"{name}_{STAGES[0]}") for name in names]
    with nc.Block(no_gpsimd_drain=True) as block:
        yield (block, *sems)
    nc.clear_and_free_semaphores(sems)
    nc.all_engine_barrier(sem_only=True)


@contextmanager
def Memory(nc):
    with ExitStack() as stack:
        def tensor(name, *shape, dtype=F32):
            STAGES[0] += 1
            return stack.enter_context(nc.sbuf_tensor(f"{name}_{STAGES[0]}", list(shape), dtype))

        yield tensor


class Weights:

    def __init__(self, nc, mem, plan, rows):
        self.nc = nc
        self.slots = [mem(f"w_slot{i}", P, CHUNK_K, P) for i in range(RING)]
        self.high = [mem(f"w_high{i}", P, CHUNK_K, P, dtype=F32R) for i in range(SPLIT_RING)]
        self.low = [mem(f"w_low{i}", P, CHUNK_K, P, dtype=F32R) for i in range(SPLIT_RING)]
        self.landed = [nc.alloc_semaphore(f"w_landed{i}") for i in range(RING)]
        self.used, self.high_done, self.low_done = (nc.alloc_semaphore(f"w_{n}") for n in ("used", "high", "low"))
        self.chunks, self.first, self.shape, self.issued = [], {}, {}, 0
        self.order, self.splits, self.highs, self.lows = {}, [], 0, 0
        for name, (dram, blocks, depth) in plan.items():
            self.first[name], self.shape[name] = len(self.chunks), (blocks, depth)
            for n in range(blocks):
                for k in range(0, depth, CHUNK_K):
                    if name not in rows:
                        self.order[len(self.chunks)] = len(self.splits)
                        self.splits.append(len(self.chunks))
                    self.chunks.append((dram, n, k, min(CHUNK_K, depth - k)))

    def per(self, name):
        return -(-self.shape[name][1] // CHUNK_K)

    def done(self, name, n):
        return self.first[name] + (n + 1) * self.per(name)

    def load(self, sp, name):
        end = self.done(name, self.shape[name][0] - 1)
        while self.issued < min(len(self.chunks), end + RING):
            c = self.issued
            dram, n, k, kc = self.chunks[c]
            if c >= RING and c - RING in self.order:
                sp.wait_ge(self.low_done, self.order[c - RING] + 1)
            elif c >= RING:
                sp.wait_ge(self.used, c - RING + 1)
            sp.dma_start(self.slots[c % RING][:, 0:kc, :], dram[n, :, k:k + kc, :]).then_inc(
                self.landed[c % RING], 16)
            self.issued += 1

    def ahead(self, name, n):
        last = self.done(name, self.shape[name][0] - 1)
        return min(self.done(name, n) + SPLIT_RING, last)

    def split_high(self, act, name, n):
        while self.highs < len(self.splits) and self.splits[self.highs] < self.ahead(name, n):
            i = self.highs
            c = self.splits[i]
            kc = self.chunks[c][3]
            act.wait_ge(self.landed[c % RING], 16 * (c // RING + 1))
            if i >= SPLIT_RING:
                act.wait_ge(self.used, self.splits[i - SPLIT_RING] + 1)
            self.nc.scalar.activation(self.high[i % SPLIT_RING][:, 0:kc, :], self.slots[c % RING][:, 0:kc, :],
                                      ACT.Copy).then_inc(self.high_done, 1)
            self.highs += 1

    def split_low(self, dve, name, n):
        while self.lows < len(self.splits) and self.splits[self.lows] < self.ahead(name, n):
            i = self.lows
            c = self.splits[i]
            kc = self.chunks[c][3]
            dve.wait_ge(self.high_done, i + 1)
            self.nc.vector.tensor_tensor(self.low[i % SPLIT_RING][:, 0:kc, :], self.slots[c % RING][:, 0:kc, :],
                                         self.high[i % SPLIT_RING][:, 0:kc, :].bitcast(F32),
                                         ALU.subtract).then_inc(self.low_done, 1)
            self.lows += 1

    def sums(self, pe, name, bank, high, low, free, fresh=None):
        nc = self.nc
        blocks, depth = self.shape[name]
        for n in range(blocks):
            if free(n):
                pe.wait_ge(*free(n))
            out = bank(n)
            for part in range(self.per(name)):
                c = self.first[name] + n * self.per(name) + part
                i = self.order[c]
                wh, wl = self.high[i % SPLIT_RING], self.low[i % SPLIT_RING]
                pe.wait_ge(self.low_done, i + 1)
                for k in range(part * CHUNK_K, min(depth, (part + 1) * CHUNK_K)):
                    if n == 0 and fresh is not None:
                        pe.wait_ge(fresh, k + 1)
                    j = k - part * CHUNK_K
                    nc.tensor.matmul(out, wh[:, j, :], high[:, k, :], start=k == 0, stop=False)
                    nc.tensor.matmul(out, wh[:, j, :], low[:, k, :], start=False, stop=False)
                    last = nc.tensor.matmul(out, wl[:, j, :], high[:, k, :], start=False, stop=k == depth - 1)
                last.then_inc(self.used, 1)

    def sums_rows(self, pe, name, bank, stationary, tiles, free):
        blocks, depth = self.shape[name]
        for n in range(blocks):
            if free(n):
                pe.wait_ge(*free(n))
            c = self.first[name] + n
            slot = self.slots[c % RING]
            pe.wait_ge(self.landed[c % RING], 16 * (c // RING + 1))
            for t in range(tiles):
                for k in range(depth):
                    last = self.nc.tensor.matmul(bank(n)[:, t * P:(t + 1) * P], stationary(k, t, n), slot[:, k, :],
                                                 start=k == 0, stop=k == depth - 1)
            last.then_inc(self.used, 1)


def split_high(nc, src, high, high_ok):
    for k in range(src.shape[1]):
        nc.scalar.activation(high[:, k, :], src[:, k, :], ACT.Copy).then_inc(high_ok, 1)


def split_low(nc, dve, src, high, low, high_ok, low_ok):
    for k in range(src.shape[1]):
        dve.wait_ge(high_ok, k + 1)
        nc.vector.tensor_tensor(low[:, k, :], src[:, k, :], high[:, k, :].bitcast(F32), ALU.subtract).then_inc(
            low_ok, 1)


def project(nc, W, PS, name, src=None, halves=None, evac=None, banks=4):
    who, emit = evac
    blocks, depth = W.shape[name]
    width = (src if src is not None else halves[0]).shape[2]
    with stage(nc, "read_out", "high_ok", "low_ok", "own") as (block, read_out, high_ok, low_ok, own), \
            Memory(nc) as mem:
        if halves is None:
            halves = [mem(n, P, depth, width, dtype=F32R) for n in ("act_high", "act_low")]
        high, low = halves

        @block.sync
        def _(sp):
            W.load(sp, name)

        @block.tensor
        def _(pe):
            W.sums(pe, name, lambda n: PS[n % banks][:, 0:width], high, low,
                   lambda n: (read_out, n - banks + 1) if n >= banks else None,
                   fresh=low_ok if src is not None else None)

        def read(eng, n, steps):
            eng.wait_ge(W.used, W.done(name, n))
            emit(n, PS[n % banks][:, 0:width], steps).then_inc(read_out, 1)

        @block.scalar
        def _(act):
            steps = Steps(act, own)
            W.split_high(act, name, -1)
            if src is not None:
                split_high(nc, src, high, high_ok)
            for n in range(blocks):
                W.split_high(act, name, n)
                if who == "scalar":
                    read(act, n, steps)
            if who == "scalar":
                act.wait_ge(read_out, blocks)

        @block.vector
        def _(dve):
            steps = Steps(dve, own)
            W.split_low(dve, name, -1)
            if src is not None:
                split_low(nc, dve, src, high, low, high_ok, low_ok)
            for n in range(blocks):
                W.split_low(dve, name, n)
                if who == "vector":
                    read(dve, n, steps)
            if who == "vector":
                dve.wait_ge(read_out, blocks)


def normalise(nc, C, PS, src, dst, gain, width=S, bias=None, eps=NORM_EPS, scratch=None, final=None):
    centred = dst if bias is not None else src
    final = dst if final is None else final
    squares = scratch if bias is not None else dst
    with stage(nc, "centred", "squared", "mean", "var", "rstd", "own") as (
            block, centred_ok, squared, mean_ok, var_ok, rstd_ok, own), Memory(nc) as mem:
        rstd = mem("rstd", P, width)
        mean, var = PS[0][:, 0:width], PS[1][:, 0:width]

        @block.tensor
        def _(pe):
            if bias is not None:
                for k in range(ND):
                    last = nc.tensor.matmul(mean, C["over_d"][:], src[:, k, :], start=k == 0, stop=k == ND - 1)
                last.then_inc(mean_ok, 1)
            for k in range(ND):
                pe.wait_ge(squared, k + 1)
                last = nc.tensor.matmul(var, C["over_d"][:], squares[:, k, :], start=k == 0, stop=k == ND - 1)
            last.then_inc(var_ok, 1)

        @block.scalar
        def _(act):
            for k in range(ND):
                if bias is not None:
                    act.wait_ge(centred_ok, k + 1)
                nc.scalar.activation(squares[:, k, :], centred[:, k, :], ACT.Square).then_inc(squared, 1)
            act.wait_ge(rstd_ok, 1)
            nc.scalar.activation(rstd[:], rstd[:], ACT.Ln).then_inc(rstd_ok, 1)
            act.wait_ge(rstd_ok, 2)
            nc.scalar.activation(rstd[:], rstd[:], ACT.Exp, scale=-0.5).then_inc(rstd_ok, 1)

        @block.vector
        def _(dve):
            if bias is not None:
                dve.wait_ge(mean_ok, 1)
                for k in range(ND):
                    nc.vector.tensor_tensor(dst[:, k, :], src[:, k, :], mean, ALU.subtract).then_inc(centred_ok, 1)
            dve.wait_ge(var_ok, 1)
            nc.vector.tensor_scalar(rstd[:], var, eps, None, ALU.add).then_inc(rstd_ok, 1)
            dve.wait_ge(rstd_ok, 3)
            steps = Steps(dve, own)
            for k in range(ND):
                steps(nc.vector.scalar_tensor_tensor(final[:, k, :], centred[:, k, :], gain[:, k:k + 1], rstd[:],
                                                     ALU.mult, ALU.mult))
            if bias is not None:
                steps.wait()
                for k in range(ND):
                    steps(nc.vector.tensor_scalar(final[:, k, :], final[:, k, :], bias[:, k:k + 1], None, ALU.add))
            steps.wait()


def unit_lower_inverse(nc, C, PS, MT, TT, T, BT, W1, heads):
    groups = [(a, min(a + 4, heads)) for a in range(0, heads, 4)]
    with stage(nc, "first", "masked", "bt_sums", "bt_ready", "t_sums", "tt_ready") as (
            block, first, masked, bt_sums, bt_ready, t_sums, tt_ready):
        G = len(groups)

        @block.gpsimd
        def _(pool):
            for level in range(1, LEVELS):
                for g, (a, b) in enumerate(groups):
                    if level > 1:
                        pool.wait_ge(bt_sums, (level - 1) * G + g + 1)
                    nc.gpsimd.tensor_tensor(BT[:, a:b, :], MT[:, a:b, :],
                                            C["level_mask"][:, level:level + 1, :].broadcast_to([P, b - a, P]),
                                            ALU.mult).then_inc(masked, 1)

        @block.tensor
        def _(pe):
            for g, (a, b) in enumerate(groups):
                pe.wait_ge(first, 2 * g + 2)
                for h in range(a, b):
                    last = nc.tensor.transpose(PS[3 * g][:, (h - a) * P:(h - a + 1) * P], TT[:, h, :], C["ident"][:])
                last.then_inc(bt_sums, 1)
            for level in range(1, LEVELS):
                for g, (a, b) in enumerate(groups):
                    if level == 1:
                        pe.wait_ge(bt_ready, g + 1)
                    else:
                        pe.wait_ge(tt_ready, (level - 1) * G + g + 1)
                    pe.wait_ge(masked, (level - 1) * G + g + 1)
                    for h in range(a, b):
                        last = nc.tensor.matmul(PS[3 * g][:, (h - a) * P:(h - a + 1) * P], BT[:, h, :], T[:, h, :],
                                                start=True, stop=True)
                    last.then_inc(bt_sums, 1)
                for g, (a, b) in enumerate(groups):
                    pe.wait_ge(bt_ready, level * G + g + 1)
                    for h in range(a, b):
                        o = slice((h - a) * P, (h - a + 1) * P)
                        if level < LEVELS - 1:
                            nc.tensor.matmul(PS[3 * g + 1][:, o], TT[:, h, :], W1[:, h, :], start=True, stop=True)
                        last = nc.tensor.matmul(PS[3 * g + 2][:, o], W1[:, h, :], TT[:, h, :], start=True, stop=True)
                    last.then_inc(t_sums, 1)

        @block.scalar
        def _(act):
            for level in range(LEVELS):
                for g, (a, b) in enumerate(groups):
                    act.wait_ge(bt_sums, level * G + g + 1)
                    if level > 1:
                        act.wait_ge(t_sums, (level - 2) * G + g + 1)
                    nc.scalar.activation((W1 if level else T)[:, a:b, :], PS[3 * g][:, 0:(b - a) * P].rearrange(
                        "p (h t) -> p h t", t=P), ACT.Copy).then_inc(bt_ready, 1)

        @block.vector
        def _(dve):
            for g, (a, b) in enumerate(groups):
                n = b - a
                nc.vector.tensor_tensor(TT[:, a:b, :], MT[:, a:b, :],
                                        C["level_mask"][:, 0:1, :].broadcast_to([P, n, P]), ALU.mult).then_inc(first, 1)
                dve.wait_ge(first, 2 * g + 1)
                nc.vector.tensor_tensor(TT[:, a:b, :], TT[:, a:b, :],
                                        C["ident"][:, None, :].broadcast_to([P, n, P]), ALU.add).then_inc(first, 1)
            for g in range(G):
                dve.wait_ge(bt_ready, g + 1)
                nc.vector.memset(C["spare"][:, g:g + 1], 0.0).then_inc(tt_ready, 1)
            for level in range(1, LEVELS):
                for g, (a, b) in enumerate(groups):
                    dve.wait_ge(t_sums, (level - 1) * G + g + 1)
                    if level < LEVELS - 1:
                        nc.vector.tensor_tensor(T[:, a:b, :], T[:, a:b, :], PS[3 * g + 1][:, 0:(b - a) * P].rearrange(
                            "p (h t) -> p h t", t=P), ALU.add)
                    nc.vector.tensor_tensor(TT[:, a:b, :], TT[:, a:b, :], PS[3 * g + 2][:, 0:(b - a) * P].rearrange(
                        "p (h t) -> p h t", t=P), ALU.add).then_inc(tt_ready, 1)
            dve.wait_ge(tt_ready, LEVELS * G)


def attention(nc, C, PS, items, width, values):
    with stage(nc, "scores_ready", "logits_ready", "max_ready", "exp_ready", "probs_ready", "turned", "turned_sb",
               "pv_ready", "out_ready", "own") as (
            block, scores_ready, logits_ready, max_ready, exp_ready, probs_ready, turned, turned_sb, pv_ready,
            out_ready, own), Memory(nc) as mem:
        L = [mem(f"logits{i}", P, width) for i in range(2)]
        PT = [mem(f"probs_turned{i}", P, width) for i in range(2)]
        nmax = mem("nmax", P, 2, 2)
        tot = mem("tot", P, 2, 2)
        N = len(items)

        @block.tensor
        def _(pe):
            def turn(t):
                it, par = items[t], t % 2
                pe.wait_ge(probs_ready, t + 1)
                if t:
                    pe.wait_ge(turned_sb, t)
                for j in range(len(it["values"])):
                    last = nc.tensor.transpose(PS[4 + j // 4][:, (j % 4) * P:(j % 4 + 1) * P],
                                               L[par][:, j * P:(j + 1) * P], C["ident"][:])
                last.then_inc(turned, 1)

            def pv(t):
                it, par = items[t], t % 2
                pe.wait_ge(turned_sb, t + 1)
                if t >= 2:
                    pe.wait_ge(out_ready, t - 1)
                p0, rows, _ = it["out"]
                n = len(it["values"])
                parts = it.get("parts", 1)
                for q in range(parts):
                    for j in range(n):
                        last = nc.tensor.matmul(PS[6 + par][p0:p0 + rows, q * P:(q + 1) * P],
                                                it["values"][j](q), PT[par][:, j * P:(j + 1) * P],
                                                start=j == 0, stop=j == n - 1)
                last.then_inc(pv_ready, 1)

            for t in range(N + 2):
                if t < N:
                    if t >= 2:
                        pe.wait_ge(logits_ready, t - 1)
                    for bank, c, lhsT, rhs, start, stop in items[t]["scores"]:
                        last = nc.tensor.matmul(PS[2 * (t % 2) + bank][:, c:c + rhs.shape[-1]], lhsT, rhs,
                                                start=start, stop=stop)
                    last.then_inc(scores_ready, 1)
                if 1 <= t <= N:
                    turn(t - 1)
                if t >= 2:
                    pv(t - 2)

        @block.vector
        def _(dve):
            steps = Steps(dve, own)

            def weigh(t):
                it, par = items[t], t % 2
                dve.wait_ge(exp_ready, t + 1)
                sm = it["softmaxes"]
                steps.one(nc.vector.reciprocal(tot[:, par, 0:len(sm)], tot[:, par, 0:len(sm)]))
                (a, b), *more = sm
                if more:
                    c, d = more[0]
                    steps(nc.vector.tensor_scalar(L[par][:, c:d], L[par][:, c:d], tot[:, par, 1:2], C["lam"][:, 0:1],
                                                  ALU.mult, ALU.mult))
                    steps.wait()
                    nc.vector.scalar_tensor_tensor(L[par][:, a:b], L[par][:, a:b], tot[:, par, 0:1], L[par][:, c:d],
                                                   ALU.mult, ALU.subtract).then_inc(probs_ready, 1)
                else:
                    nc.vector.tensor_scalar(L[par][:, a:b], L[par][:, a:b], tot[:, par, 0:1], None,
                                            ALU.mult).then_inc(probs_ready, 1)

            for t in range(N + 1):
                if t < N:
                    it, par = items[t], t % 2
                    dve.wait_ge(scores_ready, t + 1)
                    if t >= 2:
                        dve.wait_ge(turned, t - 1)
                    for i, (c, w, bank, pc, bias) in enumerate(it["logits"]):
                        dst, src = L[par][:, c:c + w], PS[2 * par + bank][:, pc:pc + w]
                        if bias is None:
                            ins = nc.vector.tensor_scalar(dst, src, it["scale"], None, ALU.mult)
                        else:
                            ins = nc.vector.scalar_tensor_tensor(dst, src, it["scale"], bias, ALU.mult, ALU.add)
                        if i < len(it["logits"]) - 1:
                            steps(ins)
                        else:
                            ins.then_inc(logits_ready, 1)
                    steps.wait()
                    dve.wait_ge(logits_ready, t + 1)
                    for i, (a, b) in enumerate(it["softmaxes"]):
                        steps(nc.vector.reduce_max(nmax[:, par, i:i + 1], L[par][:, a:b], AX_X))
                    steps.wait()
                    n = len(it["softmaxes"])
                    nc.vector.tensor_scalar(nmax[:, par, 0:n], nmax[:, par, 0:n], -1.0, None,
                                            ALU.mult).then_inc(max_ready, 1)
                if t >= 1:
                    weigh(t - 1)

        @block.scalar
        def _(act):
            for t in range(N + 2):
                if t < N:
                    it, par = items[t], t % 2
                    act.wait_ge(max_ready, t + 1)
                    for i, (a, b) in enumerate(it["softmaxes"]):
                        ins = nc.scalar.activation(L[par][:, a:b], L[par][:, a:b], ACT.Exp, bias=nmax[:, par, i:i + 1],
                                                   accum_out=tot[:, par, i:i + 1])
                    ins.then_inc(exp_ready, 1)
                if 1 <= t <= N:
                    par, n = (t - 1) % 2, len(items[t - 1]["values"])
                    act.wait_ge(turned, t)
                    if t >= 3:
                        act.wait_ge(pv_ready, t - 2)
                    for bank in range(-(-n // 4)):
                        w = min(4, n - 4 * bank) * P
                        ins = nc.scalar.activation(PT[par][:, 4 * bank * P:4 * bank * P + w], PS[4 + bank][:, 0:w],
                                                   ACT.Copy)
                    ins.then_inc(turned_sb, 1)
                if t >= 2:
                    it, par = items[t - 2], t % 2
                    p0, rows, dst = it["out"]
                    act.wait_ge(pv_ready, t - 1)
                    src = PS[6 + par][p0:p0 + rows, 0:it.get("parts", 1) * P]
                    if it.get("parts", 1) > 1:
                        src = src.rearrange("p (a b) -> p a b", b=P)
                    nc.scalar.activation(dst, src, ACT.Copy).then_inc(out_ready, 1)
            act.wait_ge(out_ready, N)


def chunk(n):
    return slice(n * P, (n + 1) * P)


def causal_conv(nc, steps, dst, src, taps, bias, width):
    last = taps.shape[1] - 1
    steps.one(nc.vector.tensor_scalar(dst, src, taps[:, last:last + 1], bias, ALU.mult, ALU.add)
              if bias is not None else nc.vector.tensor_scalar(dst, src, taps[:, last:last + 1], None, ALU.mult))
    for j in range(1, last + 1):
        ins = nc.vector.scalar_tensor_tensor(dst[:, j:], src[:, 0:width - j], taps[:, last - j:last - j + 1],
                                             dst[:, j:], ALU.mult, ALU.add)
        if j < last:
            steps.one(ins)
    return ins


def mixer_projection(nc, C, W, PS, h, M, PXY):
    with stage(nc, "evacuated", "mixed", "high_ok", "low_ok", "own") as (
            block, evacuated, mixed, high_ok, low_ok, own), Memory(nc) as mem:
        high, low = (mem(n, P, ND, S, dtype=F32R) for n in ("act_high", "act_low"))
        raw = [mem(f"raw{i}", P, S) for i in range(2)]
        diff = mem("diff", P, S)
        blocks = W.shape["mix_in"][0]

        @block.sync
        def _(sp):
            W.load(sp, "mix_in")

        @block.tensor
        def _(pe):
            W.sums(pe, "mix_in", lambda n: PS[n % 4][:], high, low,
                   lambda n: (evacuated, n - 3) if n >= 4 else None, fresh=low_ok)

        @block.scalar
        def _(act):
            W.split_high(act, "mix_in", -1)
            split_high(nc, h, high, high_ok)
            for n in range(blocks):
                W.split_high(act, "mix_in", n)
                act.wait_ge(W.used, W.done("mix_in", n))
                if 2 <= n < RWKV_BLOCKS:
                    act.wait_ge(mixed, n - 1)
                dst = raw[n % 2][:] if n < RWKV_BLOCKS else PXY[:, n - RWKV_BLOCKS, :]
                nc.scalar.activation(dst, PS[n % 4][:], ACT.Identity, bias=C["b_in"][:, n:n + 1]).then_inc(evacuated, 1)
            act.wait_ge(evacuated, blocks)

        @block.vector
        def _(dve):
            steps = Steps(dve, own)
            W.split_low(dve, "mix_in", -1)
            split_low(nc, dve, h, high, low, high_ok, low_ok)
            for n in range(blocks):
                W.split_low(dve, "mix_in", n)
                if n >= RWKV_BLOCKS:
                    continue
                p = raw[n % 2]
                dve.wait_ge(evacuated, n + 1)
                if n:
                    dve.wait_ge(mixed, n)
                steps(nc.vector.tensor_tensor(diff[:, 1:], p[:, 0:S - 1], p[:, 1:], ALU.subtract))
                steps(nc.vector.tensor_scalar(diff[:, 0:1], p[:, 0:1], -1.0, None, ALU.mult))
                steps.wait()
                nc.vector.scalar_tensor_tensor(M[:, n, :], diff[:], C["mu"][:, n:n + 1], p[:], ALU.mult,
                                               ALU.add).then_inc(mixed, 1)
            dve.wait_ge(mixed, RWKV_BLOCKS)


def griffin(nc, C, PS, PXY, YB):
    with stage(nc, "conv", "gates", "act_done", "dve_done", "own_a", "own_v") as (
            block, conv, gates, act_done, dve_done, own_a, own_v), Memory(nc) as mem:
        xb, ga, gx = mem("xb", P, NB, S), mem("ga", P, NB, S), mem("gx", P, NB, S)
        t, den = mem("t", P, NB, S), mem("den", P, NB, S)
        col = mem("col", P, 4, NB)
        lam8 = col[:, 3, :]

        @block.tensor
        def _(pe):
            for k in range(NB):
                pe.wait_ge(conv, k + 1)
                nc.tensor.matmul(PS[2 * k][:], C["w_rg_a"][:, k, :], xb[:, k, :], start=True, stop=True)
                nc.tensor.matmul(PS[2 * k + 1][:], C["w_rg_x"][:, k, :], xb[:, k, :], start=True,
                                 stop=True).then_inc(gates, 1)

        @block.scalar
        def _(act):
            steps = Steps(act, own_a)
            steps.one(nc.scalar.activation(col[:, 0, :], C["lru_lambda"][:], ACT.Abs))
            nc.scalar.activation(col[:, 1, :], col[:, 0, :], ACT.Exp, scale=-1.0).then_inc(act_done, 1)
            act.wait_ge(dve_done, 1)
            nc.scalar.activation(col[:, 2, :], col[:, 1, :], ACT.Ln).then_inc(act_done, 1)
            for k in range(NB):
                act.wait_ge(gates, k + 1)
                nc.scalar.activation(ga[:, k, :], PS[2 * k][:], ACT.Sigmoid, bias=C["b_rg_a"][:, k:k + 1])
                nc.scalar.activation(gx[:, k, :], PS[2 * k + 1][:], ACT.Sigmoid,
                                     bias=C["b_rg_x"][:, k:k + 1]).then_inc(act_done, 1)
            act.wait_ge(dve_done, 2)
            nc.scalar.activation(t[:], ga[:], ACT.Tanh, scale=-1.0).then_inc(act_done, 1)
            act.wait_ge(act_done, 3 + NB)
            nc.scalar.activation(ga[:], ga[:], ACT.Exp)
            nc.scalar.activation(YB[:], PXY[:, NB:2 * NB, :], ACT.Gelu_apprx_tanh)
            act.wait_ge(dve_done, 3)
            nc.scalar.activation(t[:], t[:], ACT.Sqrt).then_inc(act_done, 1)

        @block.vector
        def _(dve):
            steps = Steps(dve, own_v)
            for k in range(NB):
                causal_conv(nc, steps, xb[:, k, :], PXY[:, k, :], C["conv_b_w"][:, k, :], C["conv_b_b"][:, k:k + 1],
                            S).then_inc(conv, 1)
            steps.one(nc.vector.tensor_scalar(lam8, C["lru_lambda"][:], 0.0, None, ALU.min))
            dve.wait_ge(act_done, 1)
            nc.vector.tensor_scalar(col[:, 1, :], col[:, 1, :], 1.0, None, ALU.add).then_inc(dve_done, 1)
            dve.wait_ge(act_done, 2)
            steps.one(nc.vector.tensor_tensor(lam8, lam8, col[:, 2, :], ALU.subtract))
            steps.one(nc.vector.tensor_scalar(lam8, lam8, 8.0, None, ALU.mult))
            dve.wait_ge(act_done, 2 + NB)
            for k in range(NB):
                ins = nc.vector.tensor_scalar(ga[:, k, :], ga[:, k, :], lam8[:, k:k + 1], None, ALU.mult)
                if k < NB - 1:
                    steps(ins)
            ins.then_inc(dve_done, 1)
            dve.wait_ge(act_done, 3 + NB)
            steps.one(nc.vector.tensor_scalar(den[:], t[:], 1.0, None, ALU.add))
            steps.one(nc.vector.reciprocal(den[:], den[:]))
            nc.vector.scalar_tensor_tensor(t[:], t[:], 2.0, den[:], ALU.mult, ALU.mult).then_inc(dve_done, 1)
            steps.one(nc.vector.tensor_tensor(xb[:], xb[:], gx[:], ALU.mult))
            dve.wait_ge(act_done, 4 + NB)
            steps.one(nc.vector.memset(t[:, :, 0:1], 1.0))
            steps.one(nc.vector.tensor_tensor(xb[:], xb[:], t[:], ALU.mult))
            for k in range(NB):
                steps(nc.vector.tensor_tensor_scan(den[:, k, :], ga[:, k, :], xb[:, k, :], 0.0, ALU.mult, ALU.add))
            steps.wait()
            steps.one(nc.vector.tensor_tensor(YB[:], YB[:], den[:], ALU.mult))


def rwkv_prepare(nc, C, PS, M, LD, CU, KN, BV):
    r, k, v = (M[:, 4 * i:4 * i + 4, :] for i in range(3))
    with stage(nc, "squashed", "lora", "act_done", "dve_done", "head_sums", "own_v") as (
            block, squashed, lora, act_done, dve_done, head_sums, own_v), Memory(nc) as mem:
        tmp = mem("tmp", P, NA, S)
        wide = mem("wide", P, S)
        scaled = mem("scaled", P, S)

        @block.tensor
        def _(pe):
            pe.wait_ge(squashed, 1)
            for n in range(NA):
                nc.tensor.matmul(PS[n][:], C["w_lora"][0:64, chunk(n)], wide[0:64, :], start=True, stop=True)
                last = nc.tensor.matmul(PS[4 + n][:], C["w_lora"][64:128, chunk(n)], M[64:128, 12, :], start=True,
                                        stop=True)
            last.then_inc(lora, 1)
            pe.wait_ge(dve_done, 1)
            for n in range(NA):
                last = nc.tensor.matmul(PS[4 + n][:], C["pair_ones"][:], tmp[:, n, :], start=True, stop=True)
            last.then_inc(head_sums, 1)

        @block.scalar
        def _(act):
            nc.scalar.activation(wide[0:64, :], M[0:64, 12, :], ACT.Tanh).then_inc(squashed, 1)
            act.wait_ge(lora, 1)
            for n in range(NA):
                nc.scalar.activation(LD[:, n, :], PS[n][:], ACT.Sigmoid, bias=C["w0"][:, n:n + 1])
                ins = nc.scalar.activation(BV[:, n, :], PS[4 + n][:], ACT.Sigmoid, bias=C["a0"][:, n:n + 1])
            ins.then_inc(act_done, 1)
            act.wait_ge(head_sums, 1)
            for n in range(NA):
                ins = nc.scalar.activation(tmp[:, n, :], PS[4 + n][:], ACT.Sqrt)
            ins.then_inc(act_done, 1)

        @block.vector
        def _(dve):
            steps = Steps(dve, own_v)
            for n in range(NA):
                steps(nc.vector.tensor_scalar(KN[:, n, :], k[:, n, :], C["k_k"][:, n:n + 1], None, ALU.mult))
            steps.wait()
            dve.wait_ge(act_done, 1)
            nc.vector.tensor_tensor(tmp[:], KN[:], KN[:], ALU.mult).then_inc(dve_done, 1)
            steps.one(nc.vector.tensor_scalar(LD[:], LD[:], -math.exp(-0.5), None, ALU.mult))
            for n in range(NA):
                steps(nc.vector.tensor_tensor_scan(CU[:, n, :], C["restart"][:], LD[:, n, :], 0.0, ALU.mult, ALU.add))
            for n in range(NA):
                steps.one(nc.vector.tensor_scalar(scaled[:], BV[:, n, :], 1.0,
                                                  C["k_a"][:, n:n + 1], ALU.subtract, ALU.mult))
                steps.one(nc.vector.scalar_tensor_tensor(k[:, n, :], scaled[:], 1.0, k[:, n, :], ALU.add, ALU.mult))
            dve.wait_ge(act_done, 2)
            steps.one(nc.vector.tensor_scalar(tmp[:], tmp[:], 1e-12, None, ALU.max))
            steps.one(nc.vector.reciprocal(tmp[:], tmp[:]))
            steps.one(nc.vector.tensor_tensor(KN[:], KN[:], tmp[:], ALU.mult))
            steps.one(nc.vector.tensor_tensor(BV[:], BV[:], KN[:], ALU.mult))


def rwkv_chunk(nc, C, PS, M, LD, CU, KN, BV, ST, Y, n):
    t = chunk(n)
    r, k, v = (M[:, 4 * i:4 * i + 4, t] for i in range(3))
    ld, cu, kn, bv = LD[:, :, t], CU[:, :, t], KN[:, :, t], BV[:, :, t]
    with Memory(nc) as mem:
        R0, A0 = mem("r_start", P, NA, P), mem("a_start", P, NA, P)
        T, BT, W1 = (mem(x, P, A_HEADS, P) for x in ("t", "bt", "w1"))
        (RT, AT), (KT, BTT), (KE, BE) = ((a[:, 0:NA, :], a[:, NA:A_HEADS, :]) for a in (T, BT, W1))
        VT, KET, BET = (mem(x, P, A_WIDTH) for x in ("v_rows", "k_end_rows", "b_end_rows"))
        gend = mem("gend", P, NA)
        with stage(nc, "exponent", "expd", "own_v", "own_a") as (block, exponent, expd, own_v, own_a), \
                Memory(nc) as mem2:
            X = [mem2(f"x{i}", P, NA, P) for i in range(6)]
            mid = CU[:, :, n * P + 63:n * P + 64].broadcast_to([P, NA, P])
            end = CU[:, :, n * P + P - 1:n * P + P].broadcast_to([P, NA, P])

            @block.vector
            def _(dve):
                steps = Steps(dve, own_v)
                steps(nc.vector.tensor_tensor(X[0][:], cu, mid, ALU.subtract))
                steps(nc.vector.tensor_tensor(X[5][:], cu, ld, ALU.subtract))
                steps(nc.vector.tensor_tensor(X[3][:], end, cu, ALU.subtract))
                steps.wait()
                nc.vector.tensor_tensor(X[1][:], X[0][:], ld, ALU.subtract).then_inc(exponent, 1)
                dve.wait_ge(expd, 1)
                steps(nc.vector.tensor_tensor(RT, r, X[0][:], ALU.mult))
                steps(nc.vector.scalar_tensor_tensor(AT, kn, -1.0, X[1][:], ALU.mult, ALU.mult))
                steps(nc.vector.tensor_tensor(KT, k, X[2][:], ALU.mult))
                steps(nc.vector.tensor_tensor(BTT, bv, X[2][:], ALU.mult))
                steps(nc.vector.tensor_tensor(KE, k, X[3][:], ALU.mult))
                steps(nc.vector.tensor_tensor(BE, bv, X[3][:], ALU.mult))
                steps(nc.vector.tensor_tensor(R0[:], r, X[4][:], ALU.mult))
                steps(nc.vector.scalar_tensor_tensor(A0[:], kn, -1.0, X[5][:], ALU.mult, ALU.mult))
                steps.wait()

            @block.scalar
            def _(act):
                steps = Steps(act, own_a)
                steps(nc.scalar.activation(X[4][:], cu, ACT.Exp))
                steps(nc.scalar.activation(gend[:], CU[:, :, n * P + P - 1], ACT.Exp))
                act.wait_ge(exponent, 1)
                steps(nc.scalar.activation(X[2][:], X[0][:], ACT.Exp, scale=-1.0))
                steps.wait()
                steps(nc.scalar.activation(X[0][:], X[0][:], ACT.Exp))
                steps(nc.scalar.activation(X[3][:], X[3][:], ACT.Exp))
                steps(nc.scalar.activation(X[5][:], X[5][:], ACT.Exp))
                nc.scalar.activation(X[1][:], X[1][:], ACT.Exp).then_inc(expd, 1)

        MAB, MAK, MRB, MRK, TT = (mem(x, P, A_HEADS, P) for x in ("m_ab", "m_ak", "m_rb", "m_rk", "tt"))
        pairs = [(BTT, AT, MAB, C["before"]), (KT, AT, MAK, C["before"]), (BTT, RT, MRB, C["until"]), (KT, RT, MRK, C["until"])]
        with stage(nc, "scored", "kept", "turned", "rows_ready") as (block, scored, kept, turned, rows_ready):
            @block.tensor
            def _(pe):
                for i, (left, right, _, _) in enumerate(pairs):
                    for half in range(2):
                        m = 2 * i + half
                        if m >= 5:
                            pe.wait_ge(kept, m - 4)
                        for q in range(4):
                            o = slice(64 * half, 64 * half + 64)
                            last = nc.tensor.matmul(PS[m % 5][:, chunk(q)], left[o, q, :], right[o, q, :],
                                                    start=True, stop=True)
                        last.then_inc(scored, 1)
                for i, src in enumerate((v, KE, BE)):
                    for j in range(NA):
                        last = nc.tensor.transpose(PS[5 + i][:, chunk(j)], src[:, j, :], C["ident"][:])
                    last.then_inc(turned, 1)

            @block.scalar
            def _(act):
                for i, dst in enumerate((VT, KET, BET)):
                    act.wait_ge(turned, i + 1)
                    nc.scalar.activation(dst[:], PS[5 + i][:], ACT.Copy).then_inc(rows_ready, 1)
                act.wait_ge(rows_ready, 3)

            @block.vector
            def _(dve):
                for i, (_, _, dst, mask) in enumerate(pairs):
                    for half in range(2):
                        m = 2 * i + half
                        dve.wait_ge(scored, m + 1)
                        nc.vector.tensor_tensor(dst[:, half::2, :],
                                                PS[m % 5][:].rearrange("p (h t) -> p h t", t=P),
                                                mask[:, None, :].broadcast_to([P, 4, P]), ALU.mult).then_inc(kept, 1)
                dve.wait_ge(kept, 8)

        unit_lower_inverse(nc, C, PS, MAB, TT, T, BT, W1, A_HEADS)

        with stage(nc, "sums", "read", "state") as (block, sums, read, state):
            R, U = (W1[:, i:i + 4, :].rearrange("p h t -> p (h t)") for i in (0, 4))

            @block.tensor
            def _(pe):
                for j in range(NA):
                    nc.tensor.matmul(PS[0][:, chunk(j)], A0[:, j, :], ST[:, j, :], start=j == 0, stop=False,
                                     skip_group_check=True)
                for h in range(A_HEADS):
                    o = slice(64 * h, 64 * h + 64)
                    last = nc.tensor.matmul(PS[0][:, o], MAK[:, h, :], VT[:, o], start=False, stop=h == A_HEADS - 1,
                                            skip_group_check=True)
                last.then_inc(sums, 1)
                pe.wait_ge(read, 1)
                for h in range(A_HEADS):
                    o = slice(64 * h, 64 * h + 64)
                    last = nc.tensor.matmul(PS[1][:, o], TT[:, h, :], R[:, o], start=True, stop=True)
                last.then_inc(sums, 1)
                pe.wait_ge(read, 2)
                for j in range(NA):
                    nc.tensor.matmul(PS[2][:, chunk(j)], ST[:, j, :], R0[:, j, :], start=j == 0, stop=False,
                                     skip_group_check=True)
                for h in range(A_HEADS):
                    o, q = slice(64 * h, 64 * h + 64), slice(64 * (h % 2), 64 * (h % 2) + 64)
                    nc.tensor.matmul(PS[2][q, chunk(h // 2)], U[:, o], MRB[:, h, :], start=False, stop=False,
                                     skip_group_check=True)
                    last = nc.tensor.matmul(PS[2][q, chunk(h // 2)], VT[:, o], MRK[:, h, :], start=False,
                                            stop=h >= A_HEADS - 2, skip_group_check=True)
                last.then_inc(sums, 1)
                for j in range(NA):
                    nc.tensor.matmul(PS[3][:, chunk(j)], KET[:, chunk(j)], VT[:, chunk(j)], start=True, stop=False,
                                     skip_group_check=True)
                    last = nc.tensor.matmul(PS[3][:, chunk(j)], BET[:, chunk(j)], U[:, chunk(j)], start=False,
                                            stop=True, skip_group_check=True)
                last.then_inc(sums, 1)

            @block.scalar
            def _(act):
                act.wait_ge(sums, 1)
                nc.scalar.activation(R, PS[0][:], ACT.Copy).then_inc(read, 1)
                act.wait_ge(sums, 2)
                nc.scalar.activation(U, PS[1][:], ACT.Copy).then_inc(read, 1)
                act.wait_ge(sums, 3)
                nc.scalar.activation(Y[:, :, t], PS[2][:].rearrange("p (j t) -> p j t", t=P), ACT.Copy).then_inc(
                    read, 1)
                act.wait_ge(read, 3)

            @block.vector
            def _(dve):
                dve.wait_ge(sums, 4)
                for j in range(NA):
                    for q in (slice(0, 64), slice(64, 128)):
                        o = slice(j * P + q.start, j * P + q.stop)
                        nc.vector.scalar_tensor_tensor(ST[q, j, q], ST[q, j, q], gend[q, j:j + 1], PS[3][q, o],
                                                       ALU.mult, ALU.add).then_inc(state, 1)
                dve.wait_ge(state, 2 * NA)


def rwkv_finish(nc, C, PS, M, Y):
    r, k, v = (M[:, 4 * i:4 * i + 4, :] for i in range(3))
    with stage(nc, "gated", "mean", "var", "bonus", "dve_done", "act_done", "own_v") as (
            block, gated, mean, var, bonus, dve_done, act_done, own_v), Memory(nc) as mem:
        rk, sq, rstd = mem("rk", P, NA, S), mem("sq", P, NA, S), mem("rstd", P, NA, S)
        G = mem("g", P, NA, S)

        @block.tensor
        def _(pe):
            pe.wait_ge(act_done, 1)
            for j in range(NA):
                last = nc.tensor.matmul(PS[4 + j][:], C["g_lora"][:, chunk(j)], M[:, 13, :], start=True, stop=True)
            last.then_inc(gated, 1)
            for j in range(NA):
                last = nc.tensor.matmul(PS[j][:], C["pair_mean"][:], Y[:, j, :], start=True, stop=True)
            last.then_inc(mean, 1)
            pe.wait_ge(act_done, 2)
            pe.wait_ge(dve_done, 1)
            for j in range(NA):
                last = nc.tensor.matmul(PS[4 + j][:], C["pair_ones"][:], rk[:, j, :], start=True, stop=True)
            last.then_inc(bonus, 1)
            pe.wait_ge(act_done, 3)
            for j in range(NA):
                last = nc.tensor.matmul(PS[j][:], C["pair_mean"][:], sq[:, j, :], start=True, stop=True)
            last.then_inc(var, 1)

        @block.scalar
        def _(act):
            nc.scalar.activation(M[:, 13, :], M[:, 13, :], ACT.Sigmoid).then_inc(act_done, 1)
            act.wait_ge(gated, 1)
            for j in range(NA):
                ins = nc.scalar.activation(G[:, j, :], PS[4 + j][:], ACT.Copy)
            ins.then_inc(act_done, 1)
            act.wait_ge(dve_done, 2)
            nc.scalar.activation(sq[:], Y[:], ACT.Square).then_inc(act_done, 1)
            act.wait_ge(dve_done, 3)
            nc.scalar.activation(rstd[:], rstd[:], ACT.Ln).then_inc(act_done, 1)
            act.wait_ge(act_done, 4)
            nc.scalar.activation(rstd[:], rstd[:], ACT.Exp, scale=-0.5).then_inc(act_done, 1)

        @block.vector
        def _(dve):
            steps = Steps(dve, own_v)
            steps.one(nc.vector.tensor_tensor(rk[:], r, k, ALU.mult))
            for j in range(NA):
                ins = nc.vector.tensor_scalar(rk[:, j, :], rk[:, j, :], C["r_k"][:, j:j + 1], None, ALU.mult)
                if j < NA - 1:
                    steps(ins)
            ins.then_inc(dve_done, 1)
            dve.wait_ge(mean, 1)
            for j in range(NA):
                ins = nc.vector.tensor_tensor(Y[:, j, :], Y[:, j, :], PS[j][:], ALU.subtract)
                if j < NA - 1:
                    steps(ins)
            ins.then_inc(dve_done, 1)
            dve.wait_ge(bonus, 1)
            for j in range(NA):
                steps(nc.vector.tensor_tensor(v[:, j, :], v[:, j, :], PS[4 + j][:], ALU.mult))
            dve.wait_ge(var, 1)
            for j in range(NA):
                ins = nc.vector.tensor_scalar(rstd[:, j, :], PS[j][:], LNX_EPS, None, ALU.add)
                if j < NA - 1:
                    steps(ins)
            ins.then_inc(dve_done, 1)
            dve.wait_ge(act_done, 5)
            steps.wait()
            for j in range(NA):
                steps(nc.vector.scalar_tensor_tensor(Y[:, j, :], Y[:, j, :], C["lnx_g"][:, j:j + 1], rstd[:, j, :],
                                                     ALU.mult, ALU.mult))
            steps.wait()
            for j in range(NA):
                steps(nc.vector.scalar_tensor_tensor(Y[:, j, :], Y[:, j, :], C["lnx_b"][:, j:j + 1], v[:, j, :],
                                                     ALU.add, ALU.add))
            steps.wait()
            steps.one(nc.vector.tensor_tensor(Y[:], Y[:], G[:], ALU.mult))


def bank(PS, base, h):
    return PS[base + h // 4][:, chunk(h % 4)]


def conv_silu_normalise(nc, C, PS, QKV):
    H = GDN_HEADS
    with stage(nc, "conved", "silu", "squared", "summed", "rstd", "own_v", "own_a") as (
            block, conved, silu, squared, summed, rstd_ok, own_v, own_a), Memory(nc) as mem:
        buf = [mem(f"conv{i}", P, S) for i in range(2)]
        sq = [mem(f"sq{i}", P, S) for i in range(2)]
        rs = mem("rs", P, 2 * H, S)

        @block.vector
        def _(dve):
            steps = Steps(dve, own_v)
            for b in range(3 * H):
                if b >= 2:
                    dve.wait_ge(silu, b - 1)
                causal_conv(nc, steps, buf[b % 2][:], QKV[:, b, :], C["gdn_conv"][:, b, :], None, S).then_inc(conved, 1)
            for b in range(2 * H):
                dve.wait_ge(rstd_ok, b + 1)
                steps(nc.vector.scalar_tensor_tensor(QKV[:, b, :], QKV[:, b, :], (P ** -0.5 if b < H else 1.0),
                                                     rs[:, b, :], ALU.mult, ALU.mult))
            steps.wait()

        @block.scalar
        def _(act):
            steps = Steps(act, own_a)
            for b in range(3 * H):
                act.wait_ge(conved, b + 1)
                nc.scalar.activation(QKV[:, b, :], buf[b % 2][:], ACT.Silu).then_inc(silu, 1)
            act.wait_ge(silu, 3 * H)
            for b in range(2 * H):
                if b >= 2:
                    act.wait_ge(summed, b - 1)
                nc.scalar.activation(sq[b % 2][:], QKV[:, b, :], ACT.Square).then_inc(squared, 1)
                if b:
                    act.wait_ge(summed, b)
                    steps(nc.scalar.activation(rs[:, b - 1, :], PS[(b - 1) % 4][:], ACT.Ln, bias=C["rms_eps"][:, 0:1]))
            act.wait_ge(summed, 2 * H)
            steps(nc.scalar.activation(rs[:, 2 * H - 1, :], PS[(2 * H - 1) % 4][:], ACT.Ln, bias=C["rms_eps"][:, 0:1]))
            steps.wait()
            for b in range(2 * H):
                nc.scalar.activation(rs[:, b, :], rs[:, b, :], ACT.Exp, scale=-0.5).then_inc(rstd_ok, 1)

        @block.tensor
        def _(pe):
            for b in range(2 * H):
                pe.wait_ge(squared, b + 1)
                if b >= 4:
                    pe.wait_ge(own_a, b - 3)
                nc.tensor.matmul(PS[b % 4][:], C["ones"][:], sq[b % 2][:], start=True, stop=True).then_inc(summed, 1)


def gdn_gates(nc, C, PS, h, BETA, GAM):
    H = GDN_HEADS
    with stage(nc, "projected", "own_v", "own_a", "act_done", "dve_done") as (
            block, projected, own_v, own_a, act_done, dve_done), Memory(nc) as mem:
        z, e, na = mem("z", H, S), mem("e", H, S), mem("na", H, 1)

        @block.tensor
        def _(pe):
            for i in range(2):
                for k in range(ND):
                    last = nc.tensor.matmul(PS[i][0:H, :], C["w_ba"][:, k, i * H:(i + 1) * H], h[:, k, :], start=k == 0,
                                            stop=k == ND - 1)
            last.then_inc(projected, 1)

        @block.scalar
        def _(act):
            steps = Steps(act, own_a)
            nc.scalar.activation(na[:], C["gdn_a_log"][:], ACT.Exp)
            act.wait_ge(projected, 1)
            nc.scalar.activation(BETA[:], PS[0][0:H, :], ACT.Sigmoid)
            steps(nc.scalar.activation(z[:], PS[1][0:H, :], ACT.Identity, bias=C["gdn_dt"][:, 0:1]))
            steps.wait()
            steps.one(nc.scalar.activation(e[:], z[:], ACT.Abs))
            nc.scalar.activation(e[:], e[:], ACT.Exp, scale=-1.0).then_inc(act_done, 1)
            act.wait_ge(dve_done, 1)
            nc.scalar.activation(e[:], e[:], ACT.Ln).then_inc(act_done, 1)

        @block.vector
        def _(dve):
            steps = Steps(dve, own_v)
            dve.wait_ge(act_done, 1)
            nc.vector.tensor_scalar(e[:], e[:], 1.0, None, ALU.add).then_inc(dve_done, 1)
            steps.one(nc.vector.tensor_scalar(z[:], z[:], 0.0, None, ALU.max))
            dve.wait_ge(act_done, 2)
            steps.one(nc.vector.tensor_tensor(z[:], z[:], e[:], ALU.add))
            steps.one(nc.vector.tensor_scalar(z[:], z[:], na[:, 0:1], -1.0, ALU.mult, ALU.mult))
            steps.one(nc.vector.tensor_tensor_scan(GAM[:], C["restart"][0:H, :], z[:], 0.0, ALU.mult, ALU.add))


def gdn_chunk(nc, C, PS, QKV, BETA, GAM, ST, O, n):
    H = GDN_HEADS
    t = chunk(n)
    q, k, v = (QKV[:, H * i:H * i + H, t] for i in range(3))
    groups = [(0, 4), (4, H)]
    with Memory(nc) as mem:
        QE, KB, BB = (mem(x, P, H, P) for x in ("q_decayed", "k_beta", "beta"))
        DEC, MT, QK, TT = (mem(x, P, H, P) for x in ("decay", "mt", "qk", "tt"))
        KR, VR = mem("k_rows", P, H, P), mem("v_rows", P, H, P)
        col, tail, gl = mem("col", P, 2 * H), mem("tail", P, H), mem("gl", P, H)
        with stage(nc, "spread", "act_done", "dve_done", "own_v", "own_a") as (
                block, spread, act_done, dve_done, own_v, own_a):
            @block.tensor
            def _(pe):
                for h in range(H):
                    nc.tensor.matmul(bank(PS, 0, h), C["pick"][:, h, :], GAM[:, t], start=True, stop=True)
                    nc.tensor.matmul(bank(PS, 2, h), C["pick"][:, h, :], BETA[:, t], start=True, stop=True)
                nc.tensor.matmul(PS[4][:, 0:H], GAM[:, t], C["ident"][0:H, 0:H], start=True, stop=True)
                nc.tensor.matmul(PS[4][:, H:2 * H], BETA[:, t], C["ident"][0:H, 0:H], start=True,
                                 stop=True).then_inc(spread, 1)

            @block.scalar
            def _(act):
                steps = Steps(act, own_a)
                act.wait_ge(spread, 1)
                for g, (a, b) in enumerate(groups):
                    def wide(i):
                        return PS[i + g][:, 0:(b - a) * P].rearrange("p (h t) -> p h t", t=P)
                    nc.scalar.activation(BB[:, a:b, :], wide(2), ACT.Copy)
                    nc.scalar.activation(QE[:, a:b, :], wide(0), ACT.Exp)
                    ins = nc.scalar.activation(gl[:, a:b], wide(0)[:, :, P - 1], ACT.Exp)
                ins.then_inc(act_done, 1)
                act.wait_ge(dve_done, 1)
                nc.scalar.activation(tail[:], tail[:], ACT.Exp)
                nc.scalar.activation(DEC[:], DEC[:], ACT.Exp).then_inc(act_done, 1)

            @block.vector
            def _(dve):
                steps = Steps(dve, own_v)
                dve.wait_ge(spread, 1)
                dve.wait_ge(act_done, 1)
                steps.one(nc.vector.tensor_copy(col[:], PS[4][:, 0:2 * H]))
                for g, (a, b) in enumerate(groups):
                    steps(nc.vector.tensor_tensor(tail[:, a:b], PS[g][:, 0:(b - a) * P].rearrange(
                        "p (h t) -> p h t", t=P)[:, :, P - 1], col[:, a:b], ALU.subtract))
                steps.wait()
                for h in range(H):
                    ins = nc.vector.tensor_scalar(DEC[:, h, :], bank(PS, 0, h), col[:, h:h + 1], 0.0, ALU.subtract,
                                                  ALU.min)
                    if h < H - 1:
                        steps(ins)
                ins.then_inc(dve_done, 1)
                steps.one(nc.vector.tensor_tensor(KB[:], k, QE[:], ALU.mult))
                steps.one(nc.vector.tensor_tensor(KB[:], KB[:], BB[:], ALU.mult))
                steps.one(nc.vector.tensor_tensor(QE[:], QE[:], q, ALU.mult))
                dve.wait_ge(act_done, 2)
                steps.one(nc.vector.tensor_tensor(DEC[:], DEC[:], C["until"][:, None, :].broadcast_to([P, H, P]), ALU.mult))

        with stage(nc, "scored", "own_v") as (block, scored, own_v):
            @block.tensor
            def _(pe):
                for h in range(H):
                    nc.tensor.matmul(bank(PS, 0, h), k[:, h, :], k[:, h, :], start=True, stop=True)
                    nc.tensor.matmul(bank(PS, 2, h), k[:, h, :], q[:, h, :], start=True, stop=True)
                    nc.tensor.transpose(bank(PS, 4, h), k[:, h, :], C["ident"][:])
                    last = nc.tensor.transpose(bank(PS, 6, h), v[:, h, :], C["ident"][:])
                last.then_inc(scored, 1)

            @block.vector
            def _(dve):
                steps = Steps(dve, own_v)
                dve.wait_ge(scored, 1)
                for g, (a, b) in enumerate(groups):
                    def wide(i):
                        return PS[i + g][:, 0:(b - a) * P].rearrange("p (h t) -> p h t", t=P)
                    steps(nc.vector.tensor_tensor(MT[:, a:b, :], wide(0), DEC[:, a:b, :], ALU.mult))
                    steps(nc.vector.tensor_tensor(QK[:, a:b, :], wide(2), DEC[:, a:b, :], ALU.mult))
                    steps(nc.vector.tensor_tensor(KR[:, a:b, :], wide(4),
                                                  tail[:, a:b, None].broadcast_to([P, b - a, P]), ALU.mult))
                    steps(nc.vector.tensor_tensor(VR[:, a:b, :], wide(6),
                                                  col[:, H + a:H + b, None].broadcast_to([P, b - a, P]), ALU.mult))
                steps.wait()
                steps.one(nc.vector.scalar_tensor_tensor(MT[:], MT[:], -1.0, BB[:], ALU.mult, ALU.mult))
                steps.one(nc.vector.tensor_tensor(MT[:], MT[:], C["before"][:, None, :].broadcast_to([P, H, P]), ALU.mult))

        with Memory(nc) as mem2:
            T, BT, W1 = (mem2(x, P, H, P) for x in ("t", "bt", "w1"))
            unit_lower_inverse(nc, C, PS, MT, TT, T, BT, W1, H)

        with stage(nc, "sums", "read", "state") as (block, sums, read, state), Memory(nc) as mem2:
            R, U = mem2("rhs", P, H, P), mem2("delta", P, H, P)

            @block.tensor
            def _(pe):
                for h in range(H):
                    last = nc.tensor.matmul(bank(PS, 0, h), KB[:, h, :], ST[:, h, :], start=True, stop=True)
                last.then_inc(sums, 1)
                pe.wait_ge(read, 1)
                for h in range(H):
                    last = nc.tensor.matmul(bank(PS, 2, h), TT[:, h, :], R[:, h, :], start=True, stop=True)
                last.then_inc(sums, 1)
                pe.wait_ge(read, 2)
                for h in range(H):
                    nc.tensor.matmul(bank(PS, 4, h), ST[:, h, :], QE[:, h, :], start=True, stop=False)
                    last = nc.tensor.matmul(bank(PS, 4, h), U[:, h, :], QK[:, h, :], start=False, stop=True)
                last.then_inc(sums, 1)
                for h in range(H):
                    last = nc.tensor.matmul(bank(PS, 6, h), KR[:, h, :], U[:, h, :], start=True, stop=True)
                last.then_inc(sums, 1)

            @block.scalar
            def _(act):
                act.wait_ge(sums, 2)
                for g, (a, b) in enumerate(groups):
                    ins = nc.scalar.activation(U[:, a:b, :], PS[2 + g][:, 0:(b - a) * P].rearrange(
                        "p (h t) -> p h t", t=P), ACT.Copy)
                ins.then_inc(read, 1)
                act.wait_ge(sums, 3)
                for g, (a, b) in enumerate(groups):
                    ins = nc.scalar.activation(O[:, a:b, t], PS[4 + g][:, 0:(b - a) * P].rearrange(
                        "p (h t) -> p h t", t=P), ACT.Copy)
                ins.then_inc(read, 1)
                act.wait_ge(read, 3)

            @block.vector
            def _(dve):
                dve.wait_ge(sums, 1)
                for g, (a, b) in enumerate(groups):
                    ins = nc.vector.tensor_tensor(R[:, a:b, :], VR[:, a:b, :], PS[g][:, 0:(b - a) * P].rearrange(
                        "p (h t) -> p h t", t=P), ALU.subtract)
                ins.then_inc(read, 1)
                dve.wait_ge(sums, 4)
                for h in range(H):
                    nc.vector.scalar_tensor_tensor(ST[:, h, :], ST[:, h, :], gl[:, h:h + 1], bank(PS, 6, h),
                                                   ALU.mult, ALU.add).then_inc(state, 1)
                dve.wait_ge(state, H)


def gla_decays(nc, C, PS, GD, CU):
    with stage(nc, "projected", "act_done", "dve_done", "own_v", "own_a") as (
            block, projected, act_done, dve_done, own_v, own_a), Memory(nc) as mem:
        z, e = mem("z", P, 2, S), mem("e", P, 2, S)

        @block.tensor
        def _(pe):
            for n in range(2):
                last = nc.tensor.matmul(PS[n][:], C["gla_gate"][:, chunk(n)], GD[:], start=True, stop=True)
            last.then_inc(projected, 1)

        @block.scalar
        def _(act):
            steps = Steps(act, own_a)
            act.wait_ge(projected, 1)
            for n in range(2):
                steps(nc.scalar.activation(z[:, n, :], PS[n][:], ACT.Identity, bias=C["gla_b"][:, n:n + 1]))
            steps.wait()
            steps.one(nc.scalar.activation(e[:], z[:], ACT.Abs))
            nc.scalar.activation(e[:], e[:], ACT.Exp, scale=-1.0).then_inc(act_done, 1)
            act.wait_ge(dve_done, 1)
            nc.scalar.activation(e[:], e[:], ACT.Ln).then_inc(act_done, 1)

        @block.vector
        def _(dve):
            steps = Steps(dve, own_v)
            dve.wait_ge(act_done, 1)
            nc.vector.tensor_scalar(e[:], e[:], 1.0, None, ALU.add).then_inc(dve_done, 1)
            steps.one(nc.vector.tensor_scalar(z[:], z[:], 0.0, None, ALU.min))
            dve.wait_ge(act_done, 2)
            steps.one(nc.vector.tensor_tensor(z[:], z[:], e[:], ALU.subtract))
            steps.one(nc.vector.tensor_scalar(z[:], z[:], 1.0 / GLA_TAU, None, ALU.mult))
            for n in range(2):
                steps(nc.vector.tensor_tensor_scan(CU[:, n, :], C["restart"][:], z[:, n, :], 0.0, ALU.mult, ALU.add))
            steps.wait()


def gla_chunk(nc, C, PS, Q, K, V, CU, ST, O, n):
    t = chunk(n)
    q, k, cu = Q[:, :, t], K[:, :, t], CU[:, :, t]
    subs = P // GLA_SUB
    with Memory(nc) as mem:
        KH, QH = mem("k_about", P, subs, 2, P), mem("q_about", P, 2, P)
        Q0, KE = mem("q_start", P, 2, P), mem("k_end", P, 2, P)
        KER, AT, gend = mem("k_end_rows", P, 2 * P), mem("attn", P, GLA_HEADS, P), mem("gend", P, 2)
        with stage(nc, "exponent", "expd", "own_v") as (block, exponent, expd, own_v):
            @block.vector
            def _(dve):
                steps = Steps(dve, own_v)
                steps(nc.vector.memset(KH[:], 0.0))
                steps.wait()
                for i in range(subs):
                    m, w = n * P + i * GLA_SUB + GLA_SUB // 2 - 1, (i + 1) * GLA_SUB
                    mid = CU[:, :, m:m + 1]
                    steps(nc.vector.tensor_tensor(KH[:, i, :, 0:w], mid.broadcast_to([P, 2, w]), cu[:, :, 0:w],
                                                  ALU.subtract))
                    o = slice(i * GLA_SUB, (i + 1) * GLA_SUB)
                    steps(nc.vector.tensor_tensor(QH[:, :, o], cu[:, :, o], mid.broadcast_to([P, 2, GLA_SUB]),
                                                  ALU.subtract))
                e = n * P + P - 1
                steps(nc.vector.tensor_tensor(KE[:], CU[:, :, e:e + 1].broadcast_to([P, 2, P]), cu, ALU.subtract))
                steps.wait()
                steps(nc.vector.tensor_scalar(KH[:], KH[:], EXP_CAP, None, ALU.min))
                nc.vector.tensor_scalar(QH[:], QH[:], EXP_CAP, None, ALU.min).then_inc(exponent, 1)
                dve.wait_ge(expd, 1)
                for i in range(subs):
                    w = (i + 1) * GLA_SUB
                    steps(nc.vector.tensor_tensor(KH[:, i, :, 0:w], KH[:, i, :, 0:w], k[:, :, 0:w], ALU.mult))
                    if w < P:
                        steps(nc.vector.memset(KH[:, i, :, w:], 0.0))
                steps(nc.vector.tensor_tensor(QH[:], QH[:], q, ALU.mult))
                steps(nc.vector.tensor_tensor(Q0[:], Q0[:], q, ALU.mult))
                steps(nc.vector.tensor_tensor(KE[:], KE[:], k, ALU.mult))
                steps.wait()

            @block.scalar
            def _(act):
                nc.scalar.activation(Q0[:], cu, ACT.Exp)
                nc.scalar.activation(gend[:], CU[:, :, n * P + P - 1], ACT.Exp)
                act.wait_ge(exponent, 1)
                nc.scalar.activation(KH[:], KH[:], ACT.Exp)
                nc.scalar.activation(QH[:], QH[:], ACT.Exp)
                nc.scalar.activation(KE[:], KE[:], ACT.Exp).then_inc(expd, 1)

        with stage(nc, "sums", "read", "kept", "state") as (block, sums, read, kept, state):
            @block.tensor
            def _(pe):
                for h in range(GLA_HEADS):
                    o = slice(64 * (h % 2), 64 * (h % 2) + 64)
                    for i in range(subs):
                        w = slice(i * GLA_SUB, (i + 1) * GLA_SUB)
                        last = nc.tensor.matmul(PS[4 * (h % 2)][:, (h // 2) * P + w.start:(h // 2) * P + w.stop], KH[o, i, h // 2, :],
                                                QH[o, h // 2, w], start=True, stop=True)
                last.then_inc(sums, 1)
                for j in range(2):
                    last = nc.tensor.transpose(PS[1][:, chunk(j)], KE[:, j, :], C["ident"][:])
                last.then_inc(sums, 1)
                pe.wait_ge(kept, 1)
                for h in range(GLA_HEADS):
                    o = slice(64 * (h % 2), 64 * (h % 2) + 64)
                    nc.tensor.matmul(PS[2 + 3 * (h % 2)][:, chunk(h // 2)], ST[o, h // 2, :], Q0[o, h // 2, :], start=True, stop=False)
                    last = nc.tensor.matmul(PS[2 + 3 * (h % 2)][:, chunk(h // 2)], V[:, h, n, :], AT[:, h, :], start=False, stop=True)
                last.then_inc(sums, 1)
                pe.wait_ge(read, 1)
                for h in range(GLA_HEADS):
                    o = slice(64 * (h % 2), 64 * (h % 2) + 64)
                    last = nc.tensor.matmul(PS[3][o, chunk(h // 2)], KER[:, 64 * h:64 * h + 64], V[:, h, n, :],
                                            start=True, stop=True)
                last.then_inc(sums, 1)

            @block.scalar
            def _(act):
                act.wait_ge(sums, 2)
                nc.scalar.activation(KER[:], PS[1][:, 0:2 * P], ACT.Copy).then_inc(read, 1)
                act.wait_ge(sums, 3)
                for g in range(2):
                    ins = nc.scalar.activation(O[:, g::2, t], PS[2 + 3 * g][:, 0:2 * P].rearrange(
                        "p (h t) -> p h t", t=P), ACT.Copy)
                ins.then_inc(read, 1)
                act.wait_ge(read, 2)

            @block.vector
            def _(dve):
                dve.wait_ge(sums, 1)
                for g in range(2):
                    ins = nc.vector.tensor_tensor(AT[:, g::2, :], PS[4 * g][:, 0:2 * P].rearrange(
                        "p (h t) -> p h t", t=P), C["until"][:, None, :].broadcast_to([P, 2, P]), ALU.mult)
                ins.then_inc(kept, 1)
                dve.wait_ge(sums, 4)
                for j in range(2):
                    nc.vector.scalar_tensor_tensor(ST[:, j, :], ST[:, j, :], gend[:, j:j + 1], PS[3][:, chunk(j)],
                                                   ALU.mult, ALU.add).then_inc(state, 1)
                dve.wait_ge(state, 2)


def head_norm(nc, C, PS, O, heads, gain, factor=1.0, gate=None):
    with stage(nc, "squared", "summed", "rstd_ok", "scaled", "own_v", "own_a") as (
            block, squared, summed, rstd_ok, scaled, own_v, own_a), Memory(nc) as mem:
        sq = [mem(f"sq{i}", P, S) for i in range(2)]
        rs = mem("rs", P, heads, S)

        @block.scalar
        def _(act):
            steps = Steps(act, own_a)
            if gate is not None:
                nc.scalar.activation(gate, gate, ACT.Silu)
            for b in range(heads):
                if b >= 2:
                    act.wait_ge(summed, b - 1)
                nc.scalar.activation(sq[b % 2][:], O[:, b, :], ACT.Square).then_inc(squared, 1)
                if b:
                    act.wait_ge(summed, b)
                    steps(nc.scalar.activation(rs[:, b - 1, :], PS[(b - 1) % 4][:], ACT.Ln, bias=C["rms_eps"][:, 0:1]))
            act.wait_ge(summed, heads)
            steps(nc.scalar.activation(rs[:, heads - 1, :], PS[(heads - 1) % 4][:], ACT.Ln,
                                       bias=C["rms_eps"][:, 0:1]))
            steps.wait()
            for b in range(heads):
                nc.scalar.activation(rs[:, b, :], rs[:, b, :], ACT.Exp, scale=-0.5).then_inc(rstd_ok, 1)

        @block.tensor
        def _(pe):
            for b in range(heads):
                pe.wait_ge(squared, b + 1)
                if b >= 4:
                    pe.wait_ge(own_a, b - 3)
                nc.tensor.matmul(PS[b % 4][:], C["mean_head"][:], sq[b % 2][:], start=True, stop=True).then_inc(summed, 1)

        @block.vector
        def _(dve):
            steps = Steps(dve, own_v)
            for b in range(heads):
                dve.wait_ge(rstd_ok, b + 1)
                steps.one(nc.vector.tensor_scalar(rs[:, b, :], rs[:, b, :], gain[:, 0:1], factor, ALU.mult, ALU.mult))
                nc.vector.tensor_tensor(O[:, b, :], O[:, b, :], rs[:, b, :], ALU.mult).then_inc(scaled, 1)
            dve.wait_ge(scaled, heads)
            if gate is not None:
                steps.one(nc.vector.tensor_tensor(O[:, 0:heads, :], O[:, 0:heads, :], gate, ALU.mult))


def ffn(nc, C, W, PS, h, name, taps, bias, conv_values, func, FH, FL, halves=None):
    with stage(nc, "gate_ready", "act_ready", "product", "high_ok", "low_ok", "f_high", "f_low", "own_v") as (
            block, gate_ready, act_ready, product, high_ok, low_ok, f_high, f_low, own_v), Memory(nc) as mem:
        if halves is None:
            halves = [mem(n, P, ND, S, dtype=F32R) for n in ("act_high", "act_low")]
        high, low = halves
        g = [mem(f"gate{i}", P, S) for i in range(2)]
        val = mem("val", P, S)

        @block.sync
        def _(sp):
            W.load(sp, name)

        @block.tensor
        def _(pe):
            W.sums(pe, name, lambda n: PS[n % 4][:], high, low,
                   lambda n: None if n < 4 else ((gate_ready, product)[n % 2], n // 2 - 1),
                   fresh=None if h is None else low_ok)

        @block.scalar
        def _(act):
            W.split_high(act, name, -1)
            if h is not None:
                split_high(nc, h, high, high_ok)
            for i in range(NF):
                W.split_high(act, name, 2 * i)
                act.wait_ge(gate_ready, i + 1)
                nc.scalar.activation(g[i % 2][:], g[i % 2][:], func).then_inc(act_ready, 1)
                W.split_high(act, name, 2 * i + 1)
                act.wait_ge(product, i + 1)
                nc.scalar.activation(FH[:, i, :], g[i % 2][:], ACT.Copy).then_inc(f_high, 1)

        @block.vector
        def _(dve):
            steps = Steps(dve, own_v)

            def product_low(i):
                dve.wait_ge(f_high, i + 1)
                nc.vector.tensor_tensor(FL[:, i, :], g[i % 2][:], FH[:, i, :].bitcast(F32), ALU.subtract).then_inc(
                    f_low, 1)

            W.split_low(dve, name, -1)
            if h is not None:
                split_low(nc, dve, h, high, low, high_ok, low_ok)
            for i in range(NF):
                W.split_low(dve, name, 2 * i)
                dve.wait_ge(W.used, W.done(name, 2 * i))
                if i >= 2:
                    dve.wait_ge(f_low, i - 1)
                causal_conv(nc, steps, g[i % 2][:], PS[(2 * i) % 4][:], taps[:, i, :], bias[:, i:i + 1],
                            S).then_inc(gate_ready, 1)
                W.split_low(dve, name, 2 * i + 1)
                if i:
                    product_low(i - 1)
                dve.wait_ge(W.used, W.done(name, 2 * i + 1))
                value = PS[(2 * i + 1) % 4][:]
                if conv_values:
                    if i:
                        dve.wait_ge(product, i)
                    steps.one(causal_conv(nc, steps, val[:], value, taps[:, NF + i, :], bias[:, NF + i:NF + i + 1], S))
                    value = val[:]
                dve.wait_ge(act_ready, i + 1)
                nc.vector.tensor_tensor(g[i % 2][:], g[i % 2][:], value, ALU.mult).then_inc(product, 1)
            product_low(NF - 1)
            dve.wait_ge(f_low, NF)


def load(nc, items):
    with stage(nc, "landed") as (block, landed):
        @block.sync
        def _(sp):
            for dst, src in items[0::2]:
                sp.dma_start(dst, src).then_inc(landed, 16)
            sp.wait_ge(landed, 16 * len(items))

        @block.scalar
        def _(act):
            for dst, src in items[1::2]:
                act.dma_start(dst, src).then_inc(landed, 16)


def score_biases(nc, C, PS, A, scratch, G0, G12):
    _, at = one_hot_positions()
    L = scratch.shape[2]
    with Memory(nc) as mem:
        table, rep, hot = mem("table", 33, SWA_HEADS), mem("rep", 33, SWA_HEADS, P), mem("hot", 33, L)
        rows = mem("rows", P, SWA_HEADS, L)
        with stage(nc, "landed", "filled", "sums", "rows_ready", "stored") as (
                block, landed, filled, sums, rows_ready, stored):
            @block.sync
            def _(sp):
                sp.dma_start(table[0:32, :], A["rel_bias"]).then_inc(landed, 16)
                sp.dma_start(hot[:], A["one_hot"]).then_inc(landed, 16)
                for h in range(SWA_HEADS):
                    sp.wait_ge(rows_ready, (h + 1) * (L // 512))
                    sp.dma_start(scratch[h], rows[:, h, :]).then_inc(stored, 16)
                sp.wait_ge(stored, 16 * SWA_HEADS)

            @block.vector
            def _(dve):
                nc.vector.memset(table[32:33, :], MASKED).then_inc(filled, 1)
                dve.wait_ge(landed, 32)
                dve.wait_ge(filled, 1)
                nc.vector.tensor_copy(rep[:], table[:, :, None].broadcast_to([33, SWA_HEADS, P])).then_inc(filled, 1)

            @block.tensor
            def _(pe):
                pe.wait_ge(filled, 2)
                for h in range(SWA_HEADS):
                    for c in range(L // 512):
                        m = h * (L // 512) + c
                        if m >= 4:
                            pe.wait_ge(rows_ready, m - 3)
                        nc.tensor.matmul(PS[m % 4][:], rep[:, h, :], hot[:, 512 * c:512 * c + 512], start=True,
                                         stop=True).then_inc(sums, 1)

            @block.scalar
            def _(act):
                for h in range(SWA_HEADS):
                    for c in range(L // 512):
                        m = h * (L // 512) + c
                        act.wait_ge(sums, m + 1)
                        nc.scalar.activation(rows[:, h, 512 * c:512 * c + 512], PS[m % 4][:], ACT.Copy).then_inc(
                            rows_ready, 1)
    cuts = []
    for h in range(SWA_HEADS):
        base = h * P * L
        cuts.append((G0[:, h, :], bass.AP(scratch.tensor, base + at[0] + 4 * 127, [[L - 4, P], [1, G0_W]])))
        for g in range(2):
            cuts.append((G12[:, h, g, :], bass.AP(scratch.tensor, base + at[1 + g] + 127, [[L - 1, P], [1, P]])))
    load(nc, cuts)


def full_biases(nc, scratch, TZ):
    _, at = one_hot_positions()
    L = scratch.shape[2]
    load(nc, [(TZ[:, h, :], bass.AP(scratch.tensor, h * P * L + at[3] + 127, [[L - 1, P], [1, TZ_W]]))
              for h in range(SWA_HEADS)])


def diff_lambda(nc, C, PS, lp):
    with stage(nc, "products", "sums", "expd") as (block, products, sums, expd), Memory(nc) as mem:
        prod, e = mem("prod", 64, 2), mem("e", P, 2)

        @block.vector
        def _(dve):
            nc.vector.tensor_tensor(prod[:, 0:1], lp[:, 0:1], lp[:, 1:2], ALU.mult)
            nc.vector.tensor_tensor(prod[:, 1:2], lp[:, 2:3], lp[:, 3:4], ALU.mult).then_inc(products, 1)
            dve.wait_ge(expd, 1)
            nc.vector.tensor_tensor(C["lam"][:], e[:, 0:1], e[:, 1:2], ALU.subtract).then_inc(products, 1)
            dve.wait_ge(products, 2)
            nc.vector.tensor_scalar(C["lam"][:], C["lam"][:], LAM_INIT, None, ALU.add).then_inc(products, 1)
            dve.wait_ge(products, 3)

        @block.tensor
        def _(pe):
            pe.wait_ge(products, 1)
            nc.tensor.matmul(PS[0][:, 0:2], C["ones"][0:64, :], prod[:], start=True, stop=True).then_inc(sums, 1)

        @block.scalar
        def _(act):
            act.wait_ge(sums, 1)
            nc.scalar.activation(e[:], PS[0][:, 0:2], ACT.Exp).then_inc(expd, 1)


def clear(nc, tensors):
    with stage(nc, "cleared") as (block, cleared):
        @block.vector
        def _(dve):
            for t in tensors:
                nc.vector.memset(t, 0.0).then_inc(cleared, 1)
            dve.wait_ge(cleared, len(tensors))


PROJECTIONS = [
    ("mix_in", 22, ND), ("mix_gate_a", 8, ND), ("branch_a", 8, NA), ("mix_gate_b", 8, ND), ("branch_b", 8, NB),
    ("mix_out", 8, ND), ("cq", 8, ND), ("ck", 8, ND), ("cv", 8, ND), ("co", 8, ND),
    ("ffn_in", 2 * NF, ND), ("ffn_out", 8, NF),
    ("swa_qk", 12, ND), ("swa_v", 6, ND), ("gdn_in", 24, ND), ("even_out", 8, 8),
    ("ffn_in_0", 2 * NF, ND), ("ffn_out_0", 8, NF),
    ("diff_qk", 8, ND), ("diff_v", 4, ND), ("gla_qkr", 8, ND), ("gla_v", 4, ND), ("odd_out", 8, 8),
    ("ffn_in_1", 2 * NF, ND), ("ffn_out_1", 8, NF),
]

CONSTANTS = [
    ("ident", (P, P)), ("over_d", (P, P)), ("pair_ones", (P, P)), ("pair_mean", (P, P)), ("mean_head", (P, P)),
    ("ones", (P, P)), ("level_mask", (P, LEVELS, P)), ("before", (P, P)), ("until", (P, P)), ("restart", (P, S)),
    ("pick", (GDN_HEADS, GDN_HEADS, P)),
    ("norm_mix_g", (P, ND)), ("b_in", (P, 22)), ("b_gates", (P, 16)), ("mu", (P, RWKV_BLOCKS)),
    ("w0", (P, NA)), ("a0", (P, NA)), ("k_k", (P, NA)), ("k_a", (P, NA)), ("r_k", (P, NA)), ("lnx_g", (P, NA)),
    ("lnx_b", (P, NA)), ("w_lora", (P, A_WIDTH)), ("g_lora", (P, A_WIDTH)),
    ("conv_b_w", (P, NB, B_CONV)), ("conv_b_b", (P, NB)), ("w_rg_a", (P, NB, P)), ("w_rg_x", (P, NB, P)),
    ("b_rg_a", (P, NB)), ("b_rg_x", (P, NB)), ("lru_lambda", (P, NB)),
    ("norm_x_g", (P, ND)), ("norm_mem_g", (P, ND)), ("norm_ffn_g", (P, ND)), ("norm_final_g", (P, ND)),
    ("ffn_conv_w", (P, NF, FFN_CONV)), ("ffn_conv_b", (P, NF)),
    ("gdn_conv", (P, 3 * GDN_HEADS, GDN_CONV)), ("w_ba", (P, ND, 2 * GDN_HEADS)), ("gdn_a_log", (GDN_HEADS, 1)),
    ("gdn_dt", (GDN_HEADS, 1)), ("gdn_norm", (P, 1)),
    ("diff_lp", (64, 4)), ("diff_norm", (P, 1)), ("w_gd", (P, ND, 16)), ("gla_gate", (16, 2 * P)), ("gla_b", (P, 2)),
    ("gla_norm", (P, 1)),
    ("ffn_conv_w2", (P, 2, 2 * NF, FFN_CONV)), ("ffn_conv_b2", (P, 2, 2 * NF)),
    ("ln_g", (P, 4, ND)), ("ln_b", (P, 4, ND)),
]


def project_rows(nc, W, PS, name, act, tiles, dst):
    blocks = W.shape[name][0]
    with stage(nc, "read_out") as (block, read_out):
        @block.sync
        def _(sp):
            W.load(sp, name)

        @block.tensor
        def _(pe):
            W.sums_rows(pe, name, lambda n: PS[n % 4], act, tiles, lambda n: (read_out, n - 3) if n >= 4 else None)

        @block.scalar
        def _(act_e):
            for n in range(blocks):
                act_e.wait_ge(W.used, W.done(name, n))
                nc.scalar.activation(dst[:, n, :, :], PS[n % 4][:, 0:tiles * P].rearrange("p (t f) -> p t f", f=P),
                                     ACT.Copy).then_inc(read_out, 1)
            act_e.wait_ge(read_out, blocks)


def build(nc, A, out, scratch):
    with Memory(nc) as keep, ExitStack() as banks:
        PS = [banks.enter_context(nc.psum_tensor(f"bank{i}", [P, 512], F32)) for i in range(8)]
        stored = nc.alloc_semaphore("out_stored")
        W = Weights(nc, keep, {name: (A[name], blocks, depth) for name, blocks, depth in PROJECTIONS},
                    ("cv", "swa_v", "diff_v", "gla_v"))
        x = keep("x", P, ND, S)
        names, items = {}, [(x[:], A["x"])]
        for name, shape in CONSTANTS:
            names[name] = keep(name, *shape)
            items.append((names[name][:], A[name]))
        names["lam"], names["spare"], names["rms_eps"] = keep("lam", P, 1), keep("spare", P, 2), keep("rms_eps", P, 1)
        C = names
        load(nc, items)
        with stage(nc, "filled") as (block, filled):
            @block.vector
            def _(dve):
                nc.vector.memset(C["rms_eps"][:], RMS_EPS).then_inc(filled, 1)
                dve.wait_ge(filled, 1)
        diff_lambda(nc, C, PS, C["diff_lp"])

        def copy_to(t):
            return ("scalar", lambda n, s, steps: nc.scalar.activation(t[:, n, :], s, ACT.Copy))

        def add_to(t, factor=1.0):
            return ("vector", lambda n, s, steps: nc.vector.scalar_tensor_tensor(
                t[:, n, :], t[:, n, :], factor, s, ALU.mult, ALU.add))

        def sigmoid_to(t, bias):
            return ("scalar", lambda n, s, steps: nc.scalar.activation(t[:, n, :], s, ACT.Sigmoid,
                                                                       bias=bias[:, n:n + 1]))

        with Memory(nc) as mem:
            h, YB, Y = mem("h", P, ND, S), mem("y_b", P, NB, S), mem("y_a", P, NA, S)
            normalise(nc, C, PS, x, h, C["norm_mix_g"])
            with Memory(nc) as rw:
                M = rw("mixed", P, RWKV_BLOCKS, S)
                with Memory(nc) as m2:
                    PXY = m2("pxy", P, 2 * NB, S)
                    mixer_projection(nc, C, W, PS, h, M, PXY)
                    griffin(nc, C, PS, PXY, YB)
                LD, CU = x[:, 0:NA, :], x[:, NA:2 * NA, :]
                KN, BV = (rw(n, P, NA, S) for n in ("kn", "bv"))
                ST = rw("state", P, NA, P)
                rwkv_prepare(nc, C, PS, M, LD, CU, KN, BV)
                clear(nc, [ST[:]])
                for n in range(NT):
                    rwkv_chunk(nc, C, PS, M, LD, CU, KN, BV, ST, Y, n)
                rwkv_finish(nc, C, PS, M, Y)
                load(nc, [(x[:], A["x"])])
            with Memory(nc) as m2:
                SG, merged = m2("gate", P, ND, S), m2("merged", P, ND, S)
                project(nc, W, PS, "mix_gate_a", h, evac=sigmoid_to(SG, C["b_gates"][:, 0:8]))
                project(nc, W, PS, "branch_a", Y, evac=("vector", lambda n, s, steps:
                        nc.vector.tensor_tensor(merged[:, n, :], SG[:, n, :], s, ALU.mult)))
                project(nc, W, PS, "mix_gate_b", h, evac=sigmoid_to(SG, C["b_gates"][:, 8:16]))

                def gated_add(n, s, steps):
                    steps.one(nc.vector.tensor_tensor(SG[:, n, :], SG[:, n, :], s, ALU.mult))
                    return nc.vector.tensor_tensor(merged[:, n, :], merged[:, n, :], SG[:, n, :], ALU.add)

                project(nc, W, PS, "branch_b", YB, evac=("vector", gated_add))
                project(nc, W, PS, "mix_out", merged, evac=add_to(x))

        with Memory(nc) as mem:
            h, q, o = mem("h", P, ND, S), mem("q", P, ND, S), mem("o", P, ND, S)
            mm, k, v = mem("mm", P, ND, NMEM), mem("k", P, ND, NMEM), mem("v", P, ND, 2, P)
            normalise(nc, C, PS, x, h, C["norm_x_g"])
            project(nc, W, PS, "cq", h, evac=copy_to(q))
            raw = o[:, :, 0:NMEM]
            load(nc, [(raw, A["mem"])])
            normalise(nc, C, PS, raw, mm, C["norm_mem_g"], width=NMEM)
            project(nc, W, PS, "ck", mm, evac=copy_to(k))
            project_rows(nc, W, PS, "cv", lambda kk, t, n: mm[:, kk, chunk(t)], 2, v)
            items = []
            for hd in range(X_HEADS):
                for t in range(NT):
                    items.append({
                        "scores": [(0, 0, q[:, 2 * hd + i, chunk(t)], k[:, 2 * hd + i, :], i == 0, i == 1)
                                   for i in range(2)],
                        "logits": [(0, NMEM, 0, 0, None)], "scale": (D // X_HEADS) ** -0.5,
                        "softmaxes": [(0, NMEM)],
                        "values": [lambda part, hd=hd, j=j: v[:, 2 * hd + part, j, :] for j in range(2)],
                        "parts": 2, "out": (0, P, o[:, 2 * hd:2 * hd + 2, chunk(t)]),
                    })
            attention(nc, C, PS, items, NMEM, v)
            project(nc, W, PS, "co", o, evac=add_to(x))

        with Memory(nc) as mem:
            high, low = (mem(n, P, ND, S, dtype=F32R) for n in ("act_high", "act_low"))
            with Memory(nc) as m2:
                h = m2("h", P, ND, S)
                normalise(nc, C, PS, x, h, C["norm_ffn_g"])
                with stage(nc, "high_ok", "low_ok") as (block, high_ok, low_ok):
                    @block.scalar
                    def _(act):
                        split_high(nc, h, high, high_ok)

                    @block.vector
                    def _(dve):
                        split_low(nc, dve, h, high, low, high_ok, low_ok)
                        dve.wait_ge(low_ok, ND)
            FH, FL = mem("f_high", P, NF, S, dtype=F32R), mem("f_low", P, NF, S, dtype=F32R)
            ffn(nc, C, W, PS, None, "ffn_in", C["ffn_conv_w"], C["ffn_conv_b"], False, ACT.Gelu_apprx_tanh, FH, FL,
                halves=(high, low))
            project(nc, W, PS, "ffn_out", halves=(FH, FL), evac=add_to(x))
        with Memory(nc) as mem:
            scr = mem("scr", P, ND, S)
            normalise(nc, C, PS, x, scr, C["norm_final_g"], final=x)

        def deep_norm(i):
            with Memory(nc) as m2:
                z, scr = m2("z", P, ND, S), m2("scr", P, ND, S)
                normalise(nc, C, PS, x, z, C["ln_g"][:, i, :], bias=C["ln_b"][:, i, :], eps=LN_EPS, scratch=scr,
                          final=x)

        def second_ffn(layer):
            with Memory(nc) as m2:
                FH, FL = m2("f_high", P, NF, S, dtype=F32R), m2("f_low", P, NF, S, dtype=F32R)
                ffn(nc, C, W, PS, x, f"ffn_in_{layer}", C["ffn_conv_w2"][:, layer, :, :],
                    C["ffn_conv_b2"][:, layer, :], True, ACT.Silu, FH, FL)
                project(nc, W, PS, f"ffn_out_{layer}", halves=(FH, FL), evac=add_to(x, ALPHA))
            deep_norm(2 * layer + 1)

        with Memory(nc) as mem:
            OE = mem("o_even", P, 8, S)
            with Memory(nc) as m2:
                G0, G12 = m2("g0_bias", P, SWA_HEADS, G0_W), m2("g12_bias", P, SWA_HEADS, 2, P)
                score_biases(nc, C, PS, A, scratch, G0, G12)
                qk, vs = m2("swa_qk", P, 12, S), m2("swa_v", P, 6, NT, P)
                project(nc, W, PS, "swa_qk", x, evac=copy_to(qk))
                by_class = x[:].rearrange("p k (i r) -> p k i r", r=SWA_DIL)
                project_rows(nc, W, PS, "swa_v", lambda k, t, n: x[:, k, chunk(t)] if n < 2
                             else by_class[:, k, :, t], NT, vs)
                OB = OE[:, 6:8, :].rearrange("p k (i r) -> p k i r", r=SWA_DIL)
                cls = qk[:].rearrange("p k (i r) -> p k i r", r=SWA_DIL)
                items = []
                for hd in range(SWA_HEADS):
                    b, o = hd // 2, slice(64 * (hd % 2), 64 * (hd % 2) + 64)
                    for r in range(SWA_DIL):
                        items.append({
                            "scores": [(0, 0, cls[o, b, :, r], qk[o, 6 + b, :], True, True)] + [
                                (1, (g - 1) * P, cls[o, 2 * g + b, :, r], cls[o, 6 + 2 * g + b, :, r], True, True)
                                for g in (1, 2)],
                            "logits": [(0, S, 0, 0, G0[:, hd, 3 - r:3 - r + S]),
                                       (S, P, 1, 0, G12[:, hd, 0, :]), (S + P, P, 1, P, G12[:, hd, 1, :])],
                            "scale": SWA_DIM ** -0.5, "softmaxes": [(0, S + 2 * P)],
                            "values": [lambda part, j=j, b=b, o=o: vs[:, b, j, o] for j in range(NT)] + [
                                lambda part, g=g, b=b, r=r, o=o: vs[:, 2 * g + b, r, o] for g in (1, 2)],
                            "out": (o.start, 64, OB[o, b, :, r]),
                        })
                attention(nc, C, PS, items, S + 2 * P, vs)
            with Memory(nc) as m2:
                QKVZ, BETA, GAM = m2("qkvz", P, 24, S), m2("beta", GDN_HEADS, S), m2("gam", GDN_HEADS, S)
                ST = m2("state", P, GDN_HEADS, P)
                project(nc, W, PS, "gdn_in", x, evac=copy_to(QKVZ))
                gdn_gates(nc, C, PS, x, BETA, GAM)
                conv_silu_normalise(nc, C, PS, QKVZ)
                clear(nc, [ST[:]])
                for n in range(NT):
                    gdn_chunk(nc, C, PS, QKVZ, BETA, GAM, ST, OE, n)
                head_norm(nc, C, PS, OE, GDN_HEADS, C["gdn_norm"], gate=QKVZ[:, 18:24, :])
            project(nc, W, PS, "even_out", OE, evac=add_to(x, ALPHA))
        deep_norm(0)
        second_ffn(0)

        with Memory(nc) as mem:
            OD = mem("o_odd", P, 8, S)
            with Memory(nc) as m2:
                qk, vd = m2("diff_qk", P, 8, S), m2("diff_v", P, 4, NT, P)
                TZ = m2("full_bias", P, SWA_HEADS, TZ_W)
                full_biases(nc, scratch, TZ)
                project(nc, W, PS, "diff_qk", x, evac=copy_to(qk))
                project_rows(nc, W, PS, "diff_v", lambda k, t, n: x[:, k, chunk(t)], NT, vd)
                items = []
                for hd in range(4):
                    for t in range(NT):
                        w = (t + 1) * P
                        bias = TZ[:, hd, 384 - t * P:384 - t * P + w]
                        items.append({
                            "scores": [(c, 0, qk[64 * c:64 * c + 64, hd, chunk(t)],
                                        qk[64 * c:64 * c + 64, 4 + hd, 0:w], True, True) for c in range(2)],
                            "logits": [(c * w, w, c, 0, bias) for c in range(2)], "scale": 64 ** -0.5,
                            "softmaxes": [(0, w), (w, 2 * w)],
                            "values": [lambda part, hd=hd, j=j: vd[:, hd, j, :] for j in range(t + 1)],
                            "out": (0, P, OD[:, hd, chunk(t)]),
                        })
                attention(nc, C, PS, items, 2 * S, vd)
                head_norm(nc, C, PS, OD, 4, C["diff_norm"], factor=1.0 - LAM_INIT)
            with Memory(nc) as m2:
                QKR, vg, CU = m2("gla_qkr", P, 8, S), m2("gla_v", P, 4, NT, P), m2("cu", P, 2, S)
                GD, ST = m2("g_d", 16, S), m2("state", P, 2, P)

                def scaled_copy(n, s, steps):
                    return nc.scalar.activation(QKR[:, n, :], s, ACT.Copy, scale=64 ** -0.5 if n < 2 else 1.0)

                project(nc, W, PS, "gla_qkr", x, evac=("scalar", scaled_copy))
                project_rows(nc, W, PS, "gla_v", lambda k, t, n: x[:, k, chunk(t)], NT, vg)
                with stage(nc, "sums", "copied") as (block, sums, copied):
                    @block.tensor
                    def _(pe):
                        for k in range(ND):
                            last = nc.tensor.matmul(PS[0][0:16, :], C["w_gd"][:, k, :], x[:, k, :], start=k == 0,
                                                    stop=k == ND - 1)
                        last.then_inc(sums, 1)

                    @block.scalar
                    def _(act):
                        act.wait_ge(sums, 1)
                        nc.scalar.activation(GD[:], PS[0][0:16, :], ACT.Copy).then_inc(copied, 1)
                        act.wait_ge(copied, 1)
                gla_decays(nc, C, PS, GD, CU)
                clear(nc, [ST[:]])
                OG = OD[:, 4:8, :]
                for n in range(NT):
                    gla_chunk(nc, C, PS, QKR[:, 0:2, :], QKR[:, 2:4, :], vg, CU, ST, OG, n)
                head_norm(nc, C, PS, OG, 4, C["gla_norm"], gate=QKR[:, 4:8, :])
            project(nc, W, PS, "odd_out", OD, evac=add_to(x, ALPHA))
        deep_norm(2)
        second_ffn(1)

        with nc.Block() as block:
            @block.sync
            def _(sp):
                sp.dma_start(out, x[:]).then_inc(stored, 16)
                sp.wait_ge(stored, 16)


def columns(v):
    return np.ascontiguousarray(v.reshape(-1, P).T)


def taps(w):
    return np.ascontiguousarray(w.reshape(w.shape[0], -1, P).transpose(2, 1, 0))


def tiled(w):
    k, n = w.shape
    return np.ascontiguousarray(w.reshape(k // P, P, n // P, P).transpose(2, 1, 0, 3))


def features(a):
    return np.ascontiguousarray(a.T.reshape(-1, P, a.shape[0]).transpose(1, 0, 2))


def rows_of(w):
    return np.ascontiguousarray(w.reshape(-1, P, w.shape[1]).transpose(1, 0, 2))


def paired(w):
    r, c = w.shape
    return w.reshape(r, 2, c // 2 // P, P).transpose(0, 2, 1, 3).reshape(r, c)


def block_diagonal(w):
    out = np.zeros((P, w.shape[0] // 2, P), w.dtype)
    for i in range(w.shape[0]):
        o = 64 * (i % 2)
        out[o:o + 64, i // 2, o:o + 64] = w[i]
    return out


def shape_constants():
    f = np.float32
    i = np.arange(P)
    row, col = i[:, None], i[None, :]
    same64 = (row // 64 == col // 64).astype(f)
    level = np.stack([(row // (2 * m) == col // (2 * m)) & (row % (2 * m) < m) & (col % (2 * m) >= m)
                      for m in (1 << l for l in range(LEVELS))], axis=1).astype(f)
    pick = np.zeros((GDN_HEADS, GDN_HEADS, P), f)
    for h in range(GDN_HEADS):
        pick[h, h] = 1
    return {
        "ident": np.eye(P, dtype=f), "over_d": np.full((P, P), 1.0 / D, f), "pair_ones": same64,
        "pair_mean": np.where(same64 > 0, f(1 / 64), f(0)), "mean_head": np.full((P, P), 1.0 / P, f),
        "ones": np.ones((P, P), f), "level_mask": level, "before": (row < col).astype(f),
        "until": (row <= col).astype(f),
        "restart": np.broadcast_to((np.arange(S) % P != 0).astype(f), (P, S)).copy(), "pick": pick,
        "one_hot": one_hot_positions()[0],
    }


def kernel(**inputs):
    import concourse.bacc as _bacc
    from concourse.bass_utils import run_bass_kernel_spmd as _run

    I = {k: np.asarray(v) for k, v in inputs.items()}
    w_in, b_in = I["w_in"][0], I["b_in"][0]
    even, odd = I["w_in_even_2"][0], I["w_in_odd_2"][0]
    g = 2 * GDN_HEADS
    a = shape_constants()
    a.update({
        "x": features(I["x"][0]), "mem": features(I["mem"][0]),
        "mix_in": tiled(w_in[:, 0:2816]), "mix_gate_a": tiled(w_in[:, 2816:3840]), "mix_gate_b": tiled(w_in[:, 3840:]),
        "b_in": columns(b_in[0:2816]), "b_gates": columns(b_in[2816:]),
        "branch_a": tiled(I["w_branch_a"][0]), "branch_b": tiled(I["w_branch_b"][0]),
        "mix_out": tiled(I["w_mix_out"][0]), "cq": tiled(I["w_cq"][0]), "ck": tiled(I["w_ckv"][0][:, 0:D]),
        "cv": tiled(I["w_ckv"][0][:, D:]), "co": tiled(I["w_co"][0]),
        "ffn_in": tiled(paired(I["w_ffn_in"][0])), "ffn_out": tiled(I["w_ffn_out"][0]),
        "swa_qk": tiled(even[:, 3072 + g:3072 + g + 1536]), "swa_v": tiled(even[:, 3072 + g + 1536:]),
        "gdn_in": tiled(even[:, 0:3072]), "w_ba": rows_of(even[:, 3072:3072 + g]),
        "even_out": tiled(I["w_out_even_2"][0]),
        "diff_qk": tiled(odd[:, 0:1024]), "diff_v": tiled(odd[:, 1024:1536]),
        "gla_qkr": tiled(np.concatenate([odd[:, 1536:2048], odd[:, 2560:3072]], axis=1)),
        "gla_v": tiled(odd[:, 2048:2560]), "w_gd": rows_of(odd[:, 3072:]), "odd_out": tiled(I["w_out_odd_2"][0]),
        "w_lora": np.concatenate([I["w_lora_up"][0], I["a_lora_up"][0]], axis=0), "g_lora": I["g_lora_up"][0],
        "w_rg_a": block_diagonal(I["w_rg_a"][0]), "w_rg_x": block_diagonal(I["w_rg_x"][0]),
        "conv_b_w": taps(I["conv_b_w"][0]), "ffn_conv_w": taps(I["ffn_conv_w"][0]),
        "gdn_conv": taps(I["gdn_conv_w_2"][0]),
        "gdn_a_log": I["gdn_a_log_2"].reshape(-1, 1), "gdn_dt": I["gdn_dt_bias_2"].reshape(-1, 1),
        "gdn_norm": columns(I["gdn_norm_w_2"][0]), "diff_lp": np.ascontiguousarray(I["diff_lambda_2"][0].T),
        "diff_norm": columns(I["diff_norm_w_2"][0]), "gla_gate": I["gla_w_gate_2"][0],
        "gla_b": columns(I["gla_b_gate_2"][0]), "gla_norm": columns(I["gla_norm_w_2"][0]),
        "ffn_conv_w2": np.stack([taps(w) for w in I["ffn_conv_w_2"]], axis=1),
        "ffn_conv_b2": np.stack([columns(v) for v in I["ffn_conv_b_2"]], axis=1),
        "ln_g": np.stack([columns(v) for v in I["ln_g_2"].reshape(4, D)], axis=1),
        "ln_b": np.stack([columns(v) for v in I["ln_b_2"].reshape(4, D)], axis=1),
        "rel_bias": I["rel_bias_2"], "mu": columns(I["mu_shift"][0]), "r_k": columns(I["r_k"][0].reshape(-1)),
        "norm_final_g": columns(I["norm_final_g"]),
    })
    for layer in range(2):
        a[f"ffn_in_{layer}"] = tiled(paired(I["ffn_w_up_2"][layer]))
        a[f"ffn_out_{layer}"] = tiled(I["ffn_w_down_2"][layer])
    for name in ("norm_mix_g", "w0", "a0", "k_k", "k_a", "lnx_g", "lnx_b", "conv_b_b", "b_rg_a", "b_rg_x",
                 "lru_lambda", "norm_x_g", "norm_mem_g", "norm_ffn_g", "ffn_conv_b"):
        a[name] = columns(I[name][0])

    nc = _bacc.Bacc("TRN2", target_bir_lowering=False, num_devices=1)
    STAGES[0] = 0
    arrays, A = {}, {}
    for name, v in a.items():
        arrays[f"in_{name}_dram"] = np.ascontiguousarray(v)
        A[name] = nc.dram_tensor(f"in_{name}_dram", v.shape, F32, kind="ExternalInput").ap()
    out = nc.dram_tensor("out_0_dram", (P, ND, S), F32, kind="ExternalOutput").ap()
    scratch = nc.dram_tensor("bias_rows", (SWA_HEADS, P, a["one_hot"].shape[1]), F32, kind="Internal").ap()
    build(nc, A, out, scratch)
    r = _run(nc, [arrays], core_ids=[0])
    got = r.results[0]["out_0_dram"]
    return np.ascontiguousarray(got.transpose(1, 0, 2).reshape(D, S).T)[None]
```
